# Optimizing a Trainium2 kernel written in Bass

```python
import jax, jax.numpy as jnp
from jax import lax
import numpy as np

D_MODEL = 1024
BATCH = 1
SEQ = 1024
DEPTH = 2
DEC_BATCH = 8
DEC_SEQ = 4
PAST_LEN = 1024
PAGE_SIZE = 128

N_REC = (DEPTH + 1) // 2
N_ATT = DEPTH // 2
CONV_W = 4
D_RNN = D_MODEL // 2
RG_HEADS = 8
RG_BW = D_RNN // RG_HEADS
RG_C = 8.0
DN_HEADS = 4
DN_DK = 128
DN_DV = 128
DN_QK = DN_HEADS * DN_DK
DN_VD = DN_HEADS * DN_DV
DN_CHUNK = 64
CONV_CH = D_RNN + 2 * DN_QK + DN_VD
REC_IN = CONV_CH + D_RNN + DN_VD + 2 * DN_HEADS
ATT_HEADS = D_MODEL // 128
KV_HEADS = 2
HEAD_DIM = 128
GROUP = ATT_HEADS // KV_HEADS
IDX_HEADS = 8
IDX_DIM = 64
TOPK_MAX = 256
Q_BLOCK = 128
ATT_IN = ATT_HEADS * HEAD_DIM + 2 * KV_HEADS * HEAD_DIM + IDX_HEADS * IDX_DIM + IDX_DIM + IDX_HEADS
D_FF = 4 * D_MODEL
EPS = 1e-6

kernel_name = 'hybrid_rglru_gdn_dsa_step'

def rmsnorm(x, g):
    x32 = x.astype(jnp.float32)
    y = x32 * lax.rsqrt(jnp.mean(x32 * x32, axis=-1, keepdims=True) + EPS)
    return (y * g.astype(jnp.float32)).astype(x.dtype)

def l2norm(x):
    return x * lax.rsqrt(jnp.sum(x * x, axis=-1, keepdims=True) + EPS)

def mlp(x, w_up, w_down):
    h = jax.nn.relu(x @ w_up)
    return (h * h) @ w_down

def causal_dwconv(u, buf, w):
    T = u.shape[1]
    xp = jnp.concatenate([buf.astype(u.dtype), u], axis=1)
    out = xp[:, 0:T] * w[0]
    for i in range(1, CONV_W):
        out = out + xp[:, i:i + T] * w[i]
    return out, xp[:, T:]

def rglru(xr, is_first, h0, wa, ba, wx, bx, lam):
    B, T, _ = xr.shape
    f32 = jnp.float32
    x32 = xr.astype(f32)
    xb = x32.reshape(B, T, RG_HEADS, RG_BW)
    r = jax.nn.sigmoid(jnp.einsum('bthi,hij->bthj', xb, wa.astype(f32)).reshape(B, T, D_RNN) + ba.astype(f32))
    ig = jax.nn.sigmoid(jnp.einsum('bthi,hij->bthj', xb, wx.astype(f32)).reshape(B, T, D_RNN) + bx.astype(f32))
    log_a = -RG_C * r * jax.nn.softplus(-lam.astype(f32))
    a = jnp.exp(log_a)
    mult = jnp.where(is_first[None, :, None], 1.0, jnp.sqrt(jnp.maximum(1.0 - jnp.exp(2.0 * log_a), 0.0)))
    b = x32 * ig * mult
    b = b.at[:, 0].add(a[:, 0] * h0.astype(f32))

    def comb(lhs, rhs):
        return (lhs[0] * rhs[0], rhs[0] * lhs[1] + rhs[1])

    _, h = lax.associative_scan(comb, (a, b), axis=1)
    return h, h[:, -1]

def gated_delta(q, k, v, g, beta, S0):
    B, T, H, DK = q.shape
    DV = v.shape[-1]
    C = DN_CHUNK if T % DN_CHUNK == 0 else T
    n = T // C
    f32 = jnp.float32

    def chunks(x):
        return jnp.moveaxis(x.reshape((B, n, C, H) + x.shape[3:]), 3, 1)

    q = chunks(l2norm(q.astype(f32)) * DK ** -0.5)
    k = chunks(l2norm(k.astype(f32)))
    v = chunks(v.astype(f32))
    g = chunks(g.astype(f32))
    beta = chunks(beta.astype(f32))
    gc = jnp.cumsum(g, axis=-1)
    tri = jnp.tril(jnp.ones((C, C), bool))
    strict = jnp.tril(jnp.ones((C, C), bool), -1)
    decay = jnp.exp(jnp.where(tri, gc[..., :, None] - gc[..., None, :], -jnp.inf))
    kb = k * beta[..., None]
    lmat = jnp.where(strict, jnp.einsum('bhnid,bhnjd->bhnij', kb, k) * decay, 0.0)
    amat = lmat + jnp.eye(C, dtype=f32)
    rhs = jnp.concatenate([v * beta[..., None], kb * jnp.exp(gc)[..., None]], axis=-1)
    sol = lax.linalg.triangular_solve(amat, rhs, left_side=True, lower=True, unit_diagonal=True)
    u, w = sol[..., :DV], sol[..., DV:]
    attn = jnp.einsum('bhnid,bhnjd->bhnij', q, k) * decay
    qg = q * jnp.exp(gc)[..., None]
    kd = k * jnp.exp(gc[..., -1:] - gc)[..., None]
    glast = jnp.exp(gc[..., -1])

    def step(S, inp):
        u_i, w_i, a_i, qg_i, kd_i, gl_i = inp
        vnew = u_i - jnp.einsum('bhcd,bhdv->bhcv', w_i, S)
        o = jnp.einsum('bhcd,bhdv->bhcv', qg_i, S) + jnp.einsum('bhij,bhjv->bhiv', a_i, vnew)
        S = S * gl_i[..., None, None] + jnp.einsum('bhcd,bhcv->bhdv', kd_i, vnew)
        return S, o

    xs = tuple(jnp.moveaxis(t, 2, 0) for t in (u, w, attn, qg, kd, glast))
    S_T, o = lax.scan(step, S0.astype(f32), xs)
    o = jnp.moveaxis(jnp.moveaxis(o, 0, 2), 1, 3).reshape(B, T, H, DV)
    return o, S_T

def rec_mixer(xn, conv_buf, h0, S0, is_first, w_in, w_conv, b_conv, wa, ba, wx, bx, lam,
              a_log, dt_bias, dn_w, w_out):
    B, T, _ = xn.shape
    p = xn @ w_in
    u = p[..., :CONV_CH]
    gate = p[..., CONV_CH:CONV_CH + D_RNN]
    z = p[..., CONV_CH + D_RNN:CONV_CH + D_RNN + DN_VD]
    off = CONV_CH + D_RNN + DN_VD
    b_raw = p[..., off:off + DN_HEADS]
    a_raw = p[..., off + DN_HEADS:off + 2 * DN_HEADS]
    uc, new_buf = causal_dwconv(u, conv_buf, w_conv)
    xr = uc[..., :D_RNN] + b_conv
    h, hT = rglru(xr, is_first, h0, wa, ba, wx, bx, lam)
    rg_y = (h * jax.nn.gelu(gate.astype(jnp.float32))).astype(xn.dtype)
    qkv = jax.nn.silu(uc[..., D_RNN:])
    q = qkv[..., :DN_QK].reshape(B, T, DN_HEADS, DN_DK)
    k = qkv[..., DN_QK:2 * DN_QK].reshape(B, T, DN_HEADS, DN_DK)
    v = qkv[..., 2 * DN_QK:].reshape(B, T, DN_HEADS, DN_DV)
    beta = jax.nn.sigmoid(b_raw.astype(jnp.float32))
    g = -jnp.exp(a_log.astype(jnp.float32)) * jax.nn.softplus(a_raw.astype(jnp.float32) + dt_bias.astype(jnp.float32))
    o, S_T = gated_delta(q, k, v, g, beta, S0)
    o = rmsnorm(o, dn_w) * jax.nn.silu(z.astype(jnp.float32).reshape(B, T, DN_HEADS, DN_DV))
    dn_y = o.reshape(B, T, DN_VD).astype(xn.dtype)
    y = jnp.concatenate([rg_y, dn_y], axis=-1) @ w_out
    return y, new_buf, hT.astype(xn.dtype), S_T.astype(xn.dtype)

def att_project(xn, w_in):
    B, T, _ = xn.shape
    p = xn @ w_in
    o1 = ATT_HEADS * HEAD_DIM
    o2 = o1 + KV_HEADS * HEAD_DIM
    o3 = o2 + KV_HEADS * HEAD_DIM
    o4 = o3 + IDX_HEADS * IDX_DIM
    o5 = o4 + IDX_DIM
    q = p[..., :o1].reshape(B, T, ATT_HEADS, HEAD_DIM)
    k = p[..., o1:o2].reshape(B, T, KV_HEADS, HEAD_DIM)
    v = p[..., o2:o3].reshape(B, T, KV_HEADS, HEAD_DIM)
    qi = p[..., o3:o4].reshape(B, T, IDX_HEADS, IDX_DIM)
    ki = p[..., o4:o5]
    wi = p[..., o5:]
    return q, k, v, qi, ki, wi

def index_scores(qi, wi, ki):
    s = jax.nn.relu(jnp.einsum('bthd,bsd->bths', qi, ki).astype(jnp.float32))
    return jnp.einsum('bth,bths->bts', wi.astype(jnp.float32), s)

def sparse_attend(q, kg, vg, valid):
    B, T = q.shape[:2]
    qg = q.reshape(B, T, KV_HEADS, GROUP, HEAD_DIM)
    s = jnp.einsum('btkgd,btjkd->btkgj', qg, kg).astype(jnp.float32) * HEAD_DIM ** -0.5
    s = jnp.where(valid[:, :, None, None, :], s, -1e30)
    pr = jax.nn.softmax(s, axis=-1)
    o = jnp.einsum('btkgj,btjkd->btkgd', pr.astype(vg.dtype), vg)
    return o.reshape(B, T, ATT_HEADS * HEAD_DIM)

def dsa_prompt(xn, w_in, w_out):
    B, S, _ = xn.shape
    q, k, v, qi, ki, wi = att_project(xn, w_in)
    topk = min(TOPK_MAX, S // 4)
    qb = min(Q_BLOCK, S)
    nb = S // qb
    bidx = jnp.arange(B)[:, None, None]
    kpos = jnp.arange(S)

    def blocks(x):
        return jnp.moveaxis(x.reshape((B, nb, qb) + x.shape[2:]), 1, 0)

    def blk(args):
        q_b, qi_b, wi_b, bi = args
        tpos = bi * qb + jnp.arange(qb)
        sc = index_scores(qi_b, wi_b, ki)
        sc = jnp.where(kpos[None, None, :] <= tpos[None, :, None], sc, -jnp.inf)
        _, idx = lax.top_k(sc, topk)
        valid = idx <= tpos[None, :, None]
        return sparse_attend(q_b, k[bidx, idx], v[bidx, idx], valid)

    o = lax.map(blk, (blocks(q), blocks(qi), blocks(wi), jnp.arange(nb)))
    o = jnp.moveaxis(o, 0, 1).reshape(B, S, ATT_HEADS * HEAD_DIM)
    return o @ w_out, k, v, ki

def dsa_sample(xn, ck, cv, cki, page_table, w_in, w_out):
    DB, T, _ = xn.shape
    page = ck.shape[1]
    past = page_table.shape[1] * page
    L = past + T
    q, k, v, qi, ki, wi = att_project(xn, w_in)
    ki_past = cki[page_table].reshape(DB, past, IDX_DIM)
    ki_all = jnp.concatenate([ki_past, ki.astype(ki_past.dtype)], axis=1)
    tpos = past + jnp.arange(T)
    sc = index_scores(qi, wi, ki_all)
    sc = jnp.where(jnp.arange(L)[None, None, :] <= tpos[None, :, None], sc, -jnp.inf)
    _, idx = lax.top_k(sc, min(TOPK_MAX, L // 4))
    bidx = jnp.arange(DB)[:, None, None]
    pidx = jnp.minimum(idx, past - 1)
    phys = page_table[bidx, pidx // page] * page + pidx % page
    nidx = jnp.clip(idx - past, 0, T - 1)
    is_new = (idx >= past)[..., None, None]
    ck_rows = ck.reshape((-1,) + ck.shape[2:])
    cv_rows = cv.reshape((-1,) + cv.shape[2:])
    kg = jnp.where(is_new, k[bidx, nidx].astype(ck.dtype), ck_rows[phys])
    vg = jnp.where(is_new, v[bidx, nidx].astype(cv.dtype), cv_rows[phys])
    valid = idx <= tpos[None, :, None]
    o = sparse_attend(q, kg, vg, valid)
    return o @ w_out, k, v, ki

def setup_inputs(seed: int = 0) -> dict:
    key = jax.random.key(seed)
    ks = jax.random.split(key, 32)
    f32 = jnp.float32
    n_pages = PAST_LEN // PAGE_SIZE
    n_used = DEC_BATCH * n_pages
    n_pool = n_used + (n_used + 3) // 4

    def nrm(k, shape, s):
        return jax.random.normal(k, shape, f32) * s

    a0 = jax.random.uniform(ks[15], (N_REC, D_RNN), f32, 0.9, 0.999) ** (1.0 / RG_C)
    return {
        'x_prompt': nrm(ks[0], (BATCH, SEQ, D_MODEL), 1.0),
        'x_sample': nrm(ks[1], (DEC_BATCH, DEC_SEQ, D_MODEL), 1.0),
        'state_conv': nrm(ks[2], (N_REC, DEC_BATCH, CONV_W - 1, CONV_CH), 1.0),
        'state_h': nrm(ks[3], (N_REC, DEC_BATCH, D_RNN), 0.5),
        'state_S': nrm(ks[4], (N_REC, DEC_BATCH, DN_HEADS, DN_DK, DN_DV), DN_DK ** -0.5),
        'cache_k': nrm(ks[5], (N_ATT, n_pool, PAGE_SIZE, KV_HEADS, HEAD_DIM), 1.0),
        'cache_v': nrm(ks[6], (N_ATT, n_pool, PAGE_SIZE, KV_HEADS, HEAD_DIM), 1.0),
        'cache_kidx': nrm(ks[7], (N_ATT, n_pool, PAGE_SIZE, IDX_DIM), 1.0),
        'page_table': jax.random.permutation(ks[8], n_pool)[:n_used].reshape(DEC_BATCH, n_pages).astype(jnp.int32),
        'norm_mix': 1.0 + nrm(ks[9], (DEPTH, D_MODEL), 0.01),
        'norm_mlp': 1.0 + nrm(ks[10], (DEPTH, D_MODEL), 0.01),
        'norm_final': 1.0 + nrm(ks[11], (D_MODEL,), 0.01),
        'w_in_rec': nrm(ks[12], (N_REC, D_MODEL, REC_IN), D_MODEL ** -0.5),
        'w_conv': nrm(ks[13], (N_REC, CONV_W, CONV_CH), CONV_W ** -0.5),
        'b_conv': nrm(ks[14], (N_REC, D_RNN), 0.01),
        'rg_wa': nrm(ks[16], (N_REC, RG_HEADS, RG_BW, RG_BW), RG_BW ** -0.5),
        'rg_ba': nrm(ks[17], (N_REC, D_RNN), 0.01),
        'rg_wx': nrm(ks[18], (N_REC, RG_HEADS, RG_BW, RG_BW), RG_BW ** -0.5),
        'rg_bx': nrm(ks[19], (N_REC, D_RNN), 0.01),
        'rg_lambda': jnp.log(a0) - jnp.log1p(-a0),
        'dn_a_log': jnp.log(jax.random.uniform(ks[20], (N_REC, DN_HEADS), f32, 1.0, 16.0)),
        'dn_dt_bias': nrm(ks[21], (N_REC, DN_HEADS), 0.1),
        'dn_norm': 1.0 + nrm(ks[22], (N_REC, DN_DV), 0.01),
        'w_out_rec': nrm(ks[23], (N_REC, D_RNN + DN_VD, D_MODEL), (D_RNN + DN_VD) ** -0.5),
        'w_in_att': nrm(ks[24], (N_ATT, D_MODEL, ATT_IN), D_MODEL ** -0.5),
        'w_out_att': nrm(ks[25], (N_ATT, ATT_HEADS * HEAD_DIM, D_MODEL), (ATT_HEADS * HEAD_DIM) ** -0.5),
        'w_up': nrm(ks[26], (DEPTH, D_MODEL, D_FF), D_MODEL ** -0.5),
        'w_down': nrm(ks[27], (DEPTH, D_FF, D_MODEL), D_FF ** -0.5),
    }

def reference(x_prompt, x_sample, state_conv, state_h, state_S, cache_k, cache_v, cache_kidx, page_table,
              norm_mix, norm_mlp, norm_final, w_in_rec, w_conv, b_conv, rg_wa, rg_ba, rg_wx, rg_bx,
              rg_lambda, dn_a_log, dn_dt_bias, dn_norm, w_out_rec, w_in_att, w_out_att, w_up, w_down):
    B, S, _ = x_prompt.shape
    DB, T, _ = x_sample.shape
    past = page_table.shape[1] * cache_k.shape[2]
    first_p = jnp.arange(S) == 0
    first_s = (past + jnp.arange(T)) == 0
    dt = x_prompt.dtype
    xp, xs = x_prompt, x_sample
    conv_p, h_p, S_p, conv_s, h_s, S_s = [], [], [], [], [], []
    k_p, v_p, ki_p, k_s, v_s, ki_s = [], [], [], [], [], []
    for layer in range(DEPTH):
        hp = rmsnorm(xp, norm_mix[layer])
        hs = rmsnorm(xs, norm_mix[layer])
        if layer % 2 == 0:
            r = layer // 2
            prm = (w_in_rec[r], w_conv[r], b_conv[r], rg_wa[r], rg_ba[r], rg_wx[r], rg_bx[r], rg_lambda[r],
                   dn_a_log[r], dn_dt_bias[r], dn_norm[r], w_out_rec[r])
            yp, cb, hT, ST = rec_mixer(hp, jnp.zeros((B, CONV_W - 1, CONV_CH), dt), jnp.zeros((B, D_RNN), dt),
                                       jnp.zeros((B, DN_HEADS, DN_DK, DN_DV), dt), first_p, *prm)
            conv_p.append(cb); h_p.append(hT); S_p.append(ST)
            ys, cb, hT, ST = rec_mixer(hs, state_conv[r], state_h[r], state_S[r], first_s, *prm)
            conv_s.append(cb); h_s.append(hT); S_s.append(ST)
        else:
            a = layer // 2
            yp, kk, vv, kii = dsa_prompt(hp, w_in_att[a], w_out_att[a])
            k_p.append(kk); v_p.append(vv); ki_p.append(kii)
            ys, kk, vv, kii = dsa_sample(hs, cache_k[a], cache_v[a], cache_kidx[a], page_table, w_in_att[a], w_out_att[a])
            k_s.append(kk); v_s.append(vv); ki_s.append(kii)
        xp = xp + yp
        xs = xs + ys
        xp = xp + mlp(rmsnorm(xp, norm_mlp[layer]), w_up[layer], w_down[layer])
        xs = xs + mlp(rmsnorm(xs, norm_mlp[layer]), w_up[layer], w_down[layer])
    y_prompt = rmsnorm(xp, norm_final)
    y_sample = rmsnorm(xs, norm_final)
    return (y_prompt, y_sample,
            jnp.stack(conv_p), jnp.stack(h_p), jnp.stack(S_p),
            jnp.stack(k_p), jnp.stack(v_p), jnp.stack(ki_p),
            jnp.stack(conv_s), jnp.stack(h_s), jnp.stack(S_s),
            jnp.stack(k_s), jnp.stack(v_s), jnp.stack(ki_s))


_drawn_inputs = setup_inputs


def setup_inputs(seed=0):
    import zlib

    import numpy as np

    out = dict(_drawn_inputs(seed))
    spreads = {}
    factors = {'norm_mix': 3.709,
     'norm_mlp': 51.194,
     'norm_final': 180.967,
     'rg_ba': 36.778,
     'rg_bx': 30.544,
     'dn_dt_bias': 8.0,
     'dn_norm': 165.694,
     'cache_v': 21.271,
     'cache_kidx': 23.224,
     'b_conv': 3.622,
     'cache_k': 7.692,
     'w_out_att': 3.444}
    for name, (base, spread) in spreads.items():
        noise = np.random.default_rng([zlib.crc32(name.encode()), seed]).standard_normal(out[name].shape)
        drawn = base * np.exp(spread * noise) if base else spread * noise
        out[name] = __import__('jax').numpy.asarray(drawn.astype(out[name].dtype))
    for name, factor in factors.items():
        out[name] = (out[name] * factor).astype(out[name].dtype)
    return out
```

```python
from contextlib import ExitStack, contextmanager

import numpy as np

import concourse.bass as bass
from concourse import mybir

F32 = mybir.dt.float32
F32R = mybir.dt.float32r
BF16 = mybir.dt.bfloat16
I32 = mybir.dt.int32
ACT = mybir.ActivationFunctionType
ALU = mybir.AluOpType
AX = mybir.AxisListType.X

P = 128
D_MODEL = 1024
KT = D_MODEL // P
SEQ = 1024
DEC_BATCH = 8
DEC_SEQ = 4
SMP = DEC_BATCH * DEC_SEQ
TOK = SEQ + SMP
QB = SEQ // P
CONV_W = 4
CONV_CH = 2048
CT = CONV_CH // P
D_RNN = 512
RT = D_RNN // P
RG_C = 8.0
DN_H = 4
DK = 128
D_FF = 4096
FF_CHUNK = 512
FF_CHUNKS = D_FF // FF_CHUNK
FT = FF_CHUNK // P
EPS = 1e-6
PAGE = 128
PAST = 1024
PAGES = PAST // PAGE
TOPK = 256
Q_HEADS = 8
KV = 2
GRP = Q_HEADS // KV
IDX_H = 8
IDX_D = 64
SCALE = 128 ** -0.5
NEG = -3.0e38
MASKED = -1e30
UB = 3 + SEQ + DEC_BATCH * (3 + DEC_SEQ)
LEVELS = 6
CUTS512 = ((0, 512), (512, 512), (1024, 32))
CUTS352 = ((0, 352), (352, 352), (704, 352))

U_REC_IN, U_REC_OUT, U_MLP, U_ATT_IN, U_ATT_OUT = 25, 8, 96, 17, 8
FIRST = {}
_at = 0
for _name, _n in (("rec_in", U_REC_IN), ("rec_out", U_REC_OUT), ("mlp0", U_MLP), ("att_in", U_ATT_IN),
                  ("att_out", U_ATT_OUT), ("mlp1", U_MLP)):
    FIRST[_name] = _at
    _at += _n

R_MIX0, R_MIX1, R_MLP0, R_MLP1, R_FIN, R_CONV, R_BCONV, R_BA, R_BX, R_LAM, R_DN, R_ALL = (
    0, 8, 16, 24, 32, 40, 104, 108, 112, 116, 120, 121)
(C_IDENT, C_ONES, C_UPPER, C_STRICT, C_NEG1T, C_NEG1, C_LEVEL, C_SELB, C_SELG, C_UPPER_S, C_STRICT_S, C_COLS,
 C_N) = (0, 1, 2, 3, 4, 5, 6, 12, 16, 20, 21, 22, 23)


def dn_constants():
    c = np.zeros((C_N, P, P), np.float32)
    i = np.arange(P)
    row, col = i[:, None], i[None, :]
    c[C_IDENT] = row == col
    c[C_ONES] = 1.0
    c[C_UPPER] = row <= col
    c[C_STRICT] = row < col

    def level(b):
        return (row // (2 * b) == col // (2 * b)) & (row // b % 2 == 1) & (col // b % 2 == 0)

    c[C_NEG1] = -1.0 * level(1)
    c[C_NEG1T] = -1.0 * level(1).T
    for l in range(LEVELS):
        c[C_LEVEL + l] = level(2 << l)
    for h in range(DN_H):
        c[C_SELB + h, h, :] = 1.0
        c[C_SELG + h, 32 + h, :] = 1.0
    same = row // DEC_SEQ == col // DEC_SEQ
    c[C_UPPER_S] = same & (row <= col)
    c[C_STRICT_S] = same & (row < col)
    c[C_COLS, :, 0:DEC_BATCH] = row // DEC_SEQ == np.arange(DEC_BATCH)[None, :]
    return np.ascontiguousarray(c.transpose(1, 0, 2))


A_BIAS, A_CAP, A_ESEL, A_SELH, A_TOK, A_CAPS, A_BITF, A_N = 0, 128, 256, 768, 800, 1056, 1088, 1119
BITS = 31


def att_constants():
    c = np.zeros((P, A_N), np.float32)
    row, col = np.arange(P)[:, None], np.arange(P)[None, :]
    c[:, A_BIAS:A_BIAS + P] = np.where(col <= row, 0.0, MASKED)
    c[:, A_CAP:A_CAP + P] = np.where(col <= row, -NEG, NEG)
    for b in range(DEC_BATCH):
        for t in range(DEC_SEQ):
            tok = b * DEC_SEQ + t
            for kv in range(KV):
                for g in range(GRP):
                    c[tok, A_ESEL + b // 2 * P + 32 * (b % 2 * KV + kv) + g * DEC_SEQ + t] = 1.0
            for h in range(IDX_H):
                c[h * DEC_SEQ + t, A_TOK + b * SMP + tok] = 1.0
                c[h, A_SELH + h * DEC_SEQ + t] = 1.0
            for u in range(SMP):
                ok = u // DEC_SEQ == b and u % DEC_SEQ <= t
                c[tok, A_CAPS + u] = -NEG if ok else NEG
    c[:, A_BITF:A_BITF + BITS] = 2.0 ** (BITS - 1 - np.arange(BITS))
    return c


def att_bits():
    bits = [1 << (BITS - 1 - k) for k in range(BITS)] + [0xFFFF, 0x10000, -0x10000]
    return np.ascontiguousarray(np.broadcast_to(np.array(bits, np.int32), (P, BITS + 3)))


def row_reset():
    r = np.ones((DN_H, TOK), np.float32)
    r[:, 0:SEQ:P] = 0.0
    r[:, SEQ::DEC_SEQ] = 0.0
    return r


class Chain:

    def __init__(self, eng, sem):
        self.eng, self.sem, self.n, self.off = eng, sem, 0, None

    def did(self, ins):
        ins.then_inc(self.sem, 1)
        self.n += 1

    def wait(self):
        self.eng.wait_ge(self.sem, self.n if self.off is None else self.off + self.n)

    def then(self, ins):
        self.did(ins)
        self.wait()

    @contextmanager
    def loop(self, count, per):
        n0 = self.n
        with self.eng.Fori(0, count) as i:
            self.off = i * per
            yield i
            if self.n - n0 != per:
                raise ValueError(f"{self.n - n0} steps an iteration, not {per}")
        self.n, self.off = n0 + per * count, None


def ds(i, n):
    return bass.ds(i, n)


def flat(ap):
    return ap.rearrange("p a b -> p (a b)")


def build(nc, A, O):
    ctx = ExitStack()
    with ctx:
        base = 16512

        def at(name, shape, dt, off):
            return nc.alloc_sbuf_tensor_at(name, shape, dt, offset=base + off)

        ROW = TOK * 4
        G0 = 0
        X0 = G0 + 2 * KT * ROW
        W0 = X0 + KT * ROW
        S0 = W0 + 6 * KT * P * 4
        M0 = S0 + ROW + 2048
        END = 229344 - base

        xh = at("xh", [P, KT, TOK], F32R, G0)
        xl = at("xl", [P, KT, TOK], F32R, G0 + KT * ROW)
        x = at("x", [P, KT, TOK], F32, X0)
        w_raw = at("w_raw", [P, 2, KT * P], F32, W0)
        w_hi = at("w_hi", [P, 2, KT * P], F32R, W0 + 2 * KT * P * 4)
        w_lo = at("w_lo", [P, 2, KT * P], F32R, W0 + 4 * KT * P * 4)
        rstd = at("rstd", [P, TOK], F32, S0)
        ident = at("ident", [P, P], F32, S0 + ROW)
        ones = at("ones", [P, P], F32, S0 + ROW + 512)
        prm = at("prm", [P, P], F32, S0 + ROW + 1024)
        small = at("small", [P, 128], F32, S0 + ROW + 1536)
        eps_col = small[:, 0:1]
        one_col = small[:, 1:2]
        nea = small[:, 2:3]
        dtb = small[:, 3:4]
        spl = small[:, 8:12]
        spn = small[:, 12:16]
        tmp4 = [small[:, 16 + 4 * k:20 + 4 * k] for k in range(6)]
        h0T = small[:, 40:72].rearrange("p (m b) -> p m b", b=DEC_BATCH)
        hT = small[:, 72:108].rearrange("p (m b) -> p m b", b=DEC_BATCH + 1)

        xtok = at("xtok", [P, QB + 1, D_MODEL], F32, M0)
        cst_rows = at("cst_rows", [R_ALL, P], F32, M0 + 9 * 4096)
        conv_rows = at("conv_rows", [DEC_BATCH * 3, CONV_CH], F32, M0 + 9 * 4096 + 512)
        h0_rows = at("h0_rows", [DEC_BATCH, D_RNN], F32, M0 + 9 * 4096 + 512 + 8192)
        sq = at("sq", [P, 2, TOK], F32, M0)
        sumsq = at("sumsq", [P, TOK], F32, M0 + 2 * ROW)
        qkvz = at("qkvz", [P, 16, TOK], F32, M0)
        ub = at("ub", [P, UB], F32, M0 + 16 * ROW)
        uc = at("uc", [P, UB], F32, M0 + 16 * ROW + 4352)
        hist = at("hist", [P, CT, DEC_BATCH * 3], F32, M0 + 16 * ROW + 8704)
        ctail = at("ctail", [P, CT, 3 + DEC_BATCH * 3], F32, M0 + 16 * ROW + 8704 + 1536)
        xr = at("xr", [P, RT, TOK], F32, X0)
        gate = at("gate", [P, RT, TOK], F32, X0 + RT * ROW)
        r_t = at("r_t", [P, RT, TOK], F32, G0)
        i_t = at("i_t", [P, RT, TOK], F32, G0 + 4 * ROW)
        a_t = at("a_t", [P, RT, TOK], F32, G0 + 8 * ROW)
        wax = at("wax", [P, 2, RT, P], F32, G0 + 12 * ROW)
        rows_raw = at("rows_raw", [64, TOK], F32, G0 + 12 * ROW + 4096)
        rows_b = at("rows_b", [64, TOK], F32, G0 + 13 * ROW + 4096)
        tail_rows = at("tail_rows", [3 + DEC_BATCH * 3, CONV_CH], F32, M0 + 16 * ROW)
        hT_rows = at("hT_rows", [DEC_BATCH + 1, D_RNN], F32, M0 + 16 * ROW + 8192)
        reset = at("reset", [64, TOK], F32, G0 + 14 * ROW + 4096)
        cst = at("cst", [P, C_N, P], F32, X0)
        rows = at("rows", [P, TOK], F32, X0 + C_N * 512)
        HB = DN_H * P * 4
        names = ["kc", "vc", "egb", "dec", "decb", "attn", "lt", "lm", "xi", "xti", "yy", "kd", "vb", "qg", "kbg",
                 "rr", "vn", "st"] + [f"lo{l}" for l in range(LEVELS)]
        dn = {n: at("dn_" + n, [P, DN_H, P], F32, G0 + HB * k) for k, n in enumerate(names)}
        cols = at("cols", [P, P], F32, G0 + HB * len(names))
        rowc = at("rowc", [P, P], F32, G0 + HB * len(names) + 512)
        smp_q = at("smp_q", [P, DN_H, SMP], F32, G0 + HB * len(names) + 1024)
        kq_s = at("kq_s", [P, DN_H, 2, SMP], F32, G0 + HB * len(names) + 1536)
        ks_s = at("ks_s", [P, DN_H, 2, SMP], F32, G0 + HB * len(names) + 2560)
        s0 = at("s0", [P, DEC_BATCH, DN_H, P], F32, M0 + 4 * ROW)
        kdm = at("kdm", [P, DEC_BATCH, DN_H, P], F32, M0 + 8 * ROW)
        assert G0 + HB * len(names) + 3584 <= X0 and X0 + C_N * 512 + ROW <= X0 + 4 * ROW
        hh = at("hh", [P, FT, TOK], F32R, M0)
        hl = at("hl", [P, FT, TOK], F32R, M0 + FT * ROW)
        hu = at("hu", [P, 2, TOK], F32, M0 + 2 * FT * ROW)
        hs = at("hs", [P, 2, TOK], F32, M0 + (2 * FT + 2) * ROW)
        assert M0 + 19 * ROW <= END and M0 + 16 * ROW + 8704 + 1536 + 1728 <= END, (END - M0, 19 * ROW)

        x_spill = nc.dram_tensor("x_spill", (P, KT, TOK), F32, kind="Internal").ap()

        ps = ctx.enter_context(nc.psum_tensor("ps", [P, 8, 512], F32))

        def quad(bank):
            return ps[:, bank, :].rearrange("p (h n) -> p h n", h=4)

        def sem(name):
            return ctx.enter_context(nc.semaphore(name))

        pe_chain, act_chain, dve_chain, pool_chain = (sem(n) for n in ("pe_chain", "act_chain", "dve_chain", "pool_chain"))
        w_loaded = [sem("w_loaded0"), sem("w_loaded1")]
        w_hi_done = sem("w_hi_done")
        w_split = sem("w_split")
        mm_out = sem("mm_out")
        set_free = sem("set_free")
        const_in = sem("const_in")
        phase = sem("phase")
        out_done = sem("out_done")
        n_out = [0]

        block = ctx.enter_context(nc.Block())

        def out_dma(eng, dst, src):
            n_out[0] += 1
            eng.dma_start(dst, src).then_inc(out_done, 16)

        S = {n: sem(n) for n in (
            "start_in tok_in xt_mm xt_act xt_dve xh_ready xl_ready sq_ready sq_added ss_mm ms_ready rt_ready rstd_ready "
            "x_spilled x_back0 x_back1 uc0 conv_done tail_mm tail_sb gate_w ri_mm ri_read rg_exp rg_m2 rg_sqrt rg_gelu ht_mm ht_sb "
            "cn_sq cn_mm cn_sqrt cn_out rg_done rows_a rows_exp rows_b wax_zero "
            "kc_cp vc_cp rowc_cp pe_col pe_bc pe_kk pe_kt pe_vt pe_l pe_y pe_x pe_ks pe_vn pe_o pe_ds "
            "egb_r cols_r dec_r dec_e kd_r vb_r lm_r y_sb vn_r o_st kbg_r qg_r attn_r lt_r x0_r x_sb rr_r st_r lo_r "
            "state_out s0_in kdm_r s0_out silu_z mix_h mix_l seam y_r y_mm y_act y_dve hu_r hsq_r hh_r hl_r").split()}
        SHARED_N = {("mlp", 0): 1, ("mlp", 1): 3}

        N_FIN = 4
        n_phase = {"pe": 0, "act": 0, "dve": 0, "pool": 0}

        def end_phase(eng, who):
            n_phase[who] += 1
            eng.drain().then_inc(phase, 1)
            eng.wait_ge(phase, 4 * n_phase[who])

        n_seam = {"pe": 0, "act": 0, "dve": 0}

        def mlp_start(eng, who):
            n_seam[who] += 1
            eng.drain().then_inc(S["seam"], 1)
            eng.wait_ge(S["seam"], 3 * n_seam[who])

        def set_view(j, c0, n):
            return ps[:, 3 * (j % 2) + c0:3 * (j % 2) + c0 + n, :]

        def units(eng, first, count, per, body):
            if count == per:
                for j in range(per):
                    body(first + j, 0)
                return
            with eng.Fori(0, count // per) as i:
                for j in range(per):
                    body(first + j, i * per)

        w_in_rec = A["w_in_rec"][0].rearrange("(k p) n -> p k n", p=P)
        w_out_rec = A["w_out_rec"][0].rearrange("(k p) n -> p k n", p=P)

        def mlp_loads(sp, l, load):
            first = FIRST[f"mlp{l}"]
            up = A["w_up"][l].rearrange("(k p) n -> p k n", p=P)
            down = A["w_down"][l].rearrange("(c k p) n -> c p k n", p=P, k=FT)
            with sp.Fori(0, FF_CHUNKS) as c:
                for q in range(FT):
                    load(lambda j, off: up[:, :, ds(c * FF_CHUNK + q * P, P)], KT)(first + q, c * 12)
                for q in range(KT):
                    load(lambda j, off: down[ds(c, 1), :, :, q * P:(q + 1) * P].rearrange("c p k n -> (c p) k n"),
                         FT)(first + FT + q, c * 12)

        def y_pe(pe, norm_sum):
            norm_sum(N_FIN, split=False)
            pe.wait_ge(S["y_r"], KT)
            for k in range(2 * (QB + 1)):
                t, half = k // 2, k % 2
                w = P if t < QB else SMP
                if k >= 4:
                    pe.wait_ge(S["y_act"] if k % 2 == 0 else S["y_dve"], (k - 4) // 2 + 1)
                for q in range(4):
                    mm = pe.transpose(ps[0:w, k % 4, q * P:(q + 1) * P], x[:, half * 4 + q, t * P:t * P + w], ident[:, :])
                mm.then_inc(S["y_mm"], 1)

        def y_act(act, norm_squares):
            norm_squares(N_FIN)
            for k in range(0, 2 * (QB + 1), 2):
                t = k // 2
                w = P if t < QB else SMP
                act.wait_ge(S["y_mm"], k + 1)
                act.activation(xtok[0:w, t, 0:512], ps[0:w, k % 4, :], ACT.Copy).then_inc(S["y_act"], 1)

        def y_dve(dve, norm_mean):
            norm_mean(N_FIN)
            for k in range(KT):
                dve.scalar_tensor_tensor(x[:, k, :], x[:, k, :], prm[:, R_FIN + k:R_FIN + k + 1], rstd[:, :],
                                         ALU.mult, ALU.mult).then_inc(S["y_r"], 1)
            for k in range(1, 2 * (QB + 1), 2):
                t = k // 2
                w = P if t < QB else SMP
                dve.wait_ge(S["y_mm"], k + 1)
                dve.tensor_copy(xtok[0:w, t, 512:1024], ps[0:w, k % 4, :]).then_inc(S["y_dve"], 1)

        def y_store(sp):
            for t in range(QB + 1):
                sp.wait_ge(S["y_act"], t + 1)
                sp.wait_ge(S["y_dve"], t + 1)
                if t < QB:
                    out_dma(sp, O["y_prompt"][0, t * P:(t + 1) * P], xtok[:, t, :])
                else:
                    out_dma(sp, O["y_sample"].rearrange("b t d -> (b t) d"), xtok[0:SMP, t, :])
            sp.wait_ge(out_done, 16 * n_out[0])
            sp.wait_ge(S["state_out"], 16 * 6)
        oq = at("oq", [P, 16, TOK], F32, M0)
        ki = at("ki", [P, TOK], F32, M0 + 16 * ROW)
        wi = at("wi", [IDX_H, TOK], F32, M0 + 17 * ROW)
        SC_W = sum(P * (i + 1) for i in range(2, QB))
        sc_off = [sum(P * (k + 1) for k in range(2, i)) for i in range(QB)]
        o = [0]

        def scratch(name, shape, dt, size=4):
            n = size
            for d in shape[1:]:
                n *= d
            t = at(name, shape, dt, o[0])
            o[0] += -(-n // 32) * 32
            return t

        sc = scratch("sc", [P, SC_W], F32)
        sc_s = scratch("sc_s", [SMP, TOK], F32)
        vtok = scratch("vtok", [P, QB + 1, KV * P], F32)
        mb_at = o[0]
        mb = scratch("mb", [P, SC_W], BF16, 2)
        mb_s = scratch("mb_s", [SMP, TOK], BF16, 2)
        ktok = at("ktok", [P, QB + 1, KV * P], F32, mb_at)
        pr_at = o[0]
        pr0 = scratch("pr0", [P, GRP, SEQ], F32)
        pr = [pr0, at("pr1", [P, GRP, SEQ], F32, 0)]
        relu = at("relu", [P, 2, SEQ], F32, pr_at)
        relu_s = at("relu_s", [SMP, 2, SEQ], F32, pr_at + 8192)
        new_relu = at("new_relu", [SMP, DEC_BATCH, SMP], F32, pr_at)
        ptt = scratch("ptt", [P, 2, GRP * P], F32)
        scr_at = o[0]
        scr = [scratch(f"scr{k}", [P, TOK], F32) for k in range(2)]
        pt_s = at("pt_s", [P, PAGES + 1, P], F32, scr_at)
        qs = at("qs", [P, DEC_BATCH, Q_HEADS, DEC_SEQ], F32, scr_at + 4 * (PAGES + 1) * P)
        kpg_at = o[0]
        kpg0 = scratch("kpg0", [P, PAGES, KV * P], F32)
        kpg = [kpg0, at("kpg1", [P, PAGES, KV * P], F32, 8192)]
        kix = [at(f"kix{k}", [P, PAGES, IDX_D], F32, kpg_at + 2048 * k) for k in range(2)]
        kts_at = o[0]
        kts = scratch("kts", [P, KV, PAST], F32)
        kit = [at(f"kit{k}", [IDX_D, PAST], F32, kts_at + 4096 * k) for k in range(2)]
        vpg_at = o[0]
        vpg0 = scratch("vpg0", [P, PAGES, KV * P], F32)
        vpg = [vpg0, at("vpg1", [P, PAGES, KV * P], F32, 0)]
        qis = at("qis", [IDX_D, DEC_BATCH, IDX_H, DEC_SEQ], F32, vpg_at)
        w_tok = at("w_tok", [SMP, DEC_BATCH, SMP], F32, vpg_at + 1024)
        kitok = at("kitok", [P, QB + 1, IDX_D], F32, vpg_at + 4096)
        w_rows = at("w_rows", [SMP, SMP], F32, vpg_at + 2048)
        pr_new = at("pr_new", [P, 2, SMP], F32, pr_at + 8192)
        den_new = at("den_new", [P, 4], F32, pr_at + 8192 + 256)
        acst = scratch("acst", [P, A_N], F32)
        id_b = scratch("id_b", [P, P], BF16, 2)
        bias_b = scratch("bias_b", [P, P], BF16, 2)
        esel_b = scratch("esel_b", [SMP, DEC_BATCH // 2, P], BF16, 2)
        wic = scratch("wic", [P, QB + 1, IDX_H], F32)
        NB = QB - 1
        cnt, neg, quota, acc = (scratch(n, [P, NB], F32) for n in ("cnt", "neg", "quota", "acc"))
        cand, trial, hi16, carry = (scratch(n, [P, NB], I32) for n in ("cand", "trial", "hi16", "carry"))
        mx = scratch("mx", [P, 4], F32)
        den = scratch("den", [P, 8], F32)
        rden = scratch("rden", [P, 8], F32)
        bits = at("bits", [P, BITS + 3], I32, M0 + 18 * ROW + 256)
        pages = at("pages", [1, DEC_BATCH * PAGES], I32, M0 + 18 * ROW)
        assert o[0] <= X0 + KT * ROW, (o[0], X0 + KT * ROW)

        S.update({n: sem(n) for n in (
            "sample_loads acst_in pages_in kx_in0 kx_in1  kp_in0 kp_in1 vp_in0 vp_in1 vp_used kv_out tk_mm tk_act tk_dve "
            "w_tok_r new_mm new_relu_r new_acc new_out si_tr si_kt si_mm si_relu si_acc is_mm is_relu is_acc sc_done "
            "at_mm at_max at_exp at_nrm at_tr at_ptt at_pv at_o sa_tr sa_kts sa_mm sa_ptr sa_pt sa_pv").split()})
        w_in_att = A["w_in_att"][0].rearrange("(k p) n -> p k n", p=P)
        w_out_att = A["w_out_att"][0].rearrange("(k p) n -> p k n", p=P)
        GROUPS = QB * KV
        HEADS = GROUPS * GRP
        steps_before = [sum(k // KV + 1 for k in range(n)) for n in range(GROUPS + 1)]

        def cuts(w):
            return [(c, min(512, w - c)) for c in range(0, w, 512)]

        def bank2(b, w):
            return ps[:, b:b + 2, :].rearrange("p a n -> p (a n)")[:, 0:w]

        def rest_of_sync(sp, load):
            first = FIRST["att_in"]
            units(sp, first, 16, 2, load(lambda j, off: w_in_att[:, :, ds((j + off - first) * P, P)], KT))
            j = first + 16
            n_last = IDX_D + IDX_H
            sp.wait_ge(w_split, j + 1)
            last = w_raw[:, j % 2, :].rearrange("p (k n) -> p k n", k=KT)
            with nc.allow_non_contiguous_dma(reason="72 columns"):
                sp.dma_start(last[:, :, 0:n_last], w_in_att[:, :, 16 * P:16 * P + n_last]).then_inc(w_loaded[j % 2], 16)
            sp.wait_ge(S["x_spilled"], 32)
            sp.dma_start(acst[:, :], A["att_cst"]).then_inc(S["acst_in"], 16)
            sp.dma_start(bits[:, :], A["att_bits"]).then_inc(S["acst_in"], 16)
            sp.dma_start(pages[:, :], A["page_table"].rearrange("b p -> (b p)").unsqueeze(0)).then_inc(S["pages_in"], 16)
            sp.wait_ge(S["pages_in"], 16)
            n_pool = A["cache_k"].shape[1]

            def page_loads(dst, cache, b, done):
                sp.sem_inc(S["sample_loads"], 1)
                for p in range(PAGES):
                    r = sp.value_load(pages[0:1, ds(b * PAGES + p, 1)], min_val=0, max_val=n_pool - 1)
                    sp.dma_start(dst[:, p, :], cache[ds(r, 1)].rearrange("a t d -> (a t) d")).then_inc(done, 16)

            kidx_pages = A["cache_kidx"][0]
            k_pages = A["cache_k"][0].rearrange("n t k d -> n t (k d)")
            v_pages = A["cache_v"][0].rearrange("n t k d -> n t (k d)")
            sp.wait_ge(mm_out, 2 + j + 1)
            with sp.Fori(0, DEC_BATCH // 2) as i:
                for s in range(2):
                    sp.wait_ge(S["si_tr"], i * 4 + 2 * (s + 1))
                    page_loads(kix[s], kidx_pages, i * 2 + s, S[f"kx_in{s}"])
            first = FIRST["att_out"]
            sp.wait_ge(S["si_tr"], 4 + 2 * DEC_BATCH)
            sp.wait_ge(S["si_acc"], DEC_BATCH)
            sp.wait_ge(S["kv_out"], 16 * 6)
            page_loads(kpg[0], k_pages, 0, S["kp_in0"])
            page_loads(vpg[0], v_pages, 0, S["vp_in0"])
            units(sp, first, 2, 2, load(lambda j, off: w_out_att[:, :, ds((j + off - first) * P, P)], KT))
            sp.wait_ge(S["at_pv"], steps_before[GROUPS])
            page_loads(kpg[1], k_pages, 1, S["kp_in1"])
            page_loads(vpg[1], v_pages, 1, S["vp_in1"])
            with sp.Fori(0, DEC_BATCH // 2 - 1) as i:
                for s in range(2):
                    sp.wait_ge(S["sa_tr"], i * 8 + 4 * (s + 1))
                    page_loads(kpg[s], k_pages, i * 2 + (s + 2), S[f"kp_in{s}"])
                for s in range(2):
                    sp.wait_ge(S["vp_used"], i * 2 + (s + 1))
                    page_loads(vpg[s], v_pages, i * 2 + (s + 2), S[f"vp_in{s}"])
            units(sp, first + 2, U_ATT_OUT - 2, 2,
                  load(lambda j, off: w_out_att[:, :, ds((j + off - first) * P, P)], KT))
            mlp_loads(sp, 1, load)
            y_store(sp)

        def rest_of_pool(pool, split_units, mlp_split):
            split_units(FIRST["att_in"], 16, 2, KT)
            split_units(FIRST["att_in"] + 16, 1, 1, KT)
            split_units(FIRST["att_out"], U_ATT_OUT, 2, KT)
            mlp_split(1)

        def rest_of_pe(pe, unit, norm_sum, mlp):
            mlp_start(pe, "pe")
            norm_sum(2)
            units(pe, FIRST["att_in"], 16, 2, unit(KT, xh, xl, CUTS352))
            units(pe, FIRST["att_in"] + 16, 1, 1, unit(KT, xh, xl, CUTS352))
            pe.sem_inc(S["si_tr"], 4)
            mlp_start(pe, "pe")

            for t in range(QB + 1):
                c0, w = t * P, P if t < QB else SMP
                if t >= 4:
                    pe.wait_ge(S["tk_act"], t - 3)
                    pe.wait_ge(S["tk_dve"], t - 3)
                bank = 2 * (t % 4)
                for m in range(2 * KV):
                    pe.transpose(ps[0:w, bank + m // KV, m % KV * P:(m % KV + 1) * P], oq[:, 8 + m, c0:c0 + w], ident[:, :])
                pe.transpose(ps[0:w, bank + 1, KV * P:KV * P + IDX_D], ki[0:IDX_D, c0:c0 + w], ident[0:IDX_D, 0:IDX_D])
                pe.transpose(ps[0:w, bank, KV * P:KV * P + IDX_H], wi[:, c0:c0 + w], ident[0:IDX_H, 0:IDX_H])\
                    .then_inc(S["tk_mm"], 1)
            pe.wait_ge(S["acst_in"], 32)
            pe.wait_ge(S["tk_act"], QB + 1)
            pe.wait_ge(S["tk_dve"], QB + 1)
            pe.matmul(ps[0:SMP, 2, 0:SMP], acst[0:IDX_H, A_SELH:A_SELH + SMP], wi[:, SEQ:TOK], start=True, stop=True)\
                .then_inc(S["tk_mm"], 1)
            pe.wait_ge(S["w_tok_r"], 1)
            for b in range(DEC_BATCH):
                mm = pe.matmul(ps[0:SMP, 6, b * SMP:(b + 1) * SMP], qis[:, b, :, :].rearrange("p h t -> p (h t)"),
                               ki[0:IDX_D, SEQ:TOK], start=True, stop=True)
            mm.then_inc(S["new_mm"], 1)
            pe.wait_ge(S["new_relu_r"], 1)
            for b in range(DEC_BATCH):
                mm = pe.matmul(ps[0:SMP, 7, 0:SMP], w_tok[:, b, :], new_relu[:, b, :], start=b == 0, stop=b == DEC_BATCH - 1)
            mm.then_inc(S["new_acc"], 1)
            pe.wait_ge(S["new_out"], 1)

            def head_sum(b):
                pe.wait_ge(S["si_relu"], b + 1)
                for half in range(2):
                    mm = pe.matmul(ps[0:SMP, 4 + half, :], w_tok[:, b, :], relu_s[:, b % 2, half * 512:(half + 1) * 512],
                                   start=b == 0, stop=b == DEC_BATCH - 1)
                mm.then_inc(S["si_acc"], 1)

            for b in range(DEC_BATCH):
                pe.wait_ge(S[f"kx_in{b % 2}"], 16 * PAGES * (b // 2 + 1))
                for half in range(2):
                    if b:
                        pe.wait_ge(S["si_kt"], 2 * b - 1 + half)
                    for q in range(4):
                        mm = pe.transpose(ps[0:IDX_D, 6 + half, q * P:(q + 1) * P], kix[b % 2][:, 4 * half + q, :], ident[:, :])
                    mm.then_inc(S["si_tr"], 1)
                pe.wait_ge(S["si_kt"], 2 * b + 2)
                for half in range(2):
                    mm = pe.matmul(ps[0:SMP, 2 * (b % 2) + half, :], qis[:, b, :, :].rearrange("p h t -> p (h t)"),
                                   kit[b % 2][:, half * 512:(half + 1) * 512], start=True, stop=True)
                mm.then_inc(S["si_mm"], 1)
                if b:
                    head_sum(b - 1)
            head_sum(DEC_BATCH - 1)
            pe.wait_ge(S["sc_done"], 1)
            for n in range((QB - 2) * IDX_H):
                i, h = 2 + n // IDX_H, n % IDX_H
                if n >= 4:
                    pe.wait_ge(S["is_relu"], n - 3)
                half = slice(IDX_D * (h % 2), IDX_D * (h % 2) + IDX_D)
                for k, (c0, cn) in enumerate(cuts(P * (i + 1))):
                    mm = pe.matmul(ps[:, 2 * (n % 4) + k, 0:cn], oq[half, 12 + h // 2, i * P:(i + 1) * P],
                                   ki[half, c0:c0 + cn], start=True, stop=True)
                mm.then_inc(S["is_mm"], 1)
            mlp_start(pe, "pe")

            def scores(n):
                i, kv = n // KV, n % KV
                for g in range(GRP):
                    a = n * GRP + g
                    if a >= 2:
                        pe.wait_ge(S["at_exp"], a - 1)
                    for k, (c0, cn) in enumerate(cuts(P * (i + 1))):
                        bank = 2 * (a % 2) + k
                        pe.matmul(ps[:, bank, 0:cn], oq[:, GRP * kv + g, i * P:(i + 1) * P], oq[:, 8 + kv, c0:c0 + cn],
                                  start=True, stop=False, skip_group_check=True)
                        if i < 2:
                            mm = pe.matmul(ps[:, bank, i * P:(i + 1) * P], id_b[:, :], bias_b[:, :], start=False, stop=True,
                                           skip_group_check=True)
                        else:
                            mm = pe.matmul(ps[:, bank, 0:cn], id_b[:, :], mb[:, sc_off[i] + c0:sc_off[i] + c0 + cn],
                                           start=False, stop=True, skip_group_check=True)
                    mm.then_inc(S["at_mm"], 1)

            def values(n):
                i, kv = n // KV, n % KV
                pe.wait_ge(S["at_nrm"], GRP * (n + 1))
                for k in range(i + 2):
                    c = steps_before[n] + k
                    if k <= i:
                        if c >= 2:
                            pe.wait_ge(S["at_ptt"], c - 1)
                        for g in range(GRP):
                            mm = pe.transpose(quad(4 + c % 2)[:, g, :], pr[n % 2][:, g, k * P:(k + 1) * P], ident[:, :])
                        mm.then_inc(S["at_tr"], 1)
                    if k:
                        if k == 1 and n >= 2:
                            pe.wait_ge(S["at_o"], n - 1)
                        pe.wait_ge(S["at_ptt"], c)
                        pe.matmul(ps[:, 6 + n % 2, :], vtok[:, k - 1, kv * P:(kv + 1) * P], ptt[:, (c - 1) % 2, :],
                                  start=k == 1, stop=k == i + 1).then_inc(S["at_pv"], 1)

            scores(0)
            for n in range(GROUPS):
                if n + 1 < GROUPS:
                    scores(n + 1)
                values(n)
            pe.wait_ge(S["at_o"], GROUPS)
            pe.wait_ge(S["at_exp"], HEADS)

            def sample_values(G):
                s0 = 3 * (G % 2)
                pe.wait_ge(S["at_nrm"], HEADS + G + 1)
                for k in range(3):
                    tr = 3 * G + k
                    pe.wait_ge(S["sa_kts"], min(8 * (G + 2), 32))
                    if k == 2:
                        pe.wait_ge(S["sa_pt"], tr - 1)
                    if k < 2:
                        for q in range(4):
                            p = 4 * k + q
                            mm = pe.transpose(ps[:, 6 + k, q * P:(q + 1) * P], pr0[:, G % 2, p * P:(p + 1) * P], ident[:, :])
                    else:
                        mm = pe.transpose(ps[0:SMP, 6, 0:P], pr_new[:, G % 2, :], ident[:, :])
                    mm.then_inc(S["sa_ptr"], 1)
                pe.wait_ge(S["sa_pt"], 3 * G + 3)
                for b2 in range(2):
                    b = 2 * G + b2
                    pe.wait_ge(S[f"vp_in{b2}"], 16 * PAGES * (G + 1))
                    for kv in range(KV):
                        q4 = 2 * b2 + kv
                        out = ps[:, s0 + 2, 384 + 16 * q4:384 + 16 * (q4 + 1)]
                        for p in range(PAGES):
                            pe.matmul(out, vpg[b2][:, p, kv * P:(kv + 1) * P], pt_s[:, p, 32 * q4:32 * q4 + 16],
                                      start=p == 0, stop=False)
                        mm = pe.matmul(out, vtok[0:SMP, QB, kv * P:(kv + 1) * P], pt_s[0:SMP, PAGES, 32 * q4:32 * q4 + 16],
                                       start=False, stop=True)
                    mm.then_inc(S["vp_used"], 1)

            for G in range(DEC_BATCH // 2):
                s0 = 3 * (G % 2)
                if G >= 2:
                    pe.wait_ge(S["at_exp"], HEADS + G - 1)
                    pe.wait_ge(S["at_o"], GROUPS + G - 1)
                for t, (c0, cn) in enumerate(CUTS352):
                    pe.matmul(ps[:, s0 + t, 0:cn], esel_b[:, G, :], mb_s[:, c0:c0 + cn], start=True, stop=False,
                              skip_group_check=True)
                for b2 in range(2):
                    b = 2 * G + b2
                    pe.wait_ge(S[f"kp_in{b2}"], 16 * PAGES * (G + 1))
                    for s in range(4):
                        n = 4 * b + s
                        if n >= 2:
                            pe.wait_ge(S["sa_kts"], n - 1)
                        if s < 2 and b2 == 0 and G >= 2:
                            pe.wait_ge(S["sa_pt"], 3 * (G - 1))
                        for q in range(4):
                            mm = pe.transpose(ps[:, 6 + s % 2, q * P:(q + 1) * P],
                                              kpg[b2][:, 4 * (s % 2) + q, s // 2 * P:(s // 2 + 1) * P], ident[:, :])
                        mm.then_inc(S["sa_tr"], 1)
                    pe.wait_ge(S["sa_kts"], 4 * b + 4)
                    for kv in range(KV):
                        q4 = 2 * b2 + kv
                        rows_q = slice(32 * q4, 32 * q4 + 16)
                        q_rows = qs[:, b, GRP * kv:GRP * (kv + 1), :].rearrange("p h t -> p (h t)")
                        for t, (c0, cn) in enumerate(((0, 352), (352, 352), (704, 320))):
                            pe.matmul(ps[rows_q, t + s0, 0:cn], q_rows, kts[:, kv, c0:c0 + cn], start=False, stop=True,
                                      skip_group_check=True)
                        mm = pe.matmul(ps[rows_q, 2 + s0, 320:352], q_rows, oq[:, 8 + kv, SEQ:TOK], start=False, stop=True,
                                       skip_group_check=True)
                    mm.then_inc(S["sa_mm"], 1)
                if G:
                    sample_values(G - 1)
            sample_values(DEC_BATCH // 2 - 1)
            mlp_start(pe, "pe")
            pe.wait_ge(S["mix_h"], 2 * KT)
            pe.wait_ge(S["mix_l"], 2 * KT)
            units(pe, FIRST["att_out"], U_ATT_OUT, 2, unit(KT, xh, xl, CUTS352))
            mlp_start(pe, "pe")
            mlp(1)
            mlp_start(pe, "pe")
            y_pe(pe, norm_sum)

        def rest_of_act(act, own, split_hi, norm_squares, mlp):
            mlp_start(act, "act")
            split_hi(2, R_MIX1)
            act.dma_start(x_spill, x[:, :, :]).then_inc(S["x_spilled"], 16)
            act.wait_ge(S["x_spilled"], 32)
            mlp_start(act, "act")
            act.wait_ge(S["acst_in"], 32)
            own.did(act.activation(id_b[:, :], ident[:, :], ACT.Copy))
            own.did(act.activation(bias_b[:, :], acst[:, A_BIAS:A_BIAS + P], ACT.Copy))
            own.did(act.activation(flat(esel_b[:, :, :]), acst[0:SMP, A_ESEL:A_ESEL + 4 * P], ACT.Copy))
            for t in range(QB + 1):
                w, bank = P if t < QB else SMP, 2 * (t % 4)
                act.wait_ge(S["tk_mm"], t + 1)
                own.did(act.activation(kitok[0:w, t, :], ps[0:w, bank + 1, KV * P:KV * P + IDX_D], ACT.Copy))
                act.activation(vtok[0:w, t, :], ps[0:w, bank + 1, 0:KV * P], ACT.Copy).then_inc(S["tk_act"], 1)
            own.wait()
            act.wait_ge(S["tk_act"], QB + 1)
            act.wait_ge(S["tk_dve"], QB + 1)
            for name, tile in (("k", ktok), ("v", vtok), ("kidx", kitok)):
                tokens = "b (n p) k d -> p (b n) (k d)" if name != "kidx" else "b (n p) d -> p (b n) d"
                samples = "b t k d -> (b t) (k d)" if name != "kidx" else "b t d -> (b t) d"
                act.dma_start(O[name + "_p"][0].rearrange(tokens, p=P), tile[:, 0:QB, :]).then_inc(S["kv_out"], 16)
                act.dma_start(O[name + "_s"][0].rearrange(samples), tile[0:SMP, QB, :]).then_inc(S["kv_out"], 16)
            act.wait_ge(S["new_mm"], 1)
            act.activation(flat(new_relu[:, :, :]), ps[0:SMP, 6, 0:DEC_BATCH * SMP], ACT.Relu).then_inc(S["new_relu_r"], 1)
            for b in range(DEC_BATCH):
                for half in range(2):
                    act.wait_ge(S["si_tr"], 4 + 2 * b + half + 1)
                    if b >= 2:
                        act.wait_ge(S["si_mm"], b - 1)
                    act.activation(kit[b % 2][:, half * 512:(half + 1) * 512], ps[0:IDX_D, 6 + half, :], ACT.Copy)\
                        .then_inc(S["si_kt"], 1)
                act.wait_ge(S["si_mm"], b + 1)
                if b >= 2:
                    act.wait_ge(S["si_acc"], b - 1)
                bank = 2 * (b % 2)
                act.activation(relu_s[:, b % 2, :], ps[0:SMP, bank:bank + 2, :].rearrange("p a n -> p (a n)"), ACT.Relu)\
                    .then_inc(S["si_relu"], 1)
            act.wait_ge(S["new_acc"], 1)
            for n in range((QB - 2) * IDX_H):
                w = P * (3 + n // IDX_H)
                act.wait_ge(S["is_mm"], n + 1)
                if n >= 2:
                    act.wait_ge(S["is_acc"], n - 1)
                act.activation(relu[:, n % 2, 0:w], bank2(2 * (n % 4), w), ACT.Relu).then_inc(S["is_relu"], 1)
            act.wait_ge(S["kv_out"], 16 * 6)
            mlp_start(act, "act")

            def exps(n):
                w = P * (n // KV + 1)
                for g in range(GRP):
                    a = n * GRP + g
                    act.wait_ge(S["at_max"], a + 1)
                    if g == 0 and n >= 2:
                        act.wait_ge(S["at_tr"], steps_before[n - 1])
                        act.wait_ge(S["at_nrm"], GRP * (n - 1))
                    act.activation(pr[n % 2][:, g, 0:w], bank2(2 * (a % 2), w), ACT.Exp, bias=mx[:, a % 4:a % 4 + 1], scale=SCALE,
                                   accum_out=den[:, a % 8:a % 8 + 1]).then_inc(S["at_exp"], 1)

            def ptt_copies(n):
                for k in range(n // KV + 1):
                    c = steps_before[n] + k
                    act.wait_ge(S["at_tr"], c + 1)
                    if c >= 2:
                        act.wait_ge(S["at_pv"], c - 1)
                    act.activation(ptt[:, c % 2, :], ps[:, 4 + c % 2, :], ACT.Copy).then_inc(S["at_ptt"], 1)

            exps(0)
            for n in range(GROUPS):
                if n + 1 < GROUPS:
                    exps(n + 1)
                ptt_copies(n)

            def sample_copies(G):
                for k in range(3):
                    act.wait_ge(S["sa_ptr"], 3 * G + k + 1)
                    if G:
                        act.wait_ge(S["vp_used"], 2 * G)
                    if k < 2:
                        act.activation(flat(pt_s[:, 4 * k:4 * k + 4, :]), ps[:, 6 + k, :], ACT.Copy).then_inc(S["sa_pt"], 1)
                    else:
                        act.activation(pt_s[0:SMP, PAGES, :], ps[0:SMP, 6, 0:P], ACT.Copy).then_inc(S["sa_pt"], 1)

            act.wait_ge(S["at_nrm"], HEADS)
            for G in range(DEC_BATCH // 2):
                for n in range(8 * G, 8 * G + 8):
                    act.wait_ge(S["sa_tr"], n + 1)
                    if n >= 4:
                        act.wait_ge(S["sa_mm"], n // 4)
                    act.activation(kts[:, n // 2 % 2, n % 2 * 512:(n % 2 + 1) * 512], ps[:, 6 + n % 2, :], ACT.Copy)\
                        .then_inc(S["sa_kts"], 1)
                act.wait_ge(S["at_max"], HEADS + G + 1)
                if G >= 2:
                    act.wait_ge(S["sa_ptr"], 3 * (G - 1))
                    act.wait_ge(S["at_nrm"], HEADS + G - 1)
                bias, total = mx[:, G % 4:G % 4 + 1], den[:, G:G + 1]
                s0 = 3 * (G % 2)
                own.then(act.activation(pr0[:, G % 2, 0:704].rearrange("p (a n) -> p a n", a=2), ps[:, s0:s0 + 2, 0:352], ACT.Exp,
                                        bias=bias, scale=SCALE, accum_out=total))
                own.then(act.activation(pr0[:, G % 2, 704:1024], ps[:, s0 + 2, 0:320], ACT.Exp, bias=bias, scale=SCALE,
                                        accum_out=den[:, 4 + G:5 + G]))
                act.activation(pr_new[:, G % 2, :], ps[:, s0 + 2, 320:352], ACT.Exp, bias=bias, scale=SCALE,
                               accum_out=den_new[:, G:G + 1]).then_inc(S["at_exp"], 1)
                if G:
                    sample_copies(G - 1)
            sample_copies(DEC_BATCH // 2 - 1)
            mlp_start(act, "act")
            act.dma_start(x[:, 0:4, :], x_spill[:, 0:4, :]).then_inc(S["x_back0"], 16)
            act.dma_start(x[:, 4:8, :], x_spill[:, 4:8, :]).then_inc(S["x_back1"], 16)
            for m in range(KT):
                act.activation(xh[:, m, :], oq[:, m, :], ACT.Copy).then_inc(S["mix_h"], 1)
            mlp_start(act, "act")
            mlp(1)
            mlp_start(act, "act")
            y_act(act, norm_squares)

        def rest_of_dve(dve, own, split_lo, norm_mean, add_unit, mlp):
            mlp_start(dve, "dve")
            split_lo(2, R_MIX1)
            first = FIRST["att_in"]
            r3 = rstd[:, :].rearrange("p (a t) -> p a t", a=3)

            def project_unit(j, off):
                dve.wait_ge(mm_out, j + off + 3)
                dve.tensor_tensor(oq[:, ds(j + off - first, 1), :].rearrange("p o (a t) -> p (o a) t", a=3),
                                  set_view(j, 0, 3)[:, :, 0:352], r3, ALU.mult).then_inc(set_free, 1)

            units(dve, first, 16, 2, project_unit)
            j = first + 16
            dve.wait_ge(mm_out, j + 3)
            for out in (ki[0:IDX_D, :], ki[IDX_D:2 * IDX_D, :]):
                own.did(dve.tensor_tensor(out.rearrange("p (a t) -> p a t", a=3), set_view(j, 0, 3)[0:IDX_D, :, 0:352],
                                          r3[0:IDX_D], ALU.mult))
            dve.tensor_tensor(wi[:, :].rearrange("p (a t) -> p a t", a=3), set_view(j, 0, 3)[IDX_D:IDX_D + IDX_H, :, 0:352],
                              r3[IDX_D:IDX_D + IDX_H], ALU.mult).then_inc(set_free, 1)
            mlp_start(dve, "dve")

            for t in range(QB + 1):
                w, bank = P if t < QB else SMP, 2 * (t % 4)
                dve.wait_ge(S["tk_mm"], t + 1)
                own.did(dve.tensor_copy(wic[0:w, t, :], ps[0:w, bank, KV * P:KV * P + IDX_H]))
                dve.tensor_copy(ktok[0:w, t, :], ps[0:w, bank, 0:KV * P]).then_inc(S["tk_dve"], 1)
            for par in range(2):
                own.did(dve.tensor_copy(qis[:, :, par::2, :].rearrange("p b h t -> p h b t"),
                                        oq[IDX_D * par:IDX_D * (par + 1), 12:16, SEQ:TOK].rearrange("p h (b t) -> p h b t", t=DEC_SEQ)))
            dve.wait_ge(S["tk_mm"], QB + 2)
            dve.wait_ge(S["acst_in"], 32)
            own.then(dve.tensor_copy(w_rows[:, 0:SMP], ps[0:SMP, 2, 0:SMP]))
            dve.tensor_tensor(w_tok[:, :, :], acst[0:SMP, A_TOK:A_TOK + DEC_BATCH * SMP].rearrange("p (b t) -> p b t", b=DEC_BATCH),
                              w_rows[:, 0:SMP].unsqueeze(1).to_broadcast([SMP, DEC_BATCH, SMP]), ALU.mult).then_inc(S["w_tok_r"], 1)
            dve.wait_ge(S["new_acc"], 1)
            dve.tensor_tensor(sc_s[:, PAST:], ps[0:SMP, 7, 0:SMP], acst[0:SMP, A_CAPS:A_CAPS + SMP], ALU.min)\
                .then_inc(S["new_out"], 1)
            dve.wait_ge(S["si_acc"], DEC_BATCH)
            dve.tensor_copy(sc_s[:, 0:PAST], ps[0:SMP, 4:6, :].rearrange("p a n -> p (a n)")).then_inc(S["sc_done"], 1)
            for n in range((QB - 2) * IDX_H):
                i, h = 2 + n // IDX_H, n % IDX_H
                w = P * (i + 1)
                dst = sc[:, sc_off[i]:sc_off[i] + w]
                dve.wait_ge(S["is_relu"], n + 1)
                if h == 0:
                    dve.tensor_scalar(dst, relu[:, n % 2, 0:w], wic[:, i, 0:1], None, ALU.mult).then_inc(S["is_acc"], 1)
                else:
                    dve.wait_ge(S["is_acc"], n)
                    dve.scalar_tensor_tensor(dst, relu[:, n % 2, 0:w], wic[:, i, h:h + 1], dst, ALU.mult, ALU.add)\
                        .then_inc(S["is_acc"], 1)
                if h == IDX_H - 1:
                    dve.wait_ge(S["is_acc"], n + 1)
                    own.did(dve.tensor_tensor(dst[:, w - P:w], dst[:, w - P:w], acst[:, A_CAP:A_CAP + P], ALU.min))
            own.wait()
            dve.wait_ge(S["new_out"], 1)
            dve.wait_ge(S["sc_done"], 1)
            dve.wait_ge(S["kv_out"], 16 * 6)

            rows_of = [(sc[:, sc_off[i]:sc_off[i] + P * (i + 1)], mb[:, sc_off[i]:sc_off[i] + P * (i + 1)], P, P * (i + 1))
                       for i in range(2, QB)] + [(sc_s[:, :], mb_s[:, :], SMP, TOK)]
            K = TOPK

            def bit(k, n=1):
                return bits[:, ds(k, n)]

            def count(limit, op):
                for q, (s, _, pn, w) in enumerate(rows_of):
                    lim = limit if isinstance(limit, float) else limit[0:pn, q:q + 1].bitcast(F32)
                    own.then(dve.tensor_scalar(scr[q % 2][0:pn, 0:w], s, lim, 0.0, op, ALU.add, accum_out=cnt[0:pn, q:q + 1]))

            own.then(dve.memset(cnt[:, :], 0.0))
            count(0.0, ALU.is_ge)
            own.then(dve.tensor_scalar(neg[:, :], cnt[:, :], float(K), None, ALU.is_lt))
            own.then(dve.tensor_scalar(cand[:, :], neg[:, :], -2.0 ** 31, None, ALU.mult))
            with own.loop(BITS, 4 + NB) as k:
                own.then(dve.tensor_tensor(trial[:, :], cand[:, :], bit(k).to_broadcast([P, NB]), ALU.bitwise_or))
                count(trial, ALU.is_ge)
                own.then(dve.scalar_tensor_tensor(acc[:, :], cnt[:, :], float(K), neg[:, :], ALU.is_ge, ALU.not_equal))
                own.then(dve.tensor_tensor(trial[:, :], acc[:, :], acst[:, ds(A_BITF + k, 1)].to_broadcast([P, NB]), ALU.mult))
                own.then(dve.tensor_tensor(cand[:, :], cand[:, :], trial[:, :], ALU.bitwise_or))
            part = [bits[:, BITS + k:BITS + k + 1].to_broadcast([P, NB]) for k in range(3)]
            own.then(dve.tensor_tensor(hi16[:, :], cand[:, :], part[2], ALU.bitwise_and))
            own.then(dve.tensor_tensor(trial[:, :], cand[:, :], part[0], ALU.bitwise_and))
            own.then(dve.tensor_tensor(trial[:, :], trial[:, :], neg[:, :], ALU.add))
            own.then(dve.tensor_tensor(carry[:, :], trial[:, :], part[1], ALU.bitwise_and))
            own.then(dve.tensor_tensor(trial[:, :], trial[:, :], part[0], ALU.bitwise_and))
            own.then(dve.tensor_tensor(hi16[:, :], hi16[:, :], carry[:, :], ALU.add))
            own.then(dve.tensor_tensor(cand[:, :], hi16[:, :], trial[:, :], ALU.bitwise_or))
            count(cand, ALU.is_gt)
            own.then(dve.tensor_scalar(quota[:, :], cnt[:, :], -1.0, float(K), ALU.mult, ALU.add))
            for q, (s, m, pn, w) in enumerate(rows_of):
                lim = cand[0:pn, q:q + 1].bitcast(F32)
                eq, pre = scr[0][0:pn, 0:w], scr[1][0:pn, 0:w]
                own.then(dve.tensor_scalar(eq, s, lim, None, ALU.is_equal))
                own.then(dve.tensor_tensor_scan(pre, ones[0:pn, 0:1].to_broadcast([pn, w]), eq, 0.0, ALU.mult, ALU.add))
                own.then(dve.scalar_tensor_tensor(eq, pre, quota[0:pn, q:q + 1], eq, ALU.is_le, ALU.mult))
                own.then(dve.scalar_tensor_tensor(pre, s, lim, eq, ALU.is_gt, ALU.add))
                own.then(dve.tensor_scalar(m, pre, -1.0, -MASKED, ALU.add, ALU.mult))
            own.then(dve.tensor_copy(qs[:, :, :, :].rearrange("p b h t -> p h b t"),
                                     oq[:, 0:Q_HEADS, SEQ:TOK].rearrange("p h (b t) -> p h b t", t=DEC_SEQ)))
            mlp_start(dve, "dve")

            def maximum(a, view):
                col = mx[:, a % 4:a % 4 + 1]
                own.then(dve.tensor_reduce(col, view, AX, ALU.max))
                dve.tensor_scalar(col, col, -SCALE, None, ALU.mult).then_inc(S["at_max"], 1)

            def head_max(a):
                if a < HEADS:
                    dve.wait_ge(S["at_mm"], a + 1)
                    if a >= 4:
                        dve.wait_ge(S["at_exp"], a - 3)
                    maximum(a, bank2(2 * (a % 2), P * (a // (GRP * KV) + 1)))

            def output(n):
                i, kv = n // KV, n % KV
                dve.wait_ge(S["at_pv"], steps_before[n + 1])
                dve.tensor_copy(oq[:, GRP * kv:GRP * (kv + 1), i * P:(i + 1) * P], quad(6 + n % 2)).then_inc(S["at_o"], 1)

            for a in range(GRP):
                head_max(a)
            for n in range(GROUPS):
                w = P * (n // KV + 1)
                for g in range(GRP):
                    a = n * GRP + g
                    head_max(a + GRP)
                    dve.wait_ge(S["at_exp"], a + 1)
                    own.then(dve.reciprocal(rden[:, a % 8:a % 8 + 1], den[:, a % 8:a % 8 + 1]))
                    dve.tensor_scalar(pr[n % 2][:, g, 0:w], pr[n % 2][:, g, 0:w], rden[:, a % 8:a % 8 + 1], None, ALU.mult)\
                        .then_inc(S["at_nrm"], 1)
                if n:
                    output(n - 1)
            output(GROUPS - 1)

            def sample_max(G):
                dve.wait_ge(S["sa_mm"], 2 * G + 2)
                if G == 0:
                    dve.wait_ge(S["at_exp"], HEADS)
                s0 = 3 * (G % 2)
                col = mx[:, G % 4:G % 4 + 1]
                own.then(dve.tensor_reduce(rden[:, G % 2:G % 2 + 1], ps[:, s0:s0 + 3, 0:352], mybir.AxisListType.XY, ALU.max))
                dve.tensor_scalar(col, rden[:, G % 2:G % 2 + 1], -SCALE, None, ALU.mult).then_inc(S["at_max"], 1)

            def sample_output(G):
                dve.wait_ge(S["vp_used"], 2 * G + 2)
                for b2 in range(2):
                    for kv in range(KV):
                        q4, b = 2 * b2 + kv, 2 * G + b2
                        ins = dve.tensor_copy(oq[:, GRP * kv:GRP * (kv + 1), SEQ + b * DEC_SEQ:SEQ + (b + 1) * DEC_SEQ],
                                              ps[:, 3 * (G % 2) + 2, 384 + 16 * q4:400 + 16 * q4].rearrange("p (h t) -> p h t", h=GRP))
                        if q4 < 3:
                            own.did(ins)
                        else:
                            ins.then_inc(S["at_o"], 1)

            dve.wait_ge(S["at_nrm"], HEADS)
            for G in range(DEC_BATCH // 2):
                sample_max(G)
                dve.wait_ge(S["at_exp"], HEADS + G + 1)
                total = rden[:, 4 + G:5 + G]
                own.then(dve.tensor_tensor(total, den[:, G:G + 1], den[:, 4 + G:5 + G], ALU.add))
                own.then(dve.tensor_tensor(total, total, den_new[:, G:G + 1], ALU.add))
                own.then(dve.reciprocal(total, total))
                own.did(dve.tensor_scalar(pr0[:, G % 2, :], pr0[:, G % 2, :], total, None, ALU.mult))
                dve.tensor_scalar(pr_new[:, G % 2, :], pr_new[:, G % 2, :], total, None, ALU.mult).then_inc(S["at_nrm"], 1)
                if G:
                    sample_output(G - 1)
            sample_output(DEC_BATCH // 2 - 1)
            mlp_start(dve, "dve")
            for m in range(KT):
                dve.wait_ge(S["mix_h"], KT + m + 1)
                dve.tensor_tensor(xl[:, m, :], oq[:, m, :], xh[:, m, :].bitcast(F32), ALU.subtract).then_inc(S["mix_l"], 1)
            first = FIRST["att_out"]
            dve.wait_ge(S["x_back0"], 32)
            units(dve, first, 4, 2, add_unit(first))
            dve.wait_ge(S["x_back1"], 32)
            units(dve, first + 4, 4, 2, lambda j, off: add_unit(first)(j, off))
            mlp_start(dve, "dve")
            mlp(1)
            mlp_start(dve, "dve")
            y_dve(dve, norm_mean)

        @block.sync
        def _(sp):
            vec = [("norm_mix", 0, R_MIX0), ("norm_mix", 1, R_MIX1), ("norm_mlp", 0, R_MLP0), ("norm_mlp", 1, R_MLP1)]
            for name, l, r in vec:
                sp.dma_start(cst_rows[r:r + KT, :], A[name][l].rearrange("(m c) -> m c", c=P)).then_inc(S["start_in"], 16)
            sp.dma_start(cst_rows[R_FIN:R_FIN + KT, :], A["norm_final"].rearrange("(m c) -> m c", c=P)).then_inc(S["start_in"], 16)
            sp.dma_start(cst_rows[R_CONV:R_CONV + CONV_W * CT, :],
                         A["w_conv"][0].rearrange("i (m c) -> (i m) c", c=P)).then_inc(S["start_in"], 16)
            for name, r in (("b_conv", R_BCONV), ("rg_ba", R_BA), ("rg_bx", R_BX), ("rg_lambda", R_LAM)):
                sp.dma_start(cst_rows[r:r + RT, :], A[name][0].rearrange("(m c) -> m c", c=P)).then_inc(S["start_in"], 16)
            sp.dma_start(cst_rows[R_DN:R_DN + 1, :], A["dn_norm"]).then_inc(S["start_in"], 16)
            sp.dma_start(conv_rows[:, :], A["state_conv"][0].rearrange("b i c -> (b i) c")).then_inc(S["start_in"], 16)
            sp.dma_start(h0_rows[:, :], A["state_h"][0]).then_inc(S["start_in"], 16)
            sp.dma_start(nea[32:32 + DN_H, :], A["dn_a_log"].rearrange("a h -> h a")).then_inc(S["start_in"], 16)
            sp.dma_start(dtb[32:32 + DN_H, :], A["dn_dt_bias"].rearrange("a h -> h a")).then_inc(S["start_in"], 16)

            def load(src, kts):
                def body(j, off):
                    sp.wait_ge(w_split, j + off + 1)
                    sp.dma_start(w_raw[:, j % 2, 0:kts * P].rearrange("p (k n) -> p k n", k=kts), src(j, off))\
                        .then_inc(w_loaded[j % 2], 16)
                return body

            first = FIRST["rec_in"]
            units(sp, first, 24, 2, load(lambda j, off: w_in_rec[:, :, ds((j + off - first) * P, P)], KT))
            j = first + 24
            sp.wait_ge(w_split, j + 1)
            last = w_raw[:, j % 2, :].rearrange("p (k n) -> p k n", k=KT)
            with nc.allow_non_contiguous_dma(reason="eight narrow columns"):
                sp.dma_start(last[:, :, 0:DN_H], w_in_rec[:, :, 24 * P:24 * P + DN_H]).then_inc(w_loaded[j % 2], 16)
                sp.dma_start(last[:, :, 32:32 + DN_H], w_in_rec[:, :, 24 * P + DN_H:24 * P + 2 * DN_H])\
                    .then_inc(w_loaded[j % 2], 16)
            sp.wait_ge(S["wax_zero"], 1)
            for g, name in enumerate(("rg_wa", "rg_wx")):
                for half in range(2):
                    o = 64 * half
                    sp.dma_start(wax[o:o + 64, g, :, o:o + 64], A[name][0].rearrange("(m two) i j -> two i m j", two=2)[half])\
                        .then_inc(S["gate_w"], 16)
            sp.dma_start(reset[32:32 + DN_H, :], A["row_reset"]).then_inc(S["gate_w"], 16)
            first = FIRST["rec_out"]
            units(sp, first, U_REC_OUT, 2, load(lambda j, off: w_out_rec[:, :, ds((j + off - first) * P, P)], KT))
            mlp_loads(sp, 0, load)
            rest_of_sync(sp, load)

        @block.gpsimd
        def _(pool):
            own = Chain(pool, pool_chain)
            pool.memset(eps_col, EPS).then_inc(w_split, 1)
            pool.memset(one_col, 1.0).then_inc(w_split, 1)
            own.then(pool.memset(ident[:, :], 0.0))
            own.then(pool.affine_select(out=ident[:, :], in_=ident[:, :], compare_op=ALU.not_equal, fill=1.0, base=0,
                                        pattern=[[-1, P]], channel_multiplier=1))
            own.did(pool.memset(ones[:, :], 1.0))
            pool.drain().then_inc(const_in, 1)

            def split(kts, extra=0):
                def body(j, off):
                    pool.wait_ge(w_loaded[j % 2], 16 * (j // 2 + 1 + extra) + off * 8)
                    pool.wait_ge(mm_out, j + off + 1)
                    n = kts * P
                    pool.tensor_tensor(w_hi[:, j % 2, 0:n], w_raw[:, j % 2, 0:n], ones[:, 0:1].to_broadcast([P, n]),
                                       ALU.mult).then_inc(w_hi_done, 1)
                    pool.wait_ge(w_hi_done, j + off + 1)
                    pool.tensor_tensor(w_lo[:, j % 2, 0:n], w_raw[:, j % 2, 0:n], w_hi[:, j % 2, 0:n].bitcast(F32),
                                       ALU.subtract).then_inc(w_split, 1)
                return body

            extra = {0: 0, 1: 0}

            def split_units(first, count, per, kts):
                units(pool, first, count, per,
                      lambda j, off: split(kts, extra[j % 2])(j, off))

            def mlp_split(l):
                first = FIRST[f"mlp{l}"]
                with pool.Fori(0, FF_CHUNKS) as c:
                    for q in range(12):
                        split(KT if q < FT else FT, extra[(first + q) % 2])(first + q, c * 12)

            end_phase(pool, "pool")
            split_units(FIRST["rec_in"], 24, 2, KT)
            extra[0] += 1
            split_units(FIRST["rec_in"] + 24, 1, 1, KT)
            pool.wait_ge(mm_out, 2 + U_REC_IN)
            pool.memset(wax[:, :, :, :], 0.0).then_inc(S["wax_zero"], 1)
            end_phase(pool, "pool")
            end_phase(pool, "pool")
            own.then(pool.memset(rows[:, :], 0.0))
            own.then(pool.memset(dn["st"][:, :, :], 0.0))
            end_phase(pool, "pool")
            end_phase(pool, "pool")

            def pool_chunk(c, t0, w, levels):
                pool.wait_ge(S["st_r"], c + 1)
                own.did(pool.tensor_tensor(small[:, 4:5], one_col, one_col, ALU.mult))
                pool.tensor_copy(rowc[:, 0:w], rows[:, ds(t0, w)]).then_inc(S["rowc_cp"], 1)
                pool.tensor_copy(dn["kc"][:, :, 0:w], qkvz[:, 4:8, ds(t0, w)]).then_inc(S["kc_cp"], 1)
                pool.tensor_copy(dn["vc"][:, :, 0:w], qkvz[:, 8:12, ds(t0, w)]).then_inc(S["vc_cp"], 1)
                pool.wait_ge(S["lm_r"], c + 1)
                for l in range(levels):
                    pool.tensor_tensor(dn[f"lo{l}"][0:w, :, 0:w], dn["lm"][0:w, :, 0:w],
                                       cst[0:w, C_LEVEL + l:C_LEVEL + l + 1, 0:w].to_broadcast([w, DN_H, w]),
                                       ALU.mult).then_inc(S["lo_r"], 1)

            with own.loop(QB, 1) as c:
                pool_chunk(c, c * P, P, LEVELS)
            pool_chunk(QB, SEQ, SMP, 1)
            end_phase(pool, "pool")
            split_units(FIRST["rec_out"], U_REC_OUT, 2, KT)
            mlp_split(0)
            rest_of_pool(pool, split_units, mlp_split)

        @block.tensor
        def _(pe):
            pe.wait_ge(const_in, 1)
            pe.wait_ge(S["start_in"], 16 * 15)
            pe.transpose(ps[:, 0, 0:R_ALL], cst_rows[:, :], ident[0:R_ALL, 0:R_ALL]).then_inc(mm_out, 1)
            nh = DEC_BATCH * 3
            for m in range(CT):
                pe.transpose(ps[:, 1, m * nh:(m + 1) * nh], conv_rows[:, m * P:(m + 1) * P], ident[0:nh, 0:nh])
            for m in range(RT):
                o = CT * nh + m * DEC_BATCH
                last = pe.transpose(ps[:, 1, o:o + DEC_BATCH], h0_rows[:, m * P:(m + 1) * P],
                                    ident[0:DEC_BATCH, 0:DEC_BATCH])
            last.then_inc(mm_out, 1)
            pe.wait_ge(S["tok_in"], 16 * 3)
            for k in range(2 * (QB + 1)):
                t, half = k // 2, k % 2
                w = P if t < QB else SMP
                if k >= 6:
                    pe.wait_ge(S["xt_act"] if k % 2 == 0 else S["xt_dve"], (k - 6) // 2 + 1)
                for q in range(4):
                    f = half * 4 + q
                    last = pe.transpose(quad(2 + k % 6)[:, q, 0:w], xtok[0:w, t, f * P:(f + 1) * P], ident[0:w, 0:w])
                last.then_inc(S["xt_mm"], 1)
            end_phase(pe, "pe")

            def norm_sum(n, split=True):
                pe.wait_ge(S["sq_added"], 8 * (n + 1))
                pe.matmul(ps[:, 6, :], ones[:, :], sumsq[:, 0:512], start=True, stop=True)
                pe.matmul(ps[:, 7, :], ones[:, :], sumsq[:, 512:1024], start=True, stop=True)
                pe.matmul(ps[:, 5, 0:SMP], ones[:, :], sumsq[:, SEQ:TOK], start=True, stop=True).then_inc(S["ss_mm"], 1)
                if split:
                    pe.wait_ge(S["xh_ready"], 8 * (n + 1))
                    pe.wait_ge(S["xl_ready"], 8 * (n + 1))
                pe.wait_ge(S["ms_ready"], n + 1)

            def unit(kts, hi, lo, cuts):
                def body(j, off):
                    pe.wait_ge(w_split, j + off + 3)
                    pe.wait_ge(set_free, j + off + 1)
                    passes = ((w_hi, hi), (w_hi, lo), (w_lo, hi))
                    for k in range(kts):
                        for p, (w, r) in enumerate(passes):
                            for t, (c0, n) in enumerate(cuts):
                                mm = pe.matmul(ps[:, 3 * (j % 2) + t, 0:n], w[:, j % 2, k * P:(k + 1) * P],
                                               r[:, k, c0:c0 + n], start=(k == 0 and p == 0),
                                               stop=(k == kts - 1 and p == 2))
                    mm.then_inc(mm_out, 1)
                return body

            norm_sum(0)
            units(pe, FIRST["rec_in"], 24, 2, unit(KT, xh, xl, CUTS512))
            units(pe, FIRST["rec_in"] + 24, 1, 1, unit(KT, xh, xl, CUTS512))
            end_phase(pe, "pe")

            nt = 3 + DEC_BATCH * 3
            for k in range(4):
                for q in range(4):
                    last = pe.transpose(ps[0:nt, 6 + k % 2, q * P:(q + 1) * P], ctail[:, 4 * k + q, :], ident[:, :])
                last.then_inc(S["tail_mm"], 1)
                if k < 3 and k >= 1:
                    pe.wait_ge(S["tail_sb"], k)
            pe.wait_ge(S["gate_w"], 80)
            for m in range(RT):
                for g in range(2):
                    if m > 0:
                        pe.wait_ge(S["ri_read"], 2 * (m - 1) + g + 1)
                    for t, (c0, n) in enumerate(CUTS512):
                        mm = pe.matmul(ps[:, 3 * g + t, 0:n], wax[:, g, m, :], xr[:, m, c0:c0 + n], start=True, stop=True)
                    mm.then_inc(S["ri_mm"], 1)
            pe.wait_ge(S["rg_done"], RT)
            for m in range(RT):
                last = pe.transpose(ps[0:DEC_BATCH + 1, 6, m * P:(m + 1) * P], hT[:, m, :], ident[:, :])
            last.then_inc(S["ht_mm"], 1)
            end_phase(pe, "pe")
            end_phase(pe, "pe")

            def column_sums(n):
                g = n % 2
                pe.wait_ge(S["cn_sq"], n + 1)
                if n >= 2:
                    pe.wait_ge(S["cn_sqrt"], n - 1)
                for t, (c0, w) in enumerate(CUTS352):
                    mm = pe.matmul(ps[:, 3 * g + t, 0:w], ones[:, :], r_t[:, g, c0:c0 + w], start=True, stop=True)
                mm.then_inc(S["cn_mm"], 1)

            for n in range(8):
                column_sums(n)
            end_phase(pe, "pe")

            def pe_chunk(c, t0, w, levels, smp):
                pe.wait_ge(S["rowc_cp"], c + 1)
                pe.wait_ge(S["o_st"], c + 1)
                pe.transpose(ps[0:w, 2, 0:P], rowc[:, 0:w], ident[:, :]).then_inc(S["pe_col"], 1)
                pe.wait_ge(S["st_r"], c + 1)
                for bank, s in ((0, C_SELG), (1, C_SELB)):
                    for h in range(DN_H):
                        mm = pe.matmul(quad(bank)[:, h, 0:w], cst[:, s + h, :], rows[:, ds(t0, w)], start=True, stop=True)
                mm.then_inc(S["pe_bc"], 1)
                pe.wait_ge(S["kc_cp"], c + 1)
                for h in range(DN_H):
                    pe.matmul(quad(3)[0:w, h, 0:w], dn["kc"][:, h, 0:w], dn["kc"][:, h, 0:w], start=True, stop=True)
                for h in range(DN_H):
                    mm = pe.matmul(quad(4)[0:w, h, 0:w], dn["kc"][:, h, 0:w],
                                   qkvz[:, h, ds(t0, w)], start=True, stop=True)
                mm.then_inc(S["pe_kk"], 1)
                for h in range(DN_H):
                    mm = pe.transpose(quad(6)[0:w, h, :], dn["kc"][:, h, 0:w], ident[:, :])
                mm.then_inc(S["pe_kt"], 1)
                pe.wait_ge(S["vc_cp"], c + 1)
                for h in range(DN_H):
                    mm = pe.transpose(quad(7)[0:w, h, :], dn["vc"][:, h, 0:w], ident[:, :])
                mm.then_inc(S["pe_vt"], 1)
                pe.wait_ge(S["lt_r"], c + 1)
                for h in range(DN_H):
                    mm = pe.transpose(quad(5)[0:w, h, 0:w], dn["lt"][0:w, h, 0:w], ident[0:w, 0:w])
                mm.then_inc(S["pe_l"], 1)
                pe.wait_ge(S["x0_r"], c + 1)
                for l in range(levels):
                    pe.wait_ge(S["lo_r"], c * LEVELS + l + 1)
                    if l:
                        pe.wait_ge(S["x_sb"], c * LEVELS + l)
                    for h in range(DN_H):
                        mm = pe.matmul(quad(3)[0:w, h, 0:w], dn[f"lo{l}"][0:w, h, 0:w], dn["xti"][0:w, h, 0:w],
                                       start=True, stop=True)
                    mm.then_inc(S["pe_y"], 1)
                    pe.wait_ge(S["y_sb"], c * LEVELS + l + 1)
                    for h in range(DN_H):
                        pe.matmul(quad(4)[0:w, h, 0:w], dn["yy"][0:w, h, 0:w], dn["xi"][0:w, h, 0:w], start=True, stop=True)
                    for h in range(DN_H):
                        mm = pe.matmul(quad(5)[0:w, h, 0:w], dn["xi"][0:w, h, 0:w], dn["yy"][0:w, h, 0:w],
                                       start=True, stop=True)
                    mm.then_inc(S["pe_x"], 1)
                pe.wait_ge(S["kbg_r"], c + 1)
                pe.wait_ge(S["dec_r"], c + 1)
                pe.wait_ge(S["egb_r"], c + 1)
                if not smp:
                    for h in range(DN_H):
                        mm = pe.matmul(quad(0)[:, h, :], dn["kbg"][:, h, :], dn["st"][:, h, :], start=True, stop=True)
                    mm.then_inc(S["pe_ks"], 1)
                else:
                    pe.wait_ge(S["qg_r"], c + 1)
                    pe.wait_ge(S["s0_in"], 16)
                    kq_out = ps[:, 0, 0:DN_H * 2 * SMP].rearrange("p (h a t) -> p h a t", h=DN_H, a=2)
                    for b in range(DEC_BATCH):
                        sl = slice(b * DEC_SEQ, (b + 1) * DEC_SEQ)
                        for h in range(DN_H):
                            mm = pe.matmul(kq_out[:, h, :, sl], s0[:, b, h, :], kq_s[:, h, :, sl], start=True, stop=True)
                    mm.then_inc(S["pe_ks"], 1)
                    pe.wait_ge(S["y_sb"], QB * LEVELS + 2)
                    for h in range(DN_H):
                        mm = pe.transpose(quad(1)[0:w, h, :], ks_s[:, h, 0, :], ident[:, :])
                    mm.then_inc(S["pe_ks"], 1)
                pe.wait_ge(S["rr_r"], c + 1)
                pe.wait_ge(S["x_sb"], c * LEVELS + levels)
                for h in range(DN_H):
                    mm = pe.matmul(quad(1)[0:w, h, :], dn["xti"][0:w, h, 0:w], dn["rr"][0:w, h, :], start=True, stop=True)
                mm.then_inc(S["pe_vn"], 1)
                pe.wait_ge(S["vn_r"], c + 1)
                pe.wait_ge(S["attn_r"], c + 1)
                pe.wait_ge(S["cols_r"], c + 1)
                if not smp:
                    pe.wait_ge(S["qg_r"], c + 1)
                    for h in range(DN_H):
                        pe.matmul(quad(2)[:, h, :], dn["st"][:, h, :], dn["qg"][:, h, :], start=True, stop=False)
                        mm = pe.matmul(quad(2)[:, h, :], dn["vn"][:, h, :], dn["attn"][:, h, :], start=False, stop=True)
                    mm.then_inc(S["pe_o"], 1)
                    pe.wait_ge(S["kd_r"], c + 1)
                    for h in range(DN_H):
                        mm = pe.matmul(quad(6)[:, h, :], dn["kd"][:, h, :], dn["vn"][:, h, :], start=True, stop=True)
                    mm.then_inc(S["pe_ds"], 1)
                else:
                    for h in range(DN_H):
                        mm = pe.matmul(quad(2)[:, h, 0:w], dn["vn"][0:w, h, :], dn["attn"][0:w, h, 0:w],
                                       start=True, stop=True)
                    mm.then_inc(S["pe_o"], 1)
                    pe.wait_ge(S["vb_r"], c + 1)
                    for b in range(DEC_BATCH):
                        pe.wait_ge(S["kdm_r"], b + 1)
                        if b >= 4:
                            pe.wait_ge(S["s0_out"], b - 3)
                        for h in range(DN_H):
                            mm = pe.matmul(quad(4 + b % 4)[:, h, :], kdm[0:w, b, h, :], dn["vn"][0:w, h, :],
                                           start=True, stop=True)
                        mm.then_inc(S["pe_ds"], 1)

            with pe.Fori(0, QB) as c:
                pe_chunk(c, c * P, P, LEVELS, False)
            pe_chunk(QB, SEQ, SMP, 1, True)
            for n in range(8, 12):
                column_sums(n)
            end_phase(pe, "pe")
            pe.wait_ge(S["mix_h"], KT)
            pe.wait_ge(S["mix_l"], KT)
            units(pe, FIRST["rec_out"], U_REC_OUT, 2, unit(KT, xh, xl, CUTS352))

            def mlp(l):
                norm_sum(SHARED_N[("mlp", l)])
                first = FIRST[f"mlp{l}"]
                with pe.Fori(0, FF_CHUNKS) as c:
                    for q in range(FT):
                        unit(KT, xh, xl, CUTS352)(first + q, c * 12)
                    pe.wait_ge(S["hh_r"], (l * FF_CHUNKS + 1) * FT + c * FT)
                    pe.wait_ge(S["hl_r"], (l * FF_CHUNKS + 1) * FT + c * FT)
                    for q in range(KT):
                        unit(FT, hh, hl, CUTS352)(first + FT + q, c * 12)

            mlp_start(pe, "pe")
            mlp(0)
            rest_of_pe(pe, unit, norm_sum, mlp)

        @block.scalar
        def _(act):
            own = Chain(act, act_chain)
            act.dma_start(xtok[:, 0:4, :], A["x_prompt"][0, 0:512].rearrange("(t p) d -> p t d", p=P)).then_inc(S["tok_in"], 16)
            act.dma_start(xtok[:, 4:8, :], A["x_prompt"][0, 512:1024].rearrange("(t p) d -> p t d", p=P)).then_inc(S["tok_in"], 16)
            act.dma_start(xtok[0:SMP, QB, :], A["x_sample"].rearrange("b t d -> (b t) d")).then_inc(S["tok_in"], 16)
            for k in range(0, 2 * (QB + 1), 2):
                t = k // 2
                w = P if t < QB else SMP
                act.wait_ge(S["xt_mm"], k + 1)
                act.activation(x[:, 0:4, t * P:t * P + w], quad(2 + k % 6)[:, :, 0:w], ACT.Copy).then_inc(S["xt_act"], 1)
            end_phase(act, "act")

            def split_hi(n, gain):
                for k in range(KT):
                    act.activation(xh[:, k, :], x[:, k, :], ACT.Copy, scale=prm[:, gain + k:gain + k + 1])\
                        .then_inc(S["xh_ready"], 1)
                norm_squares(n)

            def norm_squares(n):
                for k in range(KT):
                    if k >= 2:
                        act.wait_ge(S["sq_added"], 8 * n + k - 1)
                    act.activation(sq[:, k % 2, :], x[:, k, :], ACT.Square).then_inc(S["sq_ready"], 1)
                act.wait_ge(S["ms_ready"], n + 1)
                act.activation(rstd[:, :], rstd[:, :], ACT.Sqrt).then_inc(S["rt_ready"], 1)

            split_hi(0, R_MIX0)
            act.dma_start(x_spill, x[:, :, :]).then_inc(S["x_spilled"], 16)
            act.wait_ge(S["x_spilled"], 16)

            def conv_unit(j, off):
                u = j + off
                act.wait_ge(set_free, u + 3)
                act.wait_ge(S["conv_done"], u + 1)
                heads = ub[:, 3 + SEQ:UB].rearrange("p (b t) -> p b t", b=DEC_BATCH)
                own.then(act.activation(heads[:, :, 0:3],
                                        hist[:, ds(u, 1), :].rearrange("p a (b t) -> p (a b) t", b=DEC_BATCH), ACT.Copy))
                own.did(act.activation(ctail[:, ds(u, 1), 0:3].rearrange("p a t -> p (a t)"), ub[:, SEQ:SEQ + 3], ACT.Copy))
                own.did(act.activation(ctail[:, ds(u, 1), 3:].rearrange("p a (b t) -> p (a b) t", b=DEC_BATCH),
                                       heads[:, :, DEC_SEQ:], ACT.Copy))
                act.activation(uc[:, 0:UB - 3], ub[:, 0:UB - 3], ACT.Copy, scale=prm[:, ds(R_CONV + u, 1)])\
                    .then_inc(S["uc0"], 1)
                act.wait_ge(S["conv_done"], u + 2)

            ucs = uc[:, 3 + SEQ:UB].rearrange("p (b t) -> p b t", b=DEC_BATCH)[:, :, 0:DEC_SEQ]

            def rg_unit(j, off):
                u = j + off
                conv_unit(j, off)
                bias = prm[:, ds(R_BCONV + u, 1)]
                own.did(act.activation(xr[:, ds(u, 1), 0:SEQ].rearrange("p a t -> p (a t)"), uc[:, 0:SEQ], ACT.Identity, bias=bias))
                own.did(act.activation(xr[:, ds(u, 1), SEQ:].rearrange("p a (b t) -> p (a b) t", b=DEC_BATCH), ucs,
                                       ACT.Identity, bias=bias))

            def qkv_unit(j, off):
                u = j + off
                conv_unit(j, off)
                own.did(act.activation(qkvz[:, ds(u - RT, 1), 0:SEQ].rearrange("p a t -> p (a t)"), uc[:, 0:SEQ], ACT.Silu))
                own.did(act.activation(qkvz[:, ds(u - RT, 1), SEQ:].rearrange("p a (b t) -> p (a b) t", b=DEC_BATCH), ucs,
                                       ACT.Silu))

            with own.loop(2, 10) as i:
                for j in range(2):
                    rg_unit(j, i * 2)
            with own.loop(6, 10) as i:
                for j in range(2):
                    qkv_unit(RT + j, i * 2)
            end_phase(act, "act")

            for k in range(4):
                act.wait_ge(S["tail_mm"], k + 1)
                act.activation(tail_rows[:, k * 512:(k + 1) * 512], ps[0:3 + DEC_BATCH * 3, 6 + k % 2, :], ACT.Copy)\
                    .then_inc(S["tail_sb"], 1)
            act.wait_ge(S["tail_sb"], 4)
            act.dma_start(O["conv_p"][0, 0], tail_rows[0:3, :]).then_inc(S["state_out"], 16)
            act.dma_start(O["conv_s"][0].rearrange("b i c -> (b i) c"), tail_rows[3:, :]).then_inc(S["state_out"], 16)

            for m in range(RT):
                for g, (dst, bias) in enumerate(((r_t, R_BA), (i_t, R_BX))):
                    act.wait_ge(S["ri_mm"], 2 * m + g + 1)
                    b = prm[:, bias + m:bias + m + 1]
                    own.did(act.activation(dst[:, m, 0:SEQ].rearrange("p (a t) -> p a t", a=2), ps[:, 3 * g:3 * g + 2, :],
                                           ACT.Sigmoid, bias=b))
                    act.activation(dst[:, m, SEQ:], ps[:, 3 * g + 2, 0:SMP], ACT.Sigmoid, bias=b).then_inc(S["ri_read"], 1)
            e, w, lw = tmp4[0], tmp4[1], tmp4[2]
            own.then(act.activation(e, prm[:, R_LAM:R_LAM + RT], ACT.Abs))
            own.then(act.activation(e, e, ACT.Exp, scale=-1.0))
            act.activation(w, e, ACT.Identity, bias=one_col).then_inc(S["rows_a"], 1)
            act.wait_ge(S["rows_a"], 1)
            act.activation(lw, w, ACT.Ln).then_inc(S["rows_a"], 1)
            own.then(act.activation(nea[32:32 + DN_H, :], nea[32:32 + DN_H, :], ACT.Exp))
            act.wait_ge(S["ri_read"], 2 * RT)
            act.wait_ge(S["rows_a"], 3)
            for m in range(RT):
                act.activation(a_t[:, m, :], r_t[:, m, :], ACT.Exp, scale=spl[:, m:m + 1]).then_inc(S["rg_exp"], 1)
                act.activation(r_t[:, m, :], r_t[:, m, :], ACT.Tanh, scale=spn[:, m:m + 1]).then_inc(S["rg_exp"], 1)
            hr = slice(32, 32 + DN_H)
            own.then(act.activation(rows_raw[hr, :], rows_b[hr, :], ACT.Abs))
            own.then(act.activation(rows_raw[hr, :], rows_raw[hr, :], ACT.Exp, scale=-1.0))
            act.activation(rows_raw[hr, :], rows_raw[hr, :], ACT.Ln, bias=one_col[hr, :]).then_inc(S["rows_exp"], 1)
            for m in range(RT):
                act.wait_ge(S["rg_m2"], m + 1)
                act.activation(r_t[:, m, :], r_t[:, m, :], ACT.Sqrt).then_inc(S["rg_sqrt"], 1)
            for m in range(RT):
                act.activation(gate[:, m, :], gate[:, m, :], ACT.Gelu_apprx_tanh).then_inc(S["rg_gelu"], 1)
            act.wait_ge(S["ht_mm"], 1)
            act.activation(hT_rows[:, :], ps[0:DEC_BATCH + 1, 6, :], ACT.Copy).then_inc(S["ht_sb"], 1)
            act.wait_ge(S["ht_sb"], 1)
            act.dma_start(O["h_p"][0], hT_rows[0:1, :]).then_inc(S["state_out"], 16)
            act.dma_start(O["h_s"][0], hT_rows[1:, :]).then_inc(S["state_out"], 16)
            end_phase(act, "act")
            act.dma_start(cst[:, :, :], A["dn_cst"]).then_inc(S["gate_w"], 16)
            end_phase(act, "act")

            def column_norm(n, tile, mean):
                act.wait_ge(S["cn_out"], max(0, n - 1))
                act.activation(r_t[:, n % 2, :], tile, ACT.Square).then_inc(S["cn_sq"], 1)

            def column_root(n, mean):
                act.wait_ge(S["cn_mm"], n + 1)
                act.activation(i_t[:, n % 2, :].rearrange("p (a t) -> p a t", a=3),
                               ps[:, 3 * (n % 2):3 * (n % 2) + 3, 0:352], ACT.Sqrt, bias=eps_col, scale=mean)\
                    .then_inc(S["cn_sqrt"], 1)

            own.did(act.activation(rows[0:DN_H, :], rows_raw[0:DN_H, :], ACT.Sigmoid))
            for n in range(9):
                if n < 8:
                    column_norm(n, qkvz[:, n, :], 1.0)
                if n:
                    column_root(n - 1, 1.0)
            act.wait_ge(S["rows_b"], 1)
            own.did(act.activation(rows[64:64 + DN_H, :], rows[64:64 + DN_H, :], ACT.Exp))
            act.wait_ge(S["gate_w"], 96)
            end_phase(act, "act")

            def act_chunk(c, t0, w, levels, smp):
                act.wait_ge(S["st_r"], c + 1)
                act.wait_ge(S["pe_bc"], c + 1)
                act.activation(dn["egb"][:, :, 0:w], quad(0)[:, :, 0:w], ACT.Exp).then_inc(S["egb_r"], 1)
                act.wait_ge(S["pe_col"], c + 1)
                act.activation(cols[0:w, :], ps[0:w, 2, 0:P], ACT.Copy).then_inc(S["cols_r"], 1)
                act.wait_ge(S["cols_r"], c + 1)
                act.wait_ge(S["pe_kt"], c + 1)
                for h in range(DN_H):
                    last = act.activation(dn["kd"][0:w, h, :], quad(6)[0:w, h, :], ACT.Copy, scale=cols[0:w, 64 + h:65 + h])
                last.then_inc(S["kd_r"], 1)
                act.wait_ge(S["dec_r"], c + 1)
                act.activation(dn["dec"][0:w, :, 0:w], dn["dec"][0:w, :, 0:w], ACT.Exp).then_inc(S["dec_e"], 1)
                act.wait_ge(S["pe_vt"], c + 1)
                for h in range(DN_H):
                    last = act.activation(dn["vb"][0:w, h, :], quad(7)[0:w, h, :], ACT.Copy, scale=cols[0:w, h:h + 1])
                last.then_inc(S["vb_r"], 1)
                act.wait_ge(S["pe_l"], c + 1)
                act.activation(dn["lm"][0:w, :, 0:w], quad(5)[0:w, :, 0:w], ACT.Copy).then_inc(S["lm_r"], 1)
                for l in range(levels):
                    act.wait_ge(S["pe_y"], c * LEVELS + l + 1)
                    act.activation(dn["yy"][0:w, :, 0:w], quad(3)[0:w, :, 0:w], ACT.Copy).then_inc(S["y_sb"], 1)
                if smp:
                    act.wait_ge(S["pe_ks"], QB + 1)
                    act.activation(ks_s[:, :, :, :].rearrange("p h a t -> p (h a t)"), ps[:, 0, 0:DN_H * 2 * SMP], ACT.Copy)\
                        .then_inc(S["y_sb"], 1)
                act.wait_ge(S["pe_vn"], c + 1)
                act.activation(dn["vn"][0:w, :, :], quad(1)[0:w, :, :], ACT.Copy).then_inc(S["vn_r"], 1)
                if not smp:
                    act.wait_ge(S["pe_o"], c + 1)
                    act.activation(qkvz[:, 0:4, ds(t0, w)], quad(2)[:, :, 0:w], ACT.Copy).then_inc(S["o_st"], 1)

            with act.Fori(0, QB) as c:
                act_chunk(c, c * P, P, LEVELS, False)
            act.wait_ge(S["st_r"], QB + 1)
            act.dma_start(O["S_p"][0, 0].rearrange("h k v -> k h v"), dn["st"][:, :, :]).then_inc(S["state_out"], 16)
            act.wait_ge(S["kc_cp"], QB + 1)
            act.dma_start(s0[:, :, :, :], A["state_S"][0].rearrange("b h k v -> k b h v")).then_inc(S["s0_in"], 16)
            act_chunk(QB, SEQ, SMP, 1, True)
            act.wait_ge(S["s0_out"], DEC_BATCH)
            act.dma_start(O["S_s"][0].rearrange("b h k v -> k b h v"), s0[:, :, :, :]).then_inc(S["state_out"], 16)
            for m in range(DN_H):
                act.activation(qkvz[:, 12 + m, :], qkvz[:, 12 + m, :], ACT.Silu).then_inc(S["silu_z"], 1)
            act.wait_ge(S["o_st"], QB + 2)
            for n in range(8, 13):
                if n < 12:
                    column_norm(n, qkvz[:, n - 8, :], 1.0 / DK)
                if n > 8:
                    column_root(n - 1, 1.0 / DK)
            act.dma_start(x[:, 0:4, :], x_spill[:, 0:4, :]).then_inc(S["x_back0"], 16)
            act.wait_ge(S["state_out"], 16 * 6)
            end_phase(act, "act")
            for m in range(RT):
                act.activation(xh[:, m, :], gate[:, m, :], ACT.Copy).then_inc(S["mix_h"], 1)
            for m in range(DN_H):
                act.activation(xh[:, RT + m, :], qkvz[:, 12 + m, :], ACT.Copy).then_inc(S["mix_h"], 1)
            act.wait_ge(S["mix_h"], KT)
            act.wait_ge(S["mix_l"], KT)
            act.dma_start(x[:, 4:8, :], x_spill[:, 4:8, :]).then_inc(S["x_back1"], 16)

            def mlp(l):
                split_hi(SHARED_N[("mlp", l)], R_MLP0 + 8 * l)
                base_h = l * FF_CHUNKS * FT
                with act.Fori(0, FF_CHUNKS) as c:
                    for q in range(FT):
                        n = c * FT + (base_h + q)
                        act.wait_ge(S["hu_r"], n + 1)
                        act.activation(hs[:, q % 2, :], hu[:, q % 2, :], ACT.Square).then_inc(S["hsq_r"], 1)
                        act.wait_ge(S["hsq_r"], n + 1)
                        act.activation(hh[:, q, :], hs[:, q % 2, :], ACT.Copy).then_inc(S["hh_r"], 1)

            mlp_start(act, "act")
            mlp(0)
            rest_of_act(act, own, split_hi, norm_squares, mlp)

        @block.vector
        def _(dve):
            own = Chain(dve, dve_chain)
            for name in ("uc0", "conv_done", "o_st", "st_r"):
                dve.sem_inc(S[name], 1)
            dve.wait_ge(mm_out, 1)
            dve.tensor_copy(prm[:, 0:R_ALL], ps[:, 0, 0:R_ALL]).then_inc(set_free, 1)
            dve.wait_ge(mm_out, 2)
            nh = CT * DEC_BATCH * 3
            own.did(dve.tensor_copy(flat(hist[:, :, :]), ps[:, 1, 0:nh]))
            dve.tensor_copy(flat(h0T), ps[:, 1, nh:nh + RT * DEC_BATCH]).then_inc(set_free, 1)
            for k in range(1, 2 * (QB + 1), 2):
                t = k // 2
                w = P if t < QB else SMP
                dve.wait_ge(S["xt_mm"], k + 1)
                dve.tensor_copy(x[:, 4:8, t * P:t * P + w], quad(2 + k % 6)[:, :, 0:w]).then_inc(S["xt_dve"], 1)
            end_phase(dve, "dve")

            def norm_mean(n):
                for k in range(KT):
                    dve.wait_ge(S["sq_ready"], 8 * n + k + 1)
                    if k == 0:
                        dve.tensor_copy(sumsq[:, :], sq[:, 0, :]).then_inc(S["sq_added"], 1)
                    else:
                        dve.wait_ge(S["sq_added"], 8 * n + k)
                        dve.tensor_tensor(sumsq[:, :], sumsq[:, :], sq[:, k % 2, :], ALU.add).then_inc(S["sq_added"], 1)
                dve.wait_ge(S["ss_mm"], n + 1)
                own.did(dve.tensor_scalar(rstd[:, 0:SEQ].rearrange("p (a t) -> p a t", a=2), ps[:, 6:8, :], 1.0 / D_MODEL, EPS,
                                          ALU.mult, ALU.add))
                dve.tensor_scalar(rstd[:, SEQ:], ps[:, 5, 0:SMP], 1.0 / D_MODEL, EPS, ALU.mult, ALU.add)\
                    .then_inc(S["ms_ready"], 1)
                dve.wait_ge(S["rt_ready"], n + 1)
                dve.reciprocal(rstd[:, :], rstd[:, :]).then_inc(S["rstd_ready"], 1)
                dve.wait_ge(S["rstd_ready"], n + 1)

            def split_lo(n, gain):
                for k in range(KT):
                    dve.wait_ge(S["xh_ready"], 8 * n + k + 1)
                    dve.scalar_tensor_tensor(xl[:, k, :], x[:, k, :], prm[:, gain + k:gain + k + 1],
                                             xh[:, k, :].bitcast(F32), ALU.mult, ALU.subtract).then_inc(S["xl_ready"], 1)
                norm_mean(n)

            own.did(dve.memset(ub[:, 0:3], 0.0))
            split_lo(0, R_MIX0)
            dve.wait_ge(S["x_spilled"], 16)
            rs_p = rstd[:, 0:SEQ].rearrange("p (a t) -> p a t", a=2)
            rs_s = rstd[:, SEQ:].rearrange("p (b t) -> p b t", b=DEC_BATCH)

            def conv_unit(j, off):
                u = j + off
                dve.wait_ge(mm_out, u + 3)
                dve.wait_ge(S["uc0"], u + 1)
                dve.wait_ge(S["conv_done"], u + 1)
                own.did(dve.tensor_tensor(ub[:, 3:3 + SEQ].rearrange("p (a t) -> p a t", a=2), set_view(j, 0, 2), rs_p, ALU.mult))
                heads = ub[:, 3 + SEQ:UB].rearrange("p (b t) -> p b t", b=DEC_BATCH)
                dve.tensor_tensor(heads[:, :, 3:], ps[:, 3 * (j % 2) + 2, 0:SMP].rearrange("p (b t) -> p b t", b=DEC_BATCH),
                                  rs_s, ALU.mult).then_inc(set_free, 1)
                dve.wait_ge(S["uc0"], u + 2)
                for i in range(1, CONV_W):
                    ins = dve.scalar_tensor_tensor(uc[:, 0:UB - 3], ub[:, i:i + UB - 3], prm[:, ds(R_CONV + i * CT + u, 1)],
                                                   uc[:, 0:UB - 3], ALU.mult, ALU.add)
                    if i < CONV_W - 1:
                        own.then(ins)
                    else:
                        ins.then_inc(S["conv_done"], 1)

            with own.loop(8, 6) as i:
                for j in range(2):
                    conv_unit(j, i * 2)

            def plain_unit(dst, first):
                def body(j, off):
                    u = j + off
                    dve.wait_ge(mm_out, u + 3)
                    own.did(dve.tensor_tensor(dst[:, ds(u - first, 1), 0:SEQ].rearrange("p o (a t) -> p (o a) t", a=2),
                                              set_view(j, 0, 2), rs_p, ALU.mult))
                    dve.tensor_tensor(dst[:, ds(u - first, 1), SEQ:].rearrange("p a t -> p (a t)"),
                                      ps[:, 3 * (j % 2) + 2, 0:SMP], rstd[:, SEQ:], ALU.mult).then_inc(set_free, 1)
                return body

            with own.loop(2, 2) as i:
                for j in range(2):
                    plain_unit(gate, 16)(16 + j, i * 2)
            with own.loop(2, 2) as i:
                for j in range(2):
                    plain_unit(qkvz, 8)(20 + j, i * 2)
            j = 24
            dve.wait_ge(mm_out, j + 3)
            own.did(dve.tensor_tensor(rows_raw[:, 0:SEQ].rearrange("p (a t) -> p a t", a=2), set_view(j, 0, 2)[0:64],
                                      rs_p[0:64], ALU.mult))
            dve.tensor_tensor(rows_raw[:, SEQ:], ps[0:64, 2, 0:SMP], rstd[0:64, SEQ:], ALU.mult).then_inc(set_free, 1)
            dve.wait_ge(set_free, 2 + U_REC_IN)
            hr = slice(32, 32 + DN_H)
            own.did(dve.tensor_scalar(rows_b[hr, :], rows_raw[hr, :], dtb[hr, :], None, ALU.add))
            end_phase(dve, "dve")

            lam = prm[:, R_LAM:R_LAM + RT]
            e, w, lw, d, z, o = tmp4
            dve.wait_ge(S["rows_a"], 2)
            own.then(dve.tensor_scalar(d, w, -1.0, 0.0, ALU.add, ALU.add))
            own.then(dve.tensor_scalar(z, d, 0.0, None, ALU.is_equal))
            own.then(dve.tensor_tensor(d, d, z, ALU.add))
            own.then(dve.reciprocal(d, d))
            own.then(dve.tensor_tensor(lw, lw, e, ALU.mult))
            own.then(dve.tensor_tensor(lw, lw, d, ALU.mult))
            own.then(dve.tensor_tensor(z, z, e, ALU.mult))
            own.then(dve.tensor_tensor(lw, lw, z, ALU.add))
            own.then(dve.tensor_scalar(o, lam, -1.0, 0.0, ALU.mult, ALU.max))
            own.then(dve.tensor_tensor(lw, lw, o, ALU.add))
            own.then(dve.tensor_scalar(spl, lw, -RG_C, None, ALU.mult))
            dve.tensor_scalar(spn, lw, RG_C, None, ALU.mult).then_inc(S["rows_a"], 1)

            for m in range(RT):
                dve.wait_ge(S["ri_read"], 2 * RT)
                own.then(dve.tensor_tensor(i_t[:, m, :], xr[:, m, :], i_t[:, m, :], ALU.mult))
                dve.wait_ge(S["rg_exp"], 2 * m + 2)
                own.then(dve.tensor_tensor(xr[:, m, :], a_t[:, m, :], a_t[:, m, :], ALU.mult))
                own.then(dve.scalar_tensor_tensor(r_t[:, m, :], xr[:, m, :], 1.0, r_t[:, m, :], ALU.add, ALU.mult))
                own.then(dve.tensor_scalar(r_t[:, m, :], r_t[:, m, :], 0.0, None, ALU.max))
                dve.memset(r_t[:, m, 0:1], 1.0).then_inc(S["rg_m2"], 1)
            first = slice(SEQ, TOK, DEC_SEQ)
            last_t = slice(SEQ + DEC_SEQ - 1, TOK, DEC_SEQ)
            for m in range(RT):
                dve.wait_ge(S["rg_sqrt"], m + 1)
                own.then(dve.tensor_tensor(i_t[:, m, :], i_t[:, m, :], r_t[:, m, :], ALU.mult))
                own.then(dve.tensor_tensor(h0T[:, m, :], a_t[:, m, first], h0T[:, m, :], ALU.mult))
                own.then(dve.tensor_tensor(i_t[:, m, first], i_t[:, m, first], h0T[:, m, :], ALU.add))
                own.then(dve.memset(a_t[:, m, first], 0.0))
                own.then(dve.tensor_tensor_scan(xr[:, m, :], a_t[:, m, :], i_t[:, m, :], 0.0, ALU.mult, ALU.add))
                own.did(dve.tensor_copy(hT[:, m, 0:1], xr[:, m, SEQ - 1:SEQ]))
                dve.tensor_copy(hT[:, m, 1:], xr[:, m, last_t]).then_inc(S["rg_done"], 1)
                dve.wait_ge(S["rg_gelu"], m + 1)
                own.did(dve.tensor_tensor(gate[:, m, :], xr[:, m, :], gate[:, m, :], ALU.mult))
            dve.wait_ge(S["rows_exp"], 1)
            own.then(dve.scalar_tensor_tensor(rows_b[hr, :], rows_b[hr, :], 0.0, rows_raw[hr, :], ALU.max, ALU.add))
            own.then(dve.tensor_scalar(rows_b[hr, :], rows_b[hr, :], nea[hr, :], -1.0, ALU.mult, ALU.mult))
            end_phase(dve, "dve")
            end_phase(dve, "dve")
            own.then(dve.tensor_tensor_scan(rows[hr, :], reset[hr, :], rows_b[hr, :], 0.0, ALU.mult, ALU.add))
            ks = slice(64, 64 + DN_H)
            for lo, n, q in ((0, QB, P), (SEQ, DEC_BATCH, DEC_SEQ)):
                g = rows[hr, lo:lo + n * q].rearrange("p (c t) -> p c t", t=q)
                e2 = rows[ks, lo:lo + n * q].rearrange("p (c t) -> p c t", t=q)
                ins = dve.tensor_tensor(e2, g[:, :, q - 1:q].to_broadcast([DN_H, n, q]), g, ALU.subtract)
                if lo == 0:
                    own.did(ins)
                else:
                    ins.then_inc(S["rows_b"], 1)

            def column_scale(n, dst, factor):
                dve.wait_ge(S["cn_sqrt"], n + 1)
                own.then(dve.reciprocal(i_t[:, n % 2, :], i_t[:, n % 2, :]))
                dve.scalar_tensor_tensor(dst, dst, factor, i_t[:, n % 2, :], ALU.mult, ALU.mult).then_inc(S["cn_out"], 1)

            for n in range(8):
                column_scale(n, qkvz[:, n, :], DK ** -0.5 if n < 4 else 1.0)
            end_phase(dve, "dve")

            def mask(k, w):
                return cst[0:w, k:k + 1, 0:w].to_broadcast([w, DN_H, w])

            def dve_chunk(c, t0, w, levels, smp):
                dve.wait_ge(S["pe_bc"], c + 1)
                dve.wait_ge(S["cols_r"], c + 1)
                for h in range(DN_H):
                    last = dve.tensor_scalar(dn["dec"][0:w, h, 0:w], quad(0)[0:w, h, 0:w], cols[0:w, 32 + h:33 + h], 0.0,
                                             ALU.subtract, ALU.min)
                last.then_inc(S["dec_r"], 1)
                dve.wait_ge(S["kc_cp"], c + 1)
                kbg = kq_s[:, :, 0, :] if smp else dn["kbg"][:, :, :]
                qg = kq_s[:, :, 1, :] if smp else dn["qg"][:, :, :]
                own.then(dve.tensor_tensor(kbg, dn["kc"][:, :, 0:w], quad(1)[:, :, 0:w], ALU.mult))
                dve.wait_ge(S["egb_r"], c + 1)
                dve.tensor_tensor(kbg, kbg, dn["egb"][:, :, 0:w], ALU.mult).then_inc(S["kbg_r"], 1)
                dve.tensor_tensor(qg, qkvz[:, 0:4, ds(t0, w)], dn["egb"][:, :, 0:w], ALU.mult).then_inc(S["qg_r"], 1)
                dve.wait_ge(S["dec_e"], c + 1)
                dec, decb = dn["dec"][0:w, :, 0:w], dn["decb"][0:w, :, 0:w]
                own.then(dve.tensor_tensor(dec, dec, mask(C_UPPER_S if smp else C_UPPER, w), ALU.mult))
                own.then(dve.tensor_tensor(decb, dec, quad(1)[0:w, :, 0:w], ALU.mult))
                own.then(dve.tensor_tensor(decb, decb, mask(C_STRICT_S if smp else C_STRICT, w), ALU.mult))
                dve.wait_ge(S["pe_kk"], c + 1)
                dve.tensor_tensor(dn["lt"][0:w, :, 0:w], quad(3)[0:w, :, 0:w], decb, ALU.mult).then_inc(S["lt_r"], 1)
                dve.tensor_tensor(dn["attn"][0:w, :, 0:w], quad(4)[0:w, :, 0:w], dec, ALU.mult).then_inc(S["attn_r"], 1)
                dve.wait_ge(S["lt_r"], c + 1)
                xi, xti = dn["xi"][0:w, :, 0:w], dn["xti"][0:w, :, 0:w]
                own.then(dve.tensor_tensor(xti, dn["lt"][0:w, :, 0:w], mask(C_NEG1T, w), ALU.mult))
                own.then(dve.tensor_tensor(xti, xti, mask(C_IDENT, w), ALU.add))
                dve.wait_ge(S["lm_r"], c + 1)
                own.then(dve.tensor_tensor(xi, dn["lm"][0:w, :, 0:w], mask(C_NEG1, w), ALU.mult))
                dve.tensor_tensor(xi, xi, mask(C_IDENT, w), ALU.add).then_inc(S["x0_r"], 1)
                dve.wait_ge(S["x0_r"], c + 1)
                for l in range(levels):
                    dve.wait_ge(S["pe_x"], c * LEVELS + l + 1)
                    own.did(dve.tensor_tensor(xi, xi, quad(4)[0:w, :, 0:w], ALU.subtract))
                    dve.tensor_tensor(xti, xti, quad(5)[0:w, :, 0:w], ALU.subtract).then_inc(S["x_sb"], 1)
                    dve.wait_ge(S["x_sb"], c * LEVELS + l + 1)
                dve.wait_ge(S["vb_r"], c + 1)
                if not smp:
                    dve.wait_ge(S["pe_ks"], c + 1)
                    dve.tensor_tensor(dn["rr"][:, :, :], dn["vb"][:, :, :], quad(0), ALU.subtract).then_inc(S["rr_r"], 1)
                    dve.wait_ge(S["pe_ds"], c + 1)
                    for h in range(DN_H):
                        last = dve.scalar_tensor_tensor(dn["st"][:, h, :], dn["st"][:, h, :], dn["egb"][:, h, w - 1:w],
                                                        quad(6)[:, h, :], ALU.mult, ALU.add)
                    last.then_inc(S["st_r"], 1)
                else:
                    dve.wait_ge(S["pe_ks"], c + 2)
                    dve.tensor_tensor(dn["rr"][0:w, :, :], dn["vb"][0:w, :, :], quad(1)[0:w], ALU.subtract)\
                        .then_inc(S["rr_r"], 1)
                    dve.wait_ge(S["kd_r"], c + 1)
                    dve.wait_ge(S["vc_cp"], c + 1)
                    for b in range(DEC_BATCH):
                        dve.tensor_scalar(kdm[0:w, b, :, :], dn["kd"][0:w, :, :], cst[0:w, C_COLS, b:b + 1], None, ALU.mult)\
                            .then_inc(S["kdm_r"], 1)
                    dve.wait_ge(S["pe_o"], c + 1)
                    dve.tensor_tensor(qkvz[:, 0:4, SEQ:TOK], quad(2)[:, :, 0:w], ks_s[:, :, 1, :], ALU.add)\
                        .then_inc(S["o_st"], 1)
                    for b in range(DEC_BATCH):
                        dve.wait_ge(S["pe_ds"], c + b + 1)
                        t = b * DEC_SEQ + DEC_SEQ - 1
                        for h in range(DN_H):
                            last = dve.scalar_tensor_tensor(s0[:, b, h, :], s0[:, b, h, :], dn["egb"][:, h, t:t + 1],
                                                            quad(4 + b % 4)[:, h, :], ALU.mult, ALU.add)
                        last.then_inc(S["s0_out"], 1)

            with own.loop(QB, 7 + LEVELS) as c:
                dve_chunk(c, c * P, P, LEVELS, False)
            dve_chunk(QB, SEQ, SMP, 1, True)
            for n in range(8, 12):
                dve.wait_ge(S["silu_z"], n - 7)
                column_scale(n, qkvz[:, n - 8, :], prm[:, R_DN:R_DN + 1])
                dve.wait_ge(S["cn_out"], n + 1)
                own.did(dve.tensor_tensor(qkvz[:, n + 4, :], qkvz[:, n - 8, :], qkvz[:, n + 4, :], ALU.mult))
            end_phase(dve, "dve")
            for m in range(KT):
                src = gate[:, m, :] if m < RT else qkvz[:, 8 + m, :]
                dve.wait_ge(S["mix_h"], m + 1)
                dve.tensor_tensor(xl[:, m, :], src, xh[:, m, :].bitcast(F32), ALU.subtract).then_inc(S["mix_l"], 1)

            def add_unit(first):
                def body(j, off):
                    dve.wait_ge(mm_out, j + off + 3)
                    xm = x[:, ds(j + off - first, 1), :].rearrange("p o (a t) -> p (o a) t", a=3)
                    dve.tensor_tensor(xm, xm, set_view(j, 0, 3)[:, :, 0:352], ALU.add).then_inc(set_free, 1)
                return body

            dve.wait_ge(S["x_back0"], 16)
            units(dve, FIRST["rec_out"], 4, 2, add_unit(FIRST["rec_out"]))
            dve.wait_ge(S["x_back1"], 16)
            units(dve, FIRST["rec_out"] + 4, 4, 2, add_unit(FIRST["rec_out"]))

            def mlp(l):
                split_lo(SHARED_N[("mlp", l)], R_MLP0 + 8 * l)
                first = FIRST[f"mlp{l}"]
                base_h = l * FF_CHUNKS * FT
                r3 = rstd[:, :].rearrange("p (a t) -> p a t", a=3)
                with dve.Fori(0, FF_CHUNKS) as c:
                    for q in range(FT + 1):
                        if q < FT:
                            n = c * FT + (base_h + q)
                            dve.wait_ge(mm_out, c * 12 + (first + q + 3))
                            if q >= 2:
                                dve.wait_ge(S["hsq_r"], n - 1)
                            dve.scalar_tensor_tensor(hu[:, q % 2, :].rearrange("p (a t) -> p a t", a=3),
                                                     set_view(first + q, 0, 3)[:, :, 0:352], 0.0, r3, ALU.max, ALU.mult)\
                                .then_inc(S["hu_r"], 1)
                            dve.wait_ge(S["hu_r"], n + 1)
                            own_sf(dve)
                        if q:
                            n = c * FT + (base_h + q - 1)
                            dve.wait_ge(S["hh_r"], n + 1)
                            dve.tensor_tensor(hl[:, q - 1, :], hs[:, (q - 1) % 2, :], hh[:, q - 1, :].bitcast(F32), ALU.subtract)\
                                .then_inc(S["hl_r"], 1)
                    for q in range(KT):
                        add_unit_at(first + FT + q, c * 12, q)

            def own_sf(dve):
                dve.sem_inc(set_free, 1)

            def add_unit_at(j, off, m):
                dve.wait_ge(mm_out, off + (j + 3))
                xm = x[:, m, :].rearrange("p (a t) -> p a t", a=3)
                dve.tensor_tensor(xm, xm, set_view(j, 0, 3)[:, :, 0:352], ALU.add).then_inc(set_free, 1)

            mlp_start(dve, "dve")
            mlp(0)
            rest_of_dve(dve, own, split_lo, norm_mean, add_unit, mlp)


_OUTS = [("y_prompt", (1, 1024, 1024)), ("y_sample", (8, 4, 1024)), ("conv_p", (1, 1, 3, 2048)), ("h_p", (1, 1, 512)),
         ("S_p", (1, 1, 4, 128, 128)), ("k_p", (1, 1, 1024, 2, 128)), ("v_p", (1, 1, 1024, 2, 128)),
         ("kidx_p", (1, 1, 1024, 64)), ("conv_s", (1, 8, 3, 2048)), ("h_s", (1, 8, 512)), ("S_s", (1, 8, 4, 128, 128)),
         ("k_s", (1, 8, 4, 2, 128)), ("v_s", (1, 8, 4, 2, 128)), ("kidx_s", (1, 8, 4, 64))]


def kernel(**inputs):
    import concourse.bacc as _bacc
    from concourse.bass_utils import run_bass_kernel_spmd as _run

    nc = _bacc.Bacc("TRN2", target_bir_lowering=False, num_devices=1)
    arrays = {name: np.ascontiguousarray(a) for name, a in inputs.items()}
    arrays["dn_cst"] = dn_constants()
    arrays["row_reset"] = row_reset()
    arrays["att_cst"] = att_constants()
    arrays["att_bits"] = att_bits()
    A, O = {}, {}
    for name, a in arrays.items():
        A[name] = nc.dram_tensor("in_" + name, a.shape, mybir.dt.from_np(a.dtype), kind="ExternalInput").ap()
    for name, shape in _OUTS:
        O[name] = nc.dram_tensor("out_" + name, shape, F32, kind="ExternalOutput").ap()
    build(nc, A, O)
    r = _run(nc, [{"in_" + name: a for name, a in arrays.items()}], core_ids=[0])
    return tuple(r.results[0]["out_" + name] for name, _ in _OUTS)
```

```python
from contextlib import ExitStack, contextmanager

import numpy as np

import concourse.bass as bass
from concourse import mybir

F32 = mybir.dt.float32
F32R = mybir.dt.float32r
BF16 = mybir.dt.bfloat16
I32 = mybir.dt.int32
ACT = mybir.ActivationFunctionType
ALU = mybir.AluOpType
AX = mybir.AxisListType.X

P = 128
D_MODEL = 1024
KT = D_MODEL // P
SEQ = 1024
DEC_BATCH = 8
DEC_SEQ = 4
SMP = DEC_BATCH * DEC_SEQ
TOK = SEQ + SMP
QB = SEQ // P
CONV_W = 4
CONV_CH = 2048
CT = CONV_CH // P
D_RNN = 512
RT = D_RNN // P
RG_C = 8.0
DN_H = 4
DK = 128
D_FF = 4096
FF_CHUNK = 512
FF_CHUNKS = D_FF // FF_CHUNK
FT = FF_CHUNK // P
EPS = 1e-6
PAGE = 128
PAST = 1024
PAGES = PAST // PAGE
TOPK = 256
Q_HEADS = 8
KV = 2
GRP = Q_HEADS // KV
IDX_H = 8
IDX_D = 64
SCALE = 128 ** -0.5
NEG = -3.0e38
MASKED = -1e30
UB = 3 + SEQ + DEC_BATCH * (3 + DEC_SEQ)
LEVELS = 6
CUTS512 = ((0, 512), (512, 512), (1024, 32))
CUTS352 = ((0, 352), (352, 352), (704, 352))

U_REC_IN, U_REC_OUT, U_MLP, U_ATT_IN, U_ATT_OUT = 25, 8, 96, 17, 8
FIRST = {}
_at = 0
for _name, _n in (("rec_in", U_REC_IN), ("rec_out", U_REC_OUT), ("mlp0", U_MLP), ("att_in", U_ATT_IN),
                  ("att_out", U_ATT_OUT), ("mlp1", U_MLP)):
    FIRST[_name] = _at
    _at += _n

R_MIX0, R_MIX1, R_MLP0, R_MLP1, R_FIN, R_CONV, R_BCONV, R_BA, R_BX, R_LAM, R_DN, R_ALL = (
    0, 8, 16, 24, 32, 40, 104, 108, 112, 116, 120, 121)
(C_IDENT, C_ONES, C_UPPER, C_STRICT, C_NEG1T, C_NEG1, C_LEVEL, C_SELB, C_SELG, C_UPPER_S, C_STRICT_S, C_COLS,
 C_STRIP, C_N) = (0, 1, 2, 3, 4, 5, 6, 12, 16, 20, 21, 22, 23, 24)


def dn_constants():
    c = np.zeros((C_N, P, P), np.float32)
    i = np.arange(P)
    row, col = i[:, None], i[None, :]
    c[C_IDENT] = row == col
    c[C_ONES] = 1.0
    c[C_UPPER] = row <= col
    c[C_STRICT] = row < col

    def level(b):
        return (row // (2 * b) == col // (2 * b)) & (row // b % 2 == 1) & (col // b % 2 == 0)

    c[C_NEG1] = -1.0 * level(1)
    c[C_NEG1T] = -1.0 * level(1).T
    for l in range(LEVELS):
        c[C_LEVEL + l] = level(2 << l)
    for h in range(DN_H):
        c[C_SELB + h, h, :] = 1.0
        c[C_SELG + h, 32 + h, :] = 1.0
    same = row // DEC_SEQ == col // DEC_SEQ
    c[C_UPPER_S] = same & (row <= col)
    c[C_STRICT_S] = same & (row < col)
    c[C_STRIP, :, 64] = 1.0
    c[C_COLS, :, 0:DEC_BATCH] = row // DEC_SEQ == np.arange(DEC_BATCH)[None, :]
    return np.ascontiguousarray(c.transpose(1, 0, 2))


A_BIAS, A_CAP, A_ESEL, A_SELH, A_TOK, A_CAPS, A_BITF, A_N = 0, 128, 256, 768, 800, 1056, 1088, 1119
BITS = 31


def att_constants():
    c = np.zeros((P, A_N), np.float32)
    row, col = np.arange(P)[:, None], np.arange(P)[None, :]
    c[:, A_BIAS:A_BIAS + P] = np.where(col <= row, 0.0, MASKED)
    c[:, A_CAP:A_CAP + P] = np.where(col <= row, -NEG, NEG)
    for b in range(DEC_BATCH):
        for t in range(DEC_SEQ):
            tok = b * DEC_SEQ + t
            for kv in range(KV):
                for g in range(GRP):
                    c[tok, A_ESEL + b // 2 * P + 32 * (b % 2 * KV + kv) + g * DEC_SEQ + t] = 1.0
            for h in range(IDX_H):
                c[h * DEC_SEQ + t, A_TOK + b * SMP + tok] = 1.0
                c[h, A_SELH + h * DEC_SEQ + t] = 1.0
            for u in range(SMP):
                ok = u // DEC_SEQ == b and u % DEC_SEQ <= t
                c[tok, A_CAPS + u] = -NEG if ok else NEG
    c[:, A_BITF:A_BITF + BITS] = 2.0 ** (BITS - 1 - np.arange(BITS))
    return c


def att_bits():
    bits = [1 << (BITS - 1 - k) for k in range(BITS)] + [0xFFFF, 0x10000, -0x10000]
    return np.ascontiguousarray(np.broadcast_to(np.array(bits, np.int32), (P, BITS + 3)))


def row_reset():
    r = np.ones((DN_H, TOK), np.float32)
    r[:, 0:SEQ:P] = 0.0
    r[:, SEQ::DEC_SEQ] = 0.0
    return r


class Chain:

    def __init__(self, eng, sem):
        self.eng, self.sem, self.n, self.off = eng, sem, 0, None

    def did(self, ins):
        ins.then_inc(self.sem, 1)
        self.n += 1

    def wait(self):
        self.eng.wait_ge(self.sem, self.n if self.off is None else self.off + self.n)

    def then(self, ins):
        self.did(ins)
        self.wait()

    @contextmanager
    def loop(self, count, per):
        n0 = self.n
        with self.eng.Fori(0, count) as i:
            self.off = i * per
            yield i
            if self.n - n0 != per:
                raise ValueError(f"{self.n - n0} steps an iteration, not {per}")
        self.n, self.off = n0 + per * count, None


def ds(i, n):
    return bass.ds(i, n)


def flat(ap):
    return ap.rearrange("p a b -> p (a b)")


def build(nc, A, O):
    ctx = ExitStack()
    with ctx:
        base = 16512

        def at(name, shape, dt, off):
            return nc.alloc_sbuf_tensor_at(name, shape, dt, offset=base + off)

        ROW = TOK * 4
        G0 = 0
        X0 = G0 + 2 * KT * ROW
        W0 = X0 + KT * ROW
        S0 = W0 + 6 * KT * P * 4
        M0 = S0 + ROW + 2048
        END = 229344 - base

        xh = at("xh", [P, KT, TOK], F32R, G0)
        xl = at("xl", [P, KT, TOK], F32R, G0 + KT * ROW)
        x = at("x", [P, KT, TOK], F32, X0)
        w_raw = at("w_raw", [P, 2, KT * P], F32, W0)
        w_hi = at("w_hi", [P, 2, KT * P], F32R, W0 + 2 * KT * P * 4)
        w_lo = at("w_lo", [P, 2, KT * P], F32R, W0 + 4 * KT * P * 4)
        rstd = at("rstd", [P, TOK], F32, S0)
        ident = at("ident", [P, P], F32, S0 + ROW)
        ones = at("ones", [P, P], F32, S0 + ROW + 512)
        prm = at("prm", [P, P], F32, S0 + ROW + 1024)
        small = at("small", [P, 128], F32, S0 + ROW + 1536)
        eps_col = small[:, 0:1]
        one_col = small[:, 1:2]
        nea = small[:, 2:3]
        dtb = small[:, 3:4]
        spl = small[:, 8:12]
        spn = small[:, 12:16]
        tmp4 = [small[:, 16 + 4 * k:20 + 4 * k] for k in range(6)]
        h0T = small[:, 40:72].rearrange("p (m b) -> p m b", b=DEC_BATCH)
        hT = small[:, 72:108].rearrange("p (m b) -> p m b", b=DEC_BATCH + 1)

        xtok = at("xtok", [P, QB + 1, D_MODEL], F32, M0)
        cst_rows = at("cst_rows", [R_ALL, P], F32, M0 + 9 * 4096)
        conv_rows = at("conv_rows", [DEC_BATCH * 3, CONV_CH], F32, M0 + 9 * 4096 + 512)
        h0_rows = at("h0_rows", [DEC_BATCH, D_RNN], F32, M0 + 9 * 4096 + 512 + 8192)
        sq = at("sq", [P, 2, TOK], F32, M0 + 12 * ROW)
        sumsq = at("sumsq", [P, TOK], F32, M0 + 14 * ROW)
        qkvz = at("qkvz", [P, 16, TOK], F32, M0)
        ub = at("ub", [P, UB], F32, M0 + 16 * ROW)
        uc = at("uc", [P, UB], F32, M0 + 16 * ROW + 4352)
        hist = at("hist", [P, CT, DEC_BATCH * 3], F32, M0 + 16 * ROW + 8704)
        ctail = at("ctail", [P, CT, 3 + DEC_BATCH * 3], F32, M0 + 16 * ROW + 8704 + 1536)
        xr = at("xr", [P, RT, TOK], F32, X0)
        gate = at("gate", [P, RT, TOK], F32, X0 + RT * ROW)
        r_t = at("r_t", [P, RT, TOK], F32, G0)
        i_t = at("i_t", [P, RT, TOK], F32, G0 + 4 * ROW)
        a_t = at("a_t", [P, RT, TOK], F32, G0 + 8 * ROW)
        sq8 = at("sq8", [P, 8, TOK], F32, G0)
        NR = 36
        norm_rows = at("norm_rows", [NR, TOK], F32, G0 + 9 * ROW)
        wax = at("wax", [P, 2, RT, P], F32, G0 + 12 * ROW)
        rows_raw = at("rows_raw", [64, TOK], F32, G0 + 12 * ROW + 4096)
        rows_b = at("rows_b", [64, TOK], F32, G0 + 13 * ROW + 4096)
        tail_rows = at("tail_rows", [3 + DEC_BATCH * 3, CONV_CH], F32, M0 + 16 * ROW)
        hT_rows = at("hT_rows", [DEC_BATCH + 1, D_RNN], F32, M0 + 16 * ROW + 8192)
        reset = at("reset", [64, TOK], F32, G0 + 14 * ROW + 4096)
        cst = at("cst", [P, C_N, P], F32, X0)
        rows = at("rows", [P, TOK], F32, X0 + C_N * 512)
        HB = DN_H * P * 4
        names = ["kc", "vc", "egb", "dec", "decb", "attn", "lt", "lm", "xi", "xti", "yy", "kd", "vb", "qg", "kbg",
                 "rr", "vn", "st"] + [f"lo{l}" for l in range(LEVELS)]
        dn = {n: at("dn_" + n, [P, DN_H, P], F32, G0 + HB * k) for k, n in enumerate(names)}
        cols = at("cols", [P, P], F32, G0 + HB * len(names))
        rowc = at("rowc", [P, P], F32, G0 + HB * len(names) + 512)
        smp_q = at("smp_q", [P, DN_H, SMP], F32, G0 + HB * len(names) + 1024)
        kq_s = at("kq_s", [P, DN_H, 2, SMP], F32, G0 + HB * len(names) + 1536)
        ks_s = at("ks_s", [P, DN_H, 2, SMP], F32, G0 + HB * len(names) + 2560)
        s0 = at("s0", [P, DEC_BATCH, DN_H, P], F32, M0 + 4 * ROW)
        kdm = at("kdm", [P, DEC_BATCH, DN_H, P], F32, M0 + 8 * ROW)
        assert G0 + HB * len(names) + 3584 <= X0 and X0 + C_N * 512 + ROW <= X0 + 4 * ROW
        hh = at("hh", [P, FT, TOK], F32R, M0)
        hl = at("hl", [P, FT, TOK], F32R, M0 + FT * ROW)
        hu = at("hu", [P, 2, TOK], F32, M0 + 2 * FT * ROW)
        hs = at("hs", [P, 2, TOK], F32, M0 + (2 * FT + 2) * ROW)
        assert M0 + 19 * ROW <= END and M0 + 16 * ROW + 8704 + 1536 + 1728 <= END, (END - M0, 19 * ROW)

        x_spill = nc.dram_tensor("x_spill", (P, KT, TOK), F32, kind="Internal").ap()

        ps = ctx.enter_context(nc.psum_tensor("ps", [P, 8, 512], F32))

        def quad(bank):
            return ps[:, bank, :].rearrange("p (h n) -> p h n", h=4)

        def sem(name):
            return ctx.enter_context(nc.semaphore(name))

        pe_chain, act_chain, dve_chain, pool_chain = (sem(n) for n in ("pe_chain", "act_chain", "dve_chain", "pool_chain"))
        w_loaded = [sem("w_loaded0"), sem("w_loaded1")]
        w_hi_done = sem("w_hi_done")
        w_split = sem("w_split")
        mm_out = sem("mm_out")
        set_free = sem("set_free")
        const_in = sem("const_in")
        phase = sem("phase")
        out_done = sem("out_done")
        n_out = [0]

        block = ctx.enter_context(nc.Block())

        def out_dma(eng, dst, src):
            n_out[0] += 1
            eng.dma_start(dst, src).then_inc(out_done, 16)

        S = {n: sem(n) for n in (
            "start_in tok_in xt_mm xt_act xt_dve xh_ready xl_ready sq_ready sq_added ss_mm ms_ready rt_ready rstd_ready "
            "x_spilled x_back0 x_back1 uc0 conv_done tail_mm tail_sb gate_w ri_mm ri_read rg_exp rg_m2 rg_sqrt rg_gelu ht_mm ht_sb "
            "cn_sq cn_mm cn_sqrt cn_out rg_done rows_a rows_exp rows_b wax_zero "
            "kc_cp vc_cp rowc_cp pe_col pe_bc pe_kk pe_kt pe_vt pe_l pe_y pe_x pe_ks pe_vn pe_o pe_ds "
            "cn_rec cn_bc pe_xi xi_sb egb_r cols_r dec_r dec_e kd_r vb_r lm_r y_sb vn_r o_st kbg_r qg_r attn_r lt_r x0_r x_sb rr_r st_r lo_r "
            "state_out s0_in kdm_r s0_out silu_z mix_h mix_l seam y_r y_mm y_act y_dve hu_r hsq_r hh_r hl_r").split()}
        SHARED_N = {("mlp", 0): 1, ("mlp", 1): 3}

        N_FIN = 4
        n_phase = {"pe": 0, "act": 0, "dve": 0, "pool": 0}

        def end_phase(eng, who):
            n_phase[who] += 1
            eng.drain().then_inc(phase, 1)
            eng.wait_ge(phase, 4 * n_phase[who])

        n_seam = {"pe": 0, "act": 0, "dve": 0}

        def mlp_start(eng, who):
            n_seam[who] += 1
            eng.drain().then_inc(S["seam"], 1)
            eng.wait_ge(S["seam"], 3 * n_seam[who])

        def set_view(j, c0, n):
            return ps[:, 3 * (j % 2) + c0:3 * (j % 2) + c0 + n, :]

        def units(eng, first, count, per, body):
            if count == per:
                for j in range(per):
                    body(first + j, 0)
                return
            with eng.Fori(0, count // per) as i:
                for j in range(per):
                    body(first + j, i * per)

        w_in_rec = A["w_in_rec"][0].rearrange("(k p) n -> p k n", p=P)
        w_out_rec = A["w_out_rec"][0].rearrange("(k p) n -> p k n", p=P)

        def mlp_loads(sp, l, load):
            first = FIRST[f"mlp{l}"]
            up = A["w_up"][l].rearrange("(k p) n -> p k n", p=P)
            down = A["w_down"][l].rearrange("(c k p) n -> c p k n", p=P, k=FT)
            with sp.Fori(0, FF_CHUNKS) as c:
                for q in range(FT):
                    load(lambda j, off: up[:, :, ds(c * FF_CHUNK + q * P, P)], KT)(first + q, c * 12)
                for q in range(KT):
                    load(lambda j, off: down[ds(c, 1), :, :, q * P:(q + 1) * P].rearrange("c p k n -> (c p) k n"),
                         FT)(first + FT + q, c * 12)

        def y_pe(pe, norm_sum):
            norm_sum(N_FIN, 0)
            for k in range(2 * (QB + 1)):
                t, half = k // 2, k % 2
                w = P if t < QB else SMP
                if t == 0:
                    pe.wait_ge(S["y_r"], 4 * (half + 1))
                if k >= 4:
                    pe.wait_ge(S["y_act"] if k % 2 == 0 else S["y_dve"], (k - 4) // 2 + 1)
                for q in range(4):
                    mm = pe.transpose(ps[0:w, k % 4, q * P:(q + 1) * P], x[:, half * 4 + q, t * P:t * P + w], ident[:, :])
                mm.then_inc(S["y_mm"], 1)

        def y_act(act, norm_root):
            norm_root(N_FIN)
            for k in range(0, 2 * (QB + 1), 2):
                t = k // 2
                w = P if t < QB else SMP
                act.wait_ge(S["y_mm"], k + 1)
                act.activation(xtok[0:w, t, 0:512], ps[0:w, k % 4, :], ACT.Copy).then_inc(S["y_act"], 1)

        def y_dve(dve, norm_mean):
            norm_mean(N_FIN, 0)
            for k in range(KT):
                dve.scalar_tensor_tensor(x[:, k, :], x[:, k, :], prm[:, R_FIN + k:R_FIN + k + 1], rstd[:, :],
                                         ALU.mult, ALU.mult).then_inc(S["y_r"], 1)
            for k in range(1, 2 * (QB + 1), 2):
                t = k // 2
                w = P if t < QB else SMP
                dve.wait_ge(S["y_mm"], k + 1)
                dve.tensor_copy(xtok[0:w, t, 512:1024], ps[0:w, k % 4, :]).then_inc(S["y_dve"], 1)

        def y_store(sp):
            for t in range(QB + 1):
                sp.wait_ge(S["y_act"], t + 1)
                sp.wait_ge(S["y_dve"], t + 1)
                if t < QB:
                    out_dma(sp, O["y_prompt"][0, t * P:(t + 1) * P], xtok[:, t, :])
                else:
                    out_dma(sp, O["y_sample"].rearrange("b t d -> (b t) d"), xtok[0:SMP, t, :])
            sp.wait_ge(out_done, 16 * n_out[0])
            sp.wait_ge(S["state_out"], 16 * 6)
        oq = at("oq", [P, 16, TOK], F32, M0)
        ki = at("ki", [P, TOK], F32, M0 + 16 * ROW)
        wi = at("wi", [IDX_H, TOK], F32, M0 + 17 * ROW)
        SC_W = sum(P * (i + 1) for i in range(2, QB))
        sc_off = [sum(P * (k + 1) for k in range(2, i)) for i in range(QB)]
        o = [0]

        def scratch(name, shape, dt, size=4):
            n = size
            for d in shape[1:]:
                n *= d
            t = at(name, shape, dt, o[0])
            o[0] += -(-n // 32) * 32
            return t

        sc = scratch("sc", [P, SC_W], F32)
        sc_s = scratch("sc_s", [SMP, TOK], F32)
        vtok = scratch("vtok", [P, QB + 1, KV * P], F32)
        mb_at = o[0]
        mb = scratch("mb", [P, SC_W], BF16, 2)
        mb_s = scratch("mb_s", [SMP, TOK], BF16, 2)
        ktok = at("ktok", [P, QB + 1, KV * P], F32, mb_at)
        pr_at = o[0]
        pr0 = scratch("pr0", [P, GRP, SEQ], F32)
        relu = at("relu", [P, 2, SEQ], F32, pr_at)
        relu_s = at("relu_s", [SMP, 2, SEQ], F32, pr_at + 8192)
        new_relu = at("new_relu", [SMP, DEC_BATCH, SMP], F32, pr_at)
        ptt = scratch("ptt", [P, 2, GRP * P], F32)
        scr_at = o[0]
        scr = [scratch(f"scr{k}", [P, TOK], F32) for k in range(2)]
        pt_s = at("pt_s", [P, PAGES + 1, P], F32, scr_at)
        qs = at("qs", [P, DEC_BATCH, Q_HEADS, DEC_SEQ], F32, scr_at + 4 * (PAGES + 1) * P)
        kpg_at = o[0]
        kpg0 = scratch("kpg0", [P, PAGES, KV * P], F32)
        kpg = [kpg0] + [at(f"kpg{k}", [P, PAGES, KV * P], F32, M0 + (8 + 2 * k) * ROW) for k in range(1, 4)]
        kix = [at(f"kix{k}", [P, PAGES, IDX_D], F32, kpg_at + 2048 * k) for k in range(2)]
        kts_at = o[0]
        kts = scratch("kts", [P, KV, PAST], F32)
        kit = [at(f"kit{k}", [IDX_D, PAST], F32, kts_at + 4096 * k) for k in range(2)]
        pr = [pr0, at("pr1", [P, GRP, SEQ], F32, kts_at)]
        vpg_at = o[0]
        vpg0 = scratch("vpg0", [P, PAGES, KV * P], F32)
        vpg = [at(f"vpg{k}", [P, PAGES, KV * P], F32, off) for k, off in ((1, 0), (2, 8192), (3, mb_at))] + [vpg0]
        qis = at("qis", [IDX_D, DEC_BATCH, IDX_H, DEC_SEQ], F32, vpg_at)
        w_tok = at("w_tok", [SMP, DEC_BATCH, SMP], F32, vpg_at + 1024)
        kitok = at("kitok", [P, QB + 1, IDX_D], F32, vpg_at + 4096)
        w_rows = at("w_rows", [SMP, SMP], F32, vpg_at + 2048)
        pr_new = at("pr_new", [P, 2, SMP], F32, pr_at + 8192)
        den_new = at("den_new", [P, 4], F32, pr_at + 8192 + 256)
        acst = scratch("acst", [P, A_N], F32)
        id_b = scratch("id_b", [P, P], BF16, 2)
        bias_b = scratch("bias_b", [P, P], BF16, 2)
        esel_b = scratch("esel_b", [SMP, DEC_BATCH // 2, P], BF16, 2)
        wic = scratch("wic", [P, QB + 1, IDX_H], F32)
        NB = QB - 1
        cnt, neg, quota, acc = (scratch(n, [P, NB], F32) for n in ("cnt", "neg", "quota", "acc"))
        cand, trial, hi16, carry = (scratch(n, [P, NB], I32) for n in ("cand", "trial", "hi16", "carry"))
        signs, half_w = (at(n, [P, 3], F32, M0 + 18 * ROW + 512 + 32 * k) for k, n in enumerate(("signs", "half_w")))
        junk = at("junk", [P, SC_W + TOK], F32, pr_at)
        junk_off = sc_off[2:] + [SC_W]
        DVE_Q, ACT_Q = range(4), range(4, 7)
        mx = scratch("mx", [P, 4], F32)
        den = scratch("den", [P, 8], F32)
        rden = scratch("rden", [P, 8], F32)
        bits = at("bits", [P, BITS + 3], I32, M0 + 18 * ROW + 256)
        pages = at("pages", [1, DEC_BATCH * PAGES], I32, M0 + 18 * ROW)
        assert o[0] <= X0 + KT * ROW, (o[0], X0 + KT * ROW)

        S.update({n: sem(n) for n in (
            "sample_loads trial_r signs_r mask_r acst_in pages_in kx_in0 kx_in1 kp_in0 kp_in1 kp_in2 kp_in3 vp_in0 vp_in1 vp_in2 vp_in3 vp_used kv_out tk_mm tk_act tk_dve "
            "w_tok_r new_mm new_relu_r new_acc new_out si_tr si_kt si_mm si_relu si_acc is_mm is_relu is_acc sc_done "
            "at_mm at_max at_exp at_nrm at_tr at_ptt at_ptt0 at_pv at_o sa_tr sa_kts sa_mm sa_ptr sa_pt sa_pv").split()})
        w_in_att = A["w_in_att"][0].rearrange("(k p) n -> p k n", p=P)
        w_out_att = A["w_out_att"][0].rearrange("(k p) n -> p k n", p=P)
        GROUPS = QB * KV
        HEADS = GROUPS * GRP
        steps_before = [sum(k // KV + 1 for k in range(n)) for n in range(GROUPS + 1)]

        def cuts(w):
            return [(c, min(512, w - c)) for c in range(0, w, 512)]

        def bank2(b, w):
            return ps[:, b:b + 2, :].rearrange("p a n -> p (a n)")[:, 0:w]

        def rest_of_sync(sp, load):
            first = FIRST["att_in"]
            units(sp, first, 16, 2, load(lambda j, off: w_in_att[:, :, ds((j + off - first) * P, P)], KT))
            j = first + 16
            n_last = IDX_D + IDX_H
            sp.wait_ge(w_split, j + 1)
            last = w_raw[:, j % 2, :].rearrange("p (k n) -> p k n", k=KT)
            with nc.allow_non_contiguous_dma(reason="72 columns"):
                sp.dma_start(last[:, :, 0:n_last], w_in_att[:, :, 16 * P:16 * P + n_last]).then_inc(w_loaded[j % 2], 16)
            sp.wait_ge(S["x_spilled"], 32)
            sp.dma_start(acst[:, :], A["att_cst"]).then_inc(S["acst_in"], 16)
            sp.dma_start(bits[:, :], A["att_bits"]).then_inc(S["acst_in"], 16)
            sp.dma_start(pages[:, :], A["page_table"].rearrange("b p -> (b p)").unsqueeze(0)).then_inc(S["pages_in"], 16)
            sp.wait_ge(S["pages_in"], 16)
            n_pool = A["cache_k"].shape[1]

            def page_loads(dst, cache, b, done):
                sp.sem_inc(S["sample_loads"], 1)
                for p in range(PAGES):
                    r = sp.value_load(pages[0:1, ds(b * PAGES + p, 1)], min_val=0, max_val=n_pool - 1)
                    sp.dma_start(dst[:, p, :], cache[ds(r, 1)].rearrange("a t d -> (a t) d")).then_inc(done, 16)

            kidx_pages = A["cache_kidx"][0]
            k_pages = A["cache_k"][0].rearrange("n t k d -> n t (k d)")
            v_pages = A["cache_v"][0].rearrange("n t k d -> n t (k d)")
            sp.wait_ge(mm_out, 2 + j + 1)
            with sp.Fori(0, DEC_BATCH // 2) as i:
                for s in range(2):
                    sp.wait_ge(S["si_tr"], i * 4 + 2 * (s + 1))
                    page_loads(kix[s], kidx_pages, i * 2 + s, S[f"kx_in{s}"])
            first = FIRST["att_out"]
            sp.wait_ge(S["si_tr"], 4 + 2 * DEC_BATCH)
            sp.wait_ge(S["si_acc"], DEC_BATCH)
            sp.wait_ge(S["kv_out"], 16 * 6)
            page_loads(kpg[0], k_pages, 0, S["kp_in0"])
            units(sp, first, 2, 2, load(lambda j, off: w_out_att[:, :, ds((j + off - first) * P, P)], KT))
            sp.wait_ge(S["trial_r"], 1)
            for b in range(1, 4):
                page_loads(kpg[b], k_pages, b, S[f"kp_in{b}"])
            sp.wait_ge(S["mask_r"], NB)
            for b in range(2):
                page_loads(vpg[b], v_pages, b, S[f"vp_in{b}"])
            sp.wait_ge(S["at_pv"], steps_before[GROUPS])
            for b in range(2, 4):
                page_loads(vpg[b], v_pages, b, S[f"vp_in{b}"])
            for pair in (4, 6):
                for b in (pair, pair + 1):
                    sp.wait_ge(S["sa_tr"], 4 * (b - 4) + 4)
                    page_loads(kpg[b - 4], k_pages, b, S[f"kp_in{b - 4}"])
                for b in (pair, pair + 1):
                    sp.wait_ge(S["vp_used"], b - 3)
                    page_loads(vpg[b - 4], v_pages, b, S[f"vp_in{b - 4}"])
            units(sp, first + 2, U_ATT_OUT - 2, 2,
                  load(lambda j, off: w_out_att[:, :, ds((j + off - first) * P, P)], KT))
            mlp_loads(sp, 1, load)
            y_store(sp)

        def rest_of_pool(pool, split_units, mlp_split):
            split_units(FIRST["att_in"], 16, 2, KT)
            split_units(FIRST["att_in"] + 16, 1, 1, KT)
            split_units(FIRST["att_out"], U_ATT_OUT, 2, KT)
            mlp_split(1)

        def rest_of_pe(pe, unit, first_unit, norm_sum, mlp):
            first_unit(2, FIRST["att_in"])
            units(pe, FIRST["att_in"] + 1, 16, 2, unit(KT, xh, xl, CUTS352))
            pe.sem_inc(S["si_tr"], 4)
            mlp_start(pe, "pe")

            for t in range(QB + 1):
                c0, w = t * P, P if t < QB else SMP
                if t >= 4:
                    pe.wait_ge(S["tk_act"], t - 3)
                    pe.wait_ge(S["tk_dve"], t - 3)
                bank = 2 * (t % 4)
                for m in range(2 * KV):
                    pe.transpose(ps[0:w, bank + m // KV, m % KV * P:(m % KV + 1) * P], oq[:, 8 + m, c0:c0 + w], ident[:, :])
                pe.transpose(ps[0:w, bank + 1, KV * P:KV * P + IDX_D], ki[0:IDX_D, c0:c0 + w], ident[0:IDX_D, 0:IDX_D])
                pe.transpose(ps[0:w, bank, KV * P:KV * P + IDX_H], wi[:, c0:c0 + w], ident[0:IDX_H, 0:IDX_H])\
                    .then_inc(S["tk_mm"], 1)
            pe.wait_ge(S["acst_in"], 32)
            pe.wait_ge(S["tk_act"], QB + 1)
            pe.wait_ge(S["tk_dve"], QB + 1)
            pe.matmul(ps[0:SMP, 2, 0:SMP], acst[0:IDX_H, A_SELH:A_SELH + SMP], wi[:, SEQ:TOK], start=True, stop=True)\
                .then_inc(S["tk_mm"], 1)
            pe.wait_ge(S["w_tok_r"], 1)
            for b in range(DEC_BATCH):
                mm = pe.matmul(ps[0:SMP, 6, b * SMP:(b + 1) * SMP], qis[:, b, :, :].rearrange("p h t -> p (h t)"),
                               ki[0:IDX_D, SEQ:TOK], start=True, stop=True)
            mm.then_inc(S["new_mm"], 1)
            pe.wait_ge(S["new_relu_r"], 1)
            for b in range(DEC_BATCH):
                mm = pe.matmul(ps[0:SMP, 7, 0:SMP], w_tok[:, b, :], new_relu[:, b, :], start=b == 0, stop=b == DEC_BATCH - 1)
            mm.then_inc(S["new_acc"], 1)
            pe.wait_ge(S["new_out"], 1)

            def head_sum(b):
                pe.wait_ge(S["si_relu"], b + 1)
                for half in range(2):
                    mm = pe.matmul(ps[0:SMP, 4 + half, :], w_tok[:, b, :], relu_s[:, b % 2, half * 512:(half + 1) * 512],
                                   start=b == 0, stop=b == DEC_BATCH - 1)
                mm.then_inc(S["si_acc"], 1)

            for b in range(DEC_BATCH):
                pe.wait_ge(S[f"kx_in{b % 2}"], 16 * PAGES * (b // 2 + 1))
                for half in range(2):
                    if b:
                        pe.wait_ge(S["si_kt"], 2 * b - 1 + half)
                    for q in range(4):
                        mm = pe.transpose(ps[0:IDX_D, 6 + half, q * P:(q + 1) * P], kix[b % 2][:, 4 * half + q, :], ident[:, :])
                    mm.then_inc(S["si_tr"], 1)
                pe.wait_ge(S["si_kt"], 2 * b + 2)
                for half in range(2):
                    mm = pe.matmul(ps[0:SMP, 2 * (b % 2) + half, :], qis[:, b, :, :].rearrange("p h t -> p (h t)"),
                                   kit[b % 2][:, half * 512:(half + 1) * 512], start=True, stop=True)
                mm.then_inc(S["si_mm"], 1)
                if b:
                    head_sum(b - 1)
            head_sum(DEC_BATCH - 1)
            pe.wait_ge(S["sc_done"], 1)
            for n in range((QB - 2) * IDX_H):
                i, h = 2 + n // IDX_H, n % IDX_H
                if n >= 4:
                    pe.wait_ge(S["is_relu"], n - 3)
                half = slice(IDX_D * (h % 2), IDX_D * (h % 2) + IDX_D)
                for k, (c0, cn) in enumerate(cuts(P * (i + 1))):
                    mm = pe.matmul(ps[:, 2 * (n % 4) + k, 0:cn], oq[half, 12 + h // 2, i * P:(i + 1) * P],
                                   ki[half, c0:c0 + cn], start=True, stop=True)
                mm.then_inc(S["is_mm"], 1)
            mlp_start(pe, "pe")

            def scores(n):
                i, kv = n // KV, n % KV
                if i >= 2:
                    pe.wait_ge(S["mask_r"], i - 1)
                for g in range(GRP):
                    a = n * GRP + g
                    if a >= 2:
                        pe.wait_ge(S["at_exp"], a - 1)
                    for k, (c0, cn) in enumerate(cuts(P * (i + 1))):
                        bank = 2 * (a % 2) + k
                        pe.matmul(ps[:, bank, 0:cn], oq[:, GRP * kv + g, i * P:(i + 1) * P], oq[:, 8 + kv, c0:c0 + cn],
                                  start=True, stop=False, skip_group_check=True)
                        if i < 2:
                            mm = pe.matmul(ps[:, bank, i * P:(i + 1) * P], id_b[:, :], bias_b[:, :], start=False, stop=True,
                                           skip_group_check=True)
                        else:
                            mm = pe.matmul(ps[:, bank, 0:cn], id_b[:, :], mb[:, sc_off[i] + c0:sc_off[i] + c0 + cn],
                                           start=False, stop=True, skip_group_check=True)
                    mm.then_inc(S["at_mm"], 1)

            def copied(c):
                n = sum(c >= s for s in steps_before) - 1
                if c == steps_before[n]:
                    pe.wait_ge(S["at_ptt0"], n + 1)
                else:
                    pe.wait_ge(S["at_ptt"], c - n)

            def values(n):
                i, kv = n // KV, n % KV
                pe.wait_ge(S["at_nrm"], GRP * (n + 1))
                for k in range(i + 2):
                    c = steps_before[n] + k
                    if k <= i:
                        if c >= 2:
                            copied(c - 2)
                        for g in range(GRP):
                            mm = pe.transpose(quad(4 + c % 2)[:, g, :], pr[n % 2][:, g, k * P:(k + 1) * P], ident[:, :])
                        mm.then_inc(S["at_tr"], 1)
                    if k:
                        if k == 1 and n >= 2:
                            pe.wait_ge(S["at_o"], n - 1)
                        copied(c - 1)
                        pe.matmul(ps[:, 6 + n % 2, :], vtok[:, k - 1, kv * P:(kv + 1) * P], ptt[:, (c - 1) % 2, :],
                                  start=k == 1, stop=k == i + 1).then_inc(S["at_pv"], 1)

            scores(0)
            for n in range(GROUPS):
                if n + 1 < GROUPS:
                    scores(n + 1)
                values(n)
            pe.wait_ge(S["at_o"], GROUPS)
            pe.wait_ge(S["at_exp"], HEADS)

            pe.wait_ge(S["mask_r"], NB + 1)
            def sample_values(G):
                s0 = 3 * (G % 2)
                pe.wait_ge(S["at_nrm"], HEADS + G + 1)
                for k in range(3):
                    tr = 3 * G + k
                    pe.wait_ge(S["sa_kts"], min(8 * (G + 2), 32))
                    if k == 2:
                        pe.wait_ge(S["sa_pt"], tr - 1)
                    if k < 2:
                        for q in range(4):
                            p = 4 * k + q
                            mm = pe.transpose(ps[:, 6 + k, q * P:(q + 1) * P], pr0[:, G % 2, p * P:(p + 1) * P], ident[:, :])
                    else:
                        mm = pe.transpose(ps[0:SMP, 6, 0:P], pr_new[:, G % 2, :], ident[:, :])
                    mm.then_inc(S["sa_ptr"], 1)
                pe.wait_ge(S["sa_pt"], 3 * G + 3)
                for b2 in range(2):
                    b = 2 * G + b2
                    pe.wait_ge(S[f"vp_in{b % 4}"], 16 * PAGES * (b // 4 + 1))
                    for kv in range(KV):
                        q4 = 2 * b2 + kv
                        out = ps[:, s0 + 2, 384 + 16 * q4:384 + 16 * (q4 + 1)]
                        for p in range(PAGES):
                            pe.matmul(out, vpg[b % 4][:, p, kv * P:(kv + 1) * P], pt_s[:, p, 32 * q4:32 * q4 + 16],
                                      start=p == 0, stop=False)
                        mm = pe.matmul(out, vtok[0:SMP, QB, kv * P:(kv + 1) * P], pt_s[0:SMP, PAGES, 32 * q4:32 * q4 + 16],
                                       start=False, stop=True)
                    mm.then_inc(S["vp_used"], 1)

            for G in range(DEC_BATCH // 2):
                s0 = 3 * (G % 2)
                if G >= 2:
                    pe.wait_ge(S["at_exp"], HEADS + G - 1)
                    pe.wait_ge(S["at_o"], GROUPS + G - 1)
                for t, (c0, cn) in enumerate(CUTS352):
                    pe.matmul(ps[:, s0 + t, 0:cn], esel_b[:, G, :], mb_s[:, c0:c0 + cn], start=True, stop=False,
                              skip_group_check=True)
                for b2 in range(2):
                    b = 2 * G + b2
                    pe.wait_ge(S[f"kp_in{b % 4}"], 16 * PAGES * (b // 4 + 1))
                    for s in range(4):
                        n = 4 * b + s
                        if n >= 2:
                            pe.wait_ge(S["sa_kts"], n - 1)
                        if s < 2 and b2 == 0 and G >= 2:
                            pe.wait_ge(S["sa_pt"], 3 * (G - 1))
                        for q in range(4):
                            mm = pe.transpose(ps[:, 6 + s % 2, q * P:(q + 1) * P],
                                              kpg[b % 4][:, 4 * (s % 2) + q, s // 2 * P:(s // 2 + 1) * P], ident[:, :])
                        mm.then_inc(S["sa_tr"], 1)
                    pe.wait_ge(S["sa_kts"], 4 * b + 4)
                    for kv in range(KV):
                        q4 = 2 * b2 + kv
                        rows_q = slice(32 * q4, 32 * q4 + 16)
                        q_rows = qs[:, b, GRP * kv:GRP * (kv + 1), :].rearrange("p h t -> p (h t)")
                        for t, (c0, cn) in enumerate(((0, 352), (352, 352), (704, 320))):
                            pe.matmul(ps[rows_q, t + s0, 0:cn], q_rows, kts[:, kv, c0:c0 + cn], start=False, stop=True,
                                      skip_group_check=True)
                        mm = pe.matmul(ps[rows_q, 2 + s0, 320:352], q_rows, oq[:, 8 + kv, SEQ:TOK], start=False, stop=True,
                                       skip_group_check=True)
                    mm.then_inc(S["sa_mm"], 1)
                if G:
                    sample_values(G - 1)
            sample_values(DEC_BATCH // 2 - 1)
            mlp_start(pe, "pe")
            pe.wait_ge(S["mix_h"], 2 * KT)
            pe.wait_ge(S["mix_l"], 2 * KT)
            units(pe, FIRST["att_out"], U_ATT_OUT, 2, unit(KT, xh, xl, CUTS352))
            mlp(1)
            mlp_start(pe, "pe")
            y_pe(pe, norm_sum)

        def rest_of_act(act, own, norm_root, square_unit, mlp):
            act.dma_start(x_spill, x[:, :, :]).then_inc(S["x_spilled"], 16)
            norm_root(2)
            act.wait_ge(S["x_spilled"], 32)
            mlp_start(act, "act")
            act.wait_ge(S["acst_in"], 32)
            own.did(act.activation(id_b[:, :], ident[:, :], ACT.Copy))
            own.did(act.activation(bias_b[:, :], acst[:, A_BIAS:A_BIAS + P], ACT.Copy))
            own.did(act.activation(flat(esel_b[:, :, :]), acst[0:SMP, A_ESEL:A_ESEL + 4 * P], ACT.Copy))
            for t in range(QB + 1):
                w, bank = P if t < QB else SMP, 2 * (t % 4)
                act.wait_ge(S["tk_mm"], t + 1)
                own.did(act.activation(kitok[0:w, t, :], ps[0:w, bank + 1, KV * P:KV * P + IDX_D], ACT.Copy))
                act.activation(vtok[0:w, t, :], ps[0:w, bank + 1, 0:KV * P], ACT.Copy).then_inc(S["tk_act"], 1)
            own.wait()
            act.wait_ge(S["tk_act"], QB + 1)
            act.wait_ge(S["tk_dve"], QB + 1)
            for name, tile in (("k", ktok), ("v", vtok), ("kidx", kitok)):
                tokens = "b (n p) k d -> p (b n) (k d)" if name != "kidx" else "b (n p) d -> p (b n) d"
                samples = "b t k d -> (b t) (k d)" if name != "kidx" else "b t d -> (b t) d"
                act.dma_start(O[name + "_p"][0].rearrange(tokens, p=P), tile[:, 0:QB, :]).then_inc(S["kv_out"], 16)
                act.dma_start(O[name + "_s"][0].rearrange(samples), tile[0:SMP, QB, :]).then_inc(S["kv_out"], 16)
            act.wait_ge(S["new_mm"], 1)
            act.activation(flat(new_relu[:, :, :]), ps[0:SMP, 6, 0:DEC_BATCH * SMP], ACT.Relu).then_inc(S["new_relu_r"], 1)
            for b in range(DEC_BATCH):
                for half in range(2):
                    act.wait_ge(S["si_tr"], 4 + 2 * b + half + 1)
                    if b >= 2:
                        act.wait_ge(S["si_mm"], b - 1)
                    act.activation(kit[b % 2][:, half * 512:(half + 1) * 512], ps[0:IDX_D, 6 + half, :], ACT.Copy)\
                        .then_inc(S["si_kt"], 1)
                act.wait_ge(S["si_mm"], b + 1)
                if b >= 2:
                    act.wait_ge(S["si_acc"], b - 1)
                bank = 2 * (b % 2)
                act.activation(relu_s[:, b % 2, :], ps[0:SMP, bank:bank + 2, :].rearrange("p a n -> p (a n)"), ACT.Relu)\
                    .then_inc(S["si_relu"], 1)
            act.wait_ge(S["new_acc"], 1)
            for n in range((QB - 2) * IDX_H):
                w = P * (3 + n // IDX_H)
                act.wait_ge(S["is_mm"], n + 1)
                if n >= 2:
                    act.wait_ge(S["is_acc"], n - 1)
                act.activation(relu[:, n % 2, 0:w], bank2(2 * (n % 4), w), ACT.Relu).then_inc(S["is_relu"], 1)
            act.wait_ge(S["kv_out"], 16 * 6)
            wide = [(sc[:, sc_off[i]:sc_off[i] + P * (i + 1)], P, P * (i + 1)) for i in (6, 7)] + [(sc_s[:, :], SMP, TOK)]

            def bit_signs(k):
                act.wait_ge(S["trial_r"], k + 1)
                for q, (s, pn, w) in zip(ACT_Q, wide):
                    ins = act.activation(junk[0:pn, junk_off[q]:junk_off[q] + w], s, ACT.Sign, scale=-1.0,
                                         bias=trial[0:pn, q:q + 1].bitcast(F32),
                                         accum_out=signs[0:pn, q - ACT_Q[0]:q - ACT_Q[0] + 1])
                ins.then_inc(S["signs_r"], 1)

            bit_signs(0)
            with act.Fori(0, BITS // 2) as i:
                for j in range(2):
                    bit_signs(i * 2 + (j + 1))
            mlp_start(act, "act")

            def exps(n):
                w = P * (n // KV + 1)
                for g in range(GRP):
                    a = n * GRP + g
                    act.wait_ge(S["at_max"], a + 1)
                    if g == 0 and n >= 2:
                        act.wait_ge(S["at_tr"], steps_before[n - 1])
                        act.wait_ge(S["at_nrm"], GRP * (n - 1))
                    act.activation(pr[n % 2][:, g, 0:w], bank2(2 * (a % 2), w), ACT.Exp, bias=mx[:, a % 4:a % 4 + 1], scale=SCALE,
                                   accum_out=den[:, a % 8:a % 8 + 1]).then_inc(S["at_exp"], 1)

            def ptt_copies(n):
                for k in range(1, n // KV + 1):
                    c = steps_before[n] + k
                    act.wait_ge(S["at_tr"], c + 1)
                    if c >= 2:
                        act.wait_ge(S["at_pv"], c - 1)
                    act.activation(ptt[:, c % 2, :], ps[:, 4 + c % 2, :], ACT.Copy).then_inc(S["at_ptt"], 1)

            exps(0)
            for n in range(GROUPS):
                if n + 1 < GROUPS:
                    exps(n + 1)
                ptt_copies(n)

            def sample_copies(G):
                for k in range(3):
                    act.wait_ge(S["sa_ptr"], 3 * G + k + 1)
                    if G:
                        act.wait_ge(S["vp_used"], 2 * G)
                    if k < 2:
                        act.activation(flat(pt_s[:, 4 * k:4 * k + 4, :]), ps[:, 6 + k, :], ACT.Copy).then_inc(S["sa_pt"], 1)
                    else:
                        act.activation(pt_s[0:SMP, PAGES, :], ps[0:SMP, 6, 0:P], ACT.Copy).then_inc(S["sa_pt"], 1)

            act.wait_ge(S["at_nrm"], HEADS)
            for G in range(DEC_BATCH // 2):
                for n in range(8 * G, 8 * G + 8):
                    act.wait_ge(S["sa_tr"], n + 1)
                    if n >= 4:
                        act.wait_ge(S["sa_mm"], n // 4)
                    act.activation(kts[:, n // 2 % 2, n % 2 * 512:(n % 2 + 1) * 512], ps[:, 6 + n % 2, :], ACT.Copy)\
                        .then_inc(S["sa_kts"], 1)
                act.wait_ge(S["at_max"], HEADS + G + 1)
                if G >= 2:
                    act.wait_ge(S["sa_ptr"], 3 * (G - 1))
                    act.wait_ge(S["at_nrm"], HEADS + G - 1)
                bias, total = mx[:, G % 4:G % 4 + 1], den[:, G:G + 1]
                s0 = 3 * (G % 2)
                own.then(act.activation(pr0[:, G % 2, 0:704].rearrange("p (a n) -> p a n", a=2), ps[:, s0:s0 + 2, 0:352], ACT.Exp,
                                        bias=bias, scale=SCALE, accum_out=total))
                own.then(act.activation(pr0[:, G % 2, 704:1024], ps[:, s0 + 2, 0:320], ACT.Exp, bias=bias, scale=SCALE,
                                        accum_out=den[:, 4 + G:5 + G]))
                act.activation(pr_new[:, G % 2, :], ps[:, s0 + 2, 320:352], ACT.Exp, bias=bias, scale=SCALE,
                               accum_out=den_new[:, G:G + 1]).then_inc(S["at_exp"], 1)
                if G:
                    sample_copies(G - 1)
            sample_copies(DEC_BATCH // 2 - 1)
            mlp_start(act, "act")
            act.dma_start(x[:, 0:4, :], x_spill[:, 0:4, :]).then_inc(S["x_back0"], 16)
            act.dma_start(x[:, 4:8, :], x_spill[:, 4:8, :]).then_inc(S["x_back1"], 16)
            for m in range(KT):
                act.activation(xh[:, m, :], oq[:, m, :], ACT.Copy).then_inc(S["mix_h"], 1)
            act.wait_ge(S["mix_l"], 2 * KT)
            units(act, FIRST["att_out"], U_ATT_OUT, 2, square_unit(3, FIRST["att_out"]))
            mlp(1, None)
            mlp_start(act, "act")
            y_act(act, norm_root)

        def rest_of_dve(dve, own, norm_mean, output_units, mlp):
            first = FIRST["att_in"]
            norm_mean(2, 3 - 3 * (first % 2))
            r3 = rstd[:, :].rearrange("p (a t) -> p a t", a=3)

            def project_unit(j, off):
                dve.wait_ge(mm_out, j + off + 3)
                dve.tensor_tensor(oq[:, ds(j + off - first, 1), :].rearrange("p o (a t) -> p (o a) t", a=3),
                                  set_view(j, 0, 3)[:, :, 0:352], r3, ALU.mult).then_inc(set_free, 1)

            units(dve, first, 16, 2, project_unit)
            j = first + 16
            dve.wait_ge(mm_out, j + 3)
            for out in (ki[0:IDX_D, :], ki[IDX_D:2 * IDX_D, :]):
                own.did(dve.tensor_tensor(out.rearrange("p (a t) -> p a t", a=3), set_view(j, 0, 3)[0:IDX_D, :, 0:352],
                                          r3[0:IDX_D], ALU.mult))
            dve.tensor_tensor(wi[:, :].rearrange("p (a t) -> p a t", a=3), set_view(j, 0, 3)[IDX_D:IDX_D + IDX_H, :, 0:352],
                              r3[IDX_D:IDX_D + IDX_H], ALU.mult).then_inc(set_free, 1)
            mlp_start(dve, "dve")

            for t in range(QB + 1):
                w, bank = P if t < QB else SMP, 2 * (t % 4)
                dve.wait_ge(S["tk_mm"], t + 1)
                own.did(dve.tensor_copy(wic[0:w, t, :], ps[0:w, bank, KV * P:KV * P + IDX_H]))
                dve.tensor_copy(ktok[0:w, t, :], ps[0:w, bank, 0:KV * P]).then_inc(S["tk_dve"], 1)
            for par in range(2):
                own.did(dve.tensor_copy(qis[:, :, par::2, :].rearrange("p b h t -> p h b t"),
                                        oq[IDX_D * par:IDX_D * (par + 1), 12:16, SEQ:TOK].rearrange("p h (b t) -> p h b t", t=DEC_SEQ)))
            dve.wait_ge(S["tk_mm"], QB + 2)
            dve.wait_ge(S["acst_in"], 32)
            own.then(dve.tensor_copy(w_rows[:, 0:SMP], ps[0:SMP, 2, 0:SMP]))
            dve.tensor_tensor(w_tok[:, :, :], acst[0:SMP, A_TOK:A_TOK + DEC_BATCH * SMP].rearrange("p (b t) -> p b t", b=DEC_BATCH),
                              w_rows[:, 0:SMP].unsqueeze(1).to_broadcast([SMP, DEC_BATCH, SMP]), ALU.mult).then_inc(S["w_tok_r"], 1)
            dve.wait_ge(S["new_acc"], 1)
            dve.tensor_tensor(sc_s[:, PAST:], ps[0:SMP, 7, 0:SMP], acst[0:SMP, A_CAPS:A_CAPS + SMP], ALU.min)\
                .then_inc(S["new_out"], 1)
            dve.wait_ge(S["si_acc"], DEC_BATCH)
            dve.tensor_copy(sc_s[:, 0:PAST], ps[0:SMP, 4:6, :].rearrange("p a n -> p (a n)")).then_inc(S["sc_done"], 1)
            for n in range((QB - 2) * IDX_H):
                i, h = 2 + n // IDX_H, n % IDX_H
                w = P * (i + 1)
                dst = sc[:, sc_off[i]:sc_off[i] + w]
                dve.wait_ge(S["is_relu"], n + 1)
                if h == 0:
                    dve.tensor_scalar(dst, relu[:, n % 2, 0:w], wic[:, i, 0:1], None, ALU.mult).then_inc(S["is_acc"], 1)
                else:
                    dve.wait_ge(S["is_acc"], n)
                    dve.scalar_tensor_tensor(dst, relu[:, n % 2, 0:w], wic[:, i, h:h + 1], dst, ALU.mult, ALU.add)\
                        .then_inc(S["is_acc"], 1)
                if h == IDX_H - 1:
                    dve.wait_ge(S["is_acc"], n + 1)
                    own.did(dve.tensor_tensor(dst[:, w - P:w], dst[:, w - P:w], acst[:, A_CAP:A_CAP + P], ALU.min))
            own.wait()
            dve.wait_ge(S["new_out"], 1)
            dve.wait_ge(S["sc_done"], 1)
            dve.wait_ge(S["kv_out"], 16 * 6)

            rows_of = [(sc[:, sc_off[i]:sc_off[i] + P * (i + 1)], mb[:, sc_off[i]:sc_off[i] + P * (i + 1)], P, P * (i + 1))
                       for i in range(2, QB)] + [(sc_s[:, :], mb_s[:, :], SMP, TOK)]
            own.did(dve.memset(cnt[:, :], 0.0))
            own.did(dve.memset(signs[:, :], 0.0))
            for q in ACT_Q:
                own.did(dve.memset(half_w[:, q - ACT_Q[0]:q - ACT_Q[0] + 1], rows_of[q][3] / 2.0))
            own.wait()

            def count(limit, op, which):
                for q in which:
                    s, _, pn, w = rows_of[q]
                    lim = limit if isinstance(limit, float) else limit[0:pn, q:q + 1].bitcast(F32)
                    own.did(dve.tensor_scalar(junk[0:pn, junk_off[q]:junk_off[q] + w], s, lim, 0.0, op, ALU.add,
                                              accum_out=cnt[0:pn, q:q + 1]))
                own.wait()

            count(0.0, ALU.is_ge, range(NB))
            own.then(dve.tensor_scalar(neg[:, :], cnt[:, :], float(TOPK), None, ALU.is_lt))
            own.then(dve.tensor_scalar(cand[:, :], neg[:, :], -2.0 ** 31, None, ALU.mult))
            act_cols = slice(ACT_Q[0], NB)

            def bit(k):
                dve.tensor_tensor(trial[:, :], cand[:, :], bits[:, ds(k, 1)].to_broadcast([P, NB]), ALU.bitwise_or)\
                    .then_inc(S["trial_r"], 1)
                dve.wait_ge(S["trial_r"], k + 1)
                count(trial, ALU.is_ge, DVE_Q)
                dve.wait_ge(S["signs_r"], k + 1)
                own.then(dve.scalar_tensor_tensor(cnt[:, act_cols], signs[:, :], -0.5, half_w[:, :], ALU.mult, ALU.add))
                own.then(dve.scalar_tensor_tensor(acc[:, :], cnt[:, :], float(TOPK), neg[:, :], ALU.is_ge, ALU.not_equal))
                own.then(dve.tensor_tensor(carry[:, :], acc[:, :], acst[:, ds(A_BITF + k, 1)].to_broadcast([P, NB]), ALU.mult))
                own.then(dve.tensor_tensor(cand[:, :], cand[:, :], carry[:, :], ALU.bitwise_or))

            bit(0)
            with own.loop(BITS // 2, 2 * (4 + len(DVE_Q))) as i:
                for j in range(2):
                    bit(i * 2 + (j + 1))
            part = [bits[:, BITS + k:BITS + k + 1].to_broadcast([P, NB]) for k in range(3)]

            def plus(dst, src, add):
                own.then(dve.tensor_tensor(hi16[:, :], src[:, :], part[2], ALU.bitwise_and))
                own.then(dve.tensor_tensor(trial[:, :], src[:, :], part[0], ALU.bitwise_and))
                own.then(dve.tensor_tensor(trial[:, :], trial[:, :], add[:, :], ALU.add))
                own.then(dve.tensor_tensor(carry[:, :], trial[:, :], part[1], ALU.bitwise_and))
                own.then(dve.tensor_tensor(trial[:, :], trial[:, :], part[0], ALU.bitwise_and))
                own.then(dve.tensor_tensor(hi16[:, :], hi16[:, :], carry[:, :], ALU.add))
                own.then(dve.tensor_tensor(dst[:, :], hi16[:, :], trial[:, :], ALU.bitwise_or))

            own.then(dve.tensor_scalar(acc[:, :], neg[:, :], -1.0, 1.0, ALU.mult, ALU.add))
            plus(trial, cand, acc)
            count(trial, ALU.is_ge, range(NB))
            own.then(dve.scalar_tensor_tensor(acc[:, :], cnt[:, :], float(TOPK), neg[:, :], ALU.is_ge, ALU.not_equal))
            plus(cand, cand, acc)
            count(cand, ALU.is_gt, range(NB))
            own.then(dve.tensor_scalar(quota[:, :], cnt[:, :], -1.0, float(TOPK), ALU.mult, ALU.add))
            mlp_start(dve, "dve")

            def mask(q):
                s, m, pn, w = rows_of[q]
                lim = cand[0:pn, q:q + 1].bitcast(F32)
                eq, pre = scr[0][0:pn, 0:w], scr[1][0:pn, 0:w]
                own.then(dve.tensor_scalar(eq, s, lim, None, ALU.is_equal))
                own.then(dve.tensor_tensor_scan(pre, ones[0:pn, 0:1].to_broadcast([pn, w]), eq, 0.0, ALU.mult, ALU.add))
                own.then(dve.scalar_tensor_tensor(eq, pre, quota[0:pn, q:q + 1], eq, ALU.is_le, ALU.mult))
                own.then(dve.scalar_tensor_tensor(pre, s, lim, eq, ALU.is_gt, ALU.add))
                dve.tensor_scalar(m, pre, -1.0, -MASKED, ALU.add, ALU.mult).then_inc(S["mask_r"], 1)
                dve.wait_ge(S["mask_r"], q + 1)

            def maximum(a, view):
                col = mx[:, a % 4:a % 4 + 1]
                own.then(dve.tensor_reduce(col, view, AX, ALU.max))
                dve.tensor_scalar(col, col, -SCALE, None, ALU.mult).then_inc(S["at_max"], 1)

            def head_max(a):
                if a < HEADS:
                    dve.wait_ge(S["at_mm"], a + 1)
                    if a >= 4:
                        dve.wait_ge(S["at_exp"], a - 3)
                    maximum(a, bank2(2 * (a % 2), P * (a // (GRP * KV) + 1)))

            def output(n):
                i, kv = n // KV, n % KV
                dve.wait_ge(S["at_pv"], steps_before[n + 1])
                dve.tensor_copy(oq[:, GRP * kv:GRP * (kv + 1), i * P:(i + 1) * P], quad(6 + n % 2)).then_inc(S["at_o"], 1)

            def normalise(n):
                w = P * (n // KV + 1)
                for g in range(GRP):
                    a = n * GRP + g
                    dve.wait_ge(S["at_exp"], a + 1)
                    own.then(dve.reciprocal(rden[:, a % 8:a % 8 + 1], den[:, a % 8:a % 8 + 1]))
                    dve.tensor_scalar(pr[n % 2][:, g, 0:w], pr[n % 2][:, g, 0:w], rden[:, a % 8:a % 8 + 1], None, ALU.mult)\
                        .then_inc(S["at_nrm"], 1)

            for a in range(GRP):
                head_max(a)
            normalise(0)
            for n in range(GROUPS):
                for g in range(GRP):
                    head_max((n + 1) * GRP + g)
                c = steps_before[n]
                dve.wait_ge(S["at_tr"], c + 1)
                if c >= 2:
                    dve.wait_ge(S["at_pv"], c - 1)
                dve.tensor_copy(ptt[:, c % 2, :], ps[:, 4 + c % 2, :]).then_inc(S["at_ptt0"], 1)
                if n:
                    output(n - 1)
                if n + 1 < GROUPS:
                    normalise(n + 1)
                if n < NB:
                    mask(n)
                if n == NB:
                    dve.tensor_copy(qs[:, :, :, :].rearrange("p b h t -> p h b t"),
                                    oq[:, 0:Q_HEADS, SEQ:TOK].rearrange("p h (b t) -> p h b t", t=DEC_SEQ))\
                        .then_inc(S["mask_r"], 1)
            output(GROUPS - 1)

            def sample_max(G):
                dve.wait_ge(S["sa_mm"], 2 * G + 2)
                if G == 0:
                    dve.wait_ge(S["at_exp"], HEADS)
                s0 = 3 * (G % 2)
                col = mx[:, G % 4:G % 4 + 1]
                own.then(dve.tensor_reduce(rden[:, G % 2:G % 2 + 1], ps[:, s0:s0 + 3, 0:352], mybir.AxisListType.XY, ALU.max))
                dve.tensor_scalar(col, rden[:, G % 2:G % 2 + 1], -SCALE, None, ALU.mult).then_inc(S["at_max"], 1)

            def sample_output(G):
                dve.wait_ge(S["vp_used"], 2 * G + 2)
                for b2 in range(2):
                    for kv in range(KV):
                        q4, b = 2 * b2 + kv, 2 * G + b2
                        ins = dve.tensor_copy(oq[:, GRP * kv:GRP * (kv + 1), SEQ + b * DEC_SEQ:SEQ + (b + 1) * DEC_SEQ],
                                              ps[:, 3 * (G % 2) + 2, 384 + 16 * q4:400 + 16 * q4].rearrange("p (h t) -> p h t", h=GRP))
                        if q4 < 3:
                            own.did(ins)
                        else:
                            ins.then_inc(S["at_o"], 1)

            dve.wait_ge(S["at_nrm"], HEADS)
            for G in range(DEC_BATCH // 2):
                sample_max(G)
                dve.wait_ge(S["at_exp"], HEADS + G + 1)
                total = rden[:, 4 + G:5 + G]
                own.then(dve.tensor_tensor(total, den[:, G:G + 1], den[:, 4 + G:5 + G], ALU.add))
                own.then(dve.tensor_tensor(total, total, den_new[:, G:G + 1], ALU.add))
                own.then(dve.reciprocal(total, total))
                own.did(dve.tensor_scalar(pr0[:, G % 2, :], pr0[:, G % 2, :], total, None, ALU.mult))
                dve.tensor_scalar(pr_new[:, G % 2, :], pr_new[:, G % 2, :], total, None, ALU.mult).then_inc(S["at_nrm"], 1)
                if G:
                    sample_output(G - 1)
            sample_output(DEC_BATCH // 2 - 1)
            mlp_start(dve, "dve")
            for m in range(KT):
                dve.wait_ge(S["mix_h"], KT + m + 1)
                dve.tensor_tensor(xl[:, m, :], oq[:, m, :], xh[:, m, :].bitcast(F32), ALU.subtract).then_inc(S["mix_l"], 1)
            output_units(FIRST["att_out"], 3, 32)
            mlp(1, None)
            mlp_start(dve, "dve")
            y_dve(dve, norm_mean)

        @block.sync
        def _(sp):
            vec = [("norm_mix", 0, R_MIX0), ("norm_mix", 1, R_MIX1), ("norm_mlp", 0, R_MLP0), ("norm_mlp", 1, R_MLP1)]
            for name, l, r in vec:
                sp.dma_start(cst_rows[r:r + KT, :], A[name][l].rearrange("(m c) -> m c", c=P)).then_inc(S["start_in"], 16)
            sp.dma_start(cst_rows[R_FIN:R_FIN + KT, :], A["norm_final"].rearrange("(m c) -> m c", c=P)).then_inc(S["start_in"], 16)
            sp.dma_start(cst_rows[R_CONV:R_CONV + CONV_W * CT, :],
                         A["w_conv"][0].rearrange("i (m c) -> (i m) c", c=P)).then_inc(S["start_in"], 16)
            for name, r in (("b_conv", R_BCONV), ("rg_ba", R_BA), ("rg_bx", R_BX), ("rg_lambda", R_LAM)):
                sp.dma_start(cst_rows[r:r + RT, :], A[name][0].rearrange("(m c) -> m c", c=P)).then_inc(S["start_in"], 16)
            sp.dma_start(cst_rows[R_DN:R_DN + 1, :], A["dn_norm"]).then_inc(S["start_in"], 16)
            sp.dma_start(conv_rows[:, :], A["state_conv"][0].rearrange("b i c -> (b i) c")).then_inc(S["start_in"], 16)
            sp.dma_start(h0_rows[:, :], A["state_h"][0]).then_inc(S["start_in"], 16)
            sp.dma_start(nea[32:32 + DN_H, :], A["dn_a_log"].rearrange("a h -> h a")).then_inc(S["start_in"], 16)
            sp.dma_start(dtb[32:32 + DN_H, :], A["dn_dt_bias"].rearrange("a h -> h a")).then_inc(S["start_in"], 16)

            def load(src, kts):
                def body(j, off):
                    sp.wait_ge(w_split, j + off + 1)
                    sp.dma_start(w_raw[:, j % 2, 0:kts * P].rearrange("p (k n) -> p k n", k=kts), src(j, off))\
                        .then_inc(w_loaded[j % 2], 16)
                return body

            first = FIRST["rec_in"]
            units(sp, first, 24, 2, load(lambda j, off: w_in_rec[:, :, ds((j + off - first) * P, P)], KT))
            j = first + 24
            sp.wait_ge(w_split, j + 1)
            last = w_raw[:, j % 2, :].rearrange("p (k n) -> p k n", k=KT)
            with nc.allow_non_contiguous_dma(reason="eight narrow columns"):
                sp.dma_start(last[:, :, 0:DN_H], w_in_rec[:, :, 24 * P:24 * P + DN_H]).then_inc(w_loaded[j % 2], 16)
                sp.dma_start(last[:, :, 32:32 + DN_H], w_in_rec[:, :, 24 * P + DN_H:24 * P + 2 * DN_H])\
                    .then_inc(w_loaded[j % 2], 16)
            sp.wait_ge(S["wax_zero"], 1)
            for g, name in enumerate(("rg_wa", "rg_wx")):
                for half in range(2):
                    o = 64 * half
                    sp.dma_start(wax[o:o + 64, g, :, o:o + 64], A[name][0].rearrange("(m two) i j -> two i m j", two=2)[half])\
                        .then_inc(S["gate_w"], 16)
            sp.dma_start(reset[32:32 + DN_H, :], A["row_reset"]).then_inc(S["gate_w"], 16)
            first = FIRST["rec_out"]
            units(sp, first, U_REC_OUT, 2, load(lambda j, off: w_out_rec[:, :, ds((j + off - first) * P, P)], KT))
            mlp_loads(sp, 0, load)
            rest_of_sync(sp, load)

        @block.gpsimd
        def _(pool):
            own = Chain(pool, pool_chain)
            pool.memset(eps_col, EPS).then_inc(w_split, 1)
            pool.memset(one_col, 1.0).then_inc(w_split, 1)
            own.then(pool.memset(ident[:, :], 0.0))
            own.then(pool.affine_select(out=ident[:, :], in_=ident[:, :], compare_op=ALU.not_equal, fill=1.0, base=0,
                                        pattern=[[-1, P]], channel_multiplier=1))
            own.did(pool.memset(ones[:, :], 1.0))
            pool.drain().then_inc(const_in, 1)

            def split(kts, extra=0):
                def body(j, off):
                    pool.wait_ge(w_loaded[j % 2], 16 * (j // 2 + 1 + extra) + off * 8)
                    pool.wait_ge(mm_out, j + off + 1)
                    n = kts * P
                    pool.tensor_tensor(w_hi[:, j % 2, 0:n], w_raw[:, j % 2, 0:n], ones[:, 0:1].to_broadcast([P, n]),
                                       ALU.mult).then_inc(w_hi_done, 1)
                    pool.wait_ge(w_hi_done, j + off + 1)
                    pool.tensor_tensor(w_lo[:, j % 2, 0:n], w_raw[:, j % 2, 0:n], w_hi[:, j % 2, 0:n].bitcast(F32),
                                       ALU.subtract).then_inc(w_split, 1)
                return body

            extra = {0: 0, 1: 0}

            def split_units(first, count, per, kts):
                units(pool, first, count, per,
                      lambda j, off: split(kts, extra[j % 2])(j, off))

            def mlp_split(l):
                first = FIRST[f"mlp{l}"]
                with pool.Fori(0, FF_CHUNKS) as c:
                    for q in range(12):
                        split(KT if q < FT else FT, extra[(first + q) % 2])(first + q, c * 12)

            end_phase(pool, "pool")
            split_units(FIRST["rec_in"], 24, 2, KT)
            extra[0] += 1
            split_units(FIRST["rec_in"] + 24, 1, 1, KT)
            pool.wait_ge(mm_out, 2 + U_REC_IN)
            pool.memset(wax[:, :, :, :], 0.0).then_inc(S["wax_zero"], 1)
            end_phase(pool, "pool")
            end_phase(pool, "pool")
            own.then(pool.memset(rows[:, :], 0.0))
            own.then(pool.memset(dn["st"][:, :, :], 0.0))
            end_phase(pool, "pool")
            end_phase(pool, "pool")

            def pool_chunk(c, t0, w, levels):
                pool.tensor_copy(rowc[:, 0:w], rows[:, ds(t0, w)]).then_inc(S["rowc_cp"], 1)
                pool.tensor_copy(dn["kc"][:, :, 0:w], qkvz[:, 4:8, ds(t0, w)]).then_inc(S["kc_cp"], 1)
                pool.tensor_copy(dn["vc"][:, :, 0:w], qkvz[:, 8:12, ds(t0, w)]).then_inc(S["vc_cp"], 1)
                pool.wait_ge(S["lm_r"], c + 1)
                for l in range(levels):
                    pool.tensor_tensor(dn[f"lo{l}"][0:w, :, 0:w], dn["lm"][0:w, :, 0:w],
                                       cst[0:w, C_LEVEL + l:C_LEVEL + l + 1, 0:w].to_broadcast([w, DN_H, w]),
                                       ALU.mult).then_inc(S["lo_r"], 1)

            with pool.Fori(0, QB) as c:
                pool_chunk(c, c * P, P, LEVELS)
            pool_chunk(QB, SEQ, SMP, 1)
            end_phase(pool, "pool")
            split_units(FIRST["rec_out"], U_REC_OUT, 2, KT)
            mlp_split(0)
            rest_of_pool(pool, split_units, mlp_split)

        @block.tensor
        def _(pe):
            pe.wait_ge(const_in, 1)
            pe.wait_ge(S["start_in"], 16 * 15)
            pe.transpose(ps[:, 0, 0:R_ALL], cst_rows[:, :], ident[0:R_ALL, 0:R_ALL]).then_inc(mm_out, 1)
            nh = DEC_BATCH * 3
            for m in range(CT):
                pe.transpose(ps[:, 1, m * nh:(m + 1) * nh], conv_rows[:, m * P:(m + 1) * P], ident[0:nh, 0:nh])
            for m in range(RT):
                o = CT * nh + m * DEC_BATCH
                last = pe.transpose(ps[:, 1, o:o + DEC_BATCH], h0_rows[:, m * P:(m + 1) * P],
                                    ident[0:DEC_BATCH, 0:DEC_BATCH])
            last.then_inc(mm_out, 1)
            pe.wait_ge(S["tok_in"], 16 * 3)
            for k in range(2 * (QB + 1)):
                t, half = k // 2, k % 2
                w = P if t < QB else SMP
                if k >= 6:
                    pe.wait_ge(S["xt_act"] if k % 2 == 0 else S["xt_dve"], (k - 6) // 2 + 1)
                for q in range(4):
                    f = half * 4 + q
                    last = pe.transpose(quad(2 + k % 6)[:, q, 0:w], xtok[0:w, t, f * P:(f + 1) * P], ident[0:w, 0:w])
                last.then_inc(S["xt_mm"], 1)
            end_phase(pe, "pe")

            def norm_sum(n, bank):
                pe.wait_ge(S["sq_added"], 8 * (n + 1))
                for t, (c0, w) in enumerate(CUTS352):
                    mm = pe.matmul(ps[:, bank + t, 0:w], ones[:, :], sumsq[:, c0:c0 + w], start=True, stop=True)
                mm.then_inc(S["ss_mm"], 1)
                pe.wait_ge(S["ms_ready"], n + 1)

            def first_unit(n, j):
                def ready(k):
                    pe.wait_ge(S["xh_ready"], 8 * n + k + 1)
                    pe.wait_ge(S["xl_ready"], 8 * n + k + 1)

                unit(KT, xh, xl, CUTS352, ready)(j, 0)
                pe.wait_ge(set_free, j + 2)
                norm_sum(n, 3 - 3 * (j % 2))

            def unit(kts, hi, lo, cuts, ready=None):
                def body(j, off):
                    pe.wait_ge(w_split, j + off + 3)
                    pe.wait_ge(set_free, j + off + 1)
                    passes = ((w_hi, hi), (w_hi, lo), (w_lo, hi))
                    for k in range(kts):
                        if ready:
                            ready(k)
                        for p, (w, r) in enumerate(passes):
                            for t, (c0, n) in enumerate(cuts):
                                mm = pe.matmul(ps[:, 3 * (j % 2) + t, 0:n], w[:, j % 2, k * P:(k + 1) * P],
                                               r[:, k, c0:c0 + n], start=(k == 0 and p == 0),
                                               stop=(k == kts - 1 and p == 2))
                    mm.then_inc(mm_out, 1)
                return body

            first_unit(0, FIRST["rec_in"])
            units(pe, FIRST["rec_in"] + 1, 24, 2, unit(KT, xh, xl, CUTS352))
            end_phase(pe, "pe")

            nt = 3 + DEC_BATCH * 3
            for k in range(4):
                for q in range(4):
                    last = pe.transpose(ps[0:nt, 6 + k % 2, q * P:(q + 1) * P], ctail[:, 4 * k + q, :], ident[:, :])
                last.then_inc(S["tail_mm"], 1)
                if k < 3 and k >= 1:
                    pe.wait_ge(S["tail_sb"], k)
            pe.wait_ge(S["gate_w"], 80)
            for m in range(RT):
                for g in range(2):
                    if m > 0:
                        pe.wait_ge(S["ri_read"], 2 * (m - 1) + g + 1)
                    for t, (c0, n) in enumerate(CUTS512):
                        mm = pe.matmul(ps[:, 3 * g + t, 0:n], wax[:, g, m, :], xr[:, m, c0:c0 + n], start=True, stop=True)
                    mm.then_inc(S["ri_mm"], 1)
            pe.wait_ge(S["rg_done"], RT)
            for m in range(RT):
                last = pe.transpose(ps[0:DEC_BATCH + 1, 6, m * P:(m + 1) * P], hT[:, m, :], ident[:, :])
            last.then_inc(S["ht_mm"], 1)
            end_phase(pe, "pe")
            end_phase(pe, "pe")

            def head_norms(batch, n0, rows_of):
                for n, r in enumerate(rows_of):
                    pe.wait_ge(S["cn_sq"], n0 + n + 1)
                    for t, (c0, w) in enumerate(CUTS352):
                        mm = pe.matmul(ps[0:NR, t, 0:w], cst[:, C_STRIP, 64 - r:64 - r + NR], sq8[:, n, c0:c0 + w],
                                       start=n == 0, stop=n == len(rows_of) - 1)
                mm.then_inc(S["cn_mm"], 1)
                pe.wait_ge(S["cn_rec"], batch + 1)
                for n, r in enumerate(rows_of):
                    if n >= 2:
                        pe.wait_ge(S["cn_out"], n0 + n - 1)
                    sel = C_SELB + r if r < DN_H else C_SELG + r - 32
                    for t, (c0, w) in enumerate(CUTS352):
                        mm = pe.matmul(ps[:, 3 * (n % 2) + t, 0:w], cst[0:NR, sel, :], norm_rows[:, c0:c0 + w],
                                       start=True, stop=True)
                    mm.then_inc(S["cn_bc"], 1)

            pe.wait_ge(S["gate_w"], 96)
            head_norms(0, 0, (0, 1, 2, 3, 32, 33, 34, 35))
            end_phase(pe, "pe")

            def pe_chunk(c, t0, w, levels, smp):
                pe.wait_ge(S["rowc_cp"], c + 1)
                pe.wait_ge(S["o_st"], c + 1)
                pe.transpose(ps[0:w, 2, 0:P], rowc[:, 0:w], ident[:, :]).then_inc(S["pe_col"], 1)
                for bank, s in ((0, C_SELG), (1, C_SELB)):
                    for h in range(DN_H):
                        mm = pe.matmul(quad(bank)[:, h, 0:w], cst[:, s + h, :], rows[:, ds(t0, w)], start=True, stop=True)
                mm.then_inc(S["pe_bc"], 1)
                pe.wait_ge(S["kc_cp"], c + 1)
                for h in range(DN_H):
                    pe.matmul(quad(3)[0:w, h, 0:w], dn["kc"][:, h, 0:w], dn["kc"][:, h, 0:w], start=True, stop=True)
                for h in range(DN_H):
                    mm = pe.matmul(quad(4)[0:w, h, 0:w], dn["kc"][:, h, 0:w],
                                   qkvz[:, h, ds(t0, w)], start=True, stop=True)
                mm.then_inc(S["pe_kk"], 1)
                pe.wait_ge(S["st_r"], c + 1)
                for h in range(DN_H):
                    mm = pe.transpose(quad(6)[0:w, h, :], dn["kc"][:, h, 0:w], ident[:, :])
                mm.then_inc(S["pe_kt"], 1)
                pe.wait_ge(S["vc_cp"], c + 1)
                for h in range(DN_H):
                    mm = pe.transpose(quad(7)[0:w, h, :], dn["vc"][:, h, 0:w], ident[:, :])
                mm.then_inc(S["pe_vt"], 1)
                pe.wait_ge(S["lt_r"], c + 1)
                for h in range(DN_H):
                    mm = pe.transpose(quad(5)[0:w, h, 0:w], dn["lt"][0:w, h, 0:w], ident[0:w, 0:w])
                mm.then_inc(S["pe_l"], 1)
                pe.wait_ge(S["x0_r"], c + 1)
                for l in range(levels):
                    pe.wait_ge(S["lo_r"], c * LEVELS + l + 1)
                    if l:
                        pe.wait_ge(S["x_sb"], c * LEVELS + l)
                    for h in range(DN_H):
                        mm = pe.matmul(quad(3)[0:w, h, 0:w], dn[f"lo{l}"][0:w, h, 0:w], dn["xti"][0:w, h, 0:w],
                                       start=True, stop=True)
                    mm.then_inc(S["pe_y"], 1)
                    pe.wait_ge(S["y_sb"], c * LEVELS + l + 1)
                    if l:
                        pe.wait_ge(S["xi_sb"], c * (LEVELS - 1) + l)
                    for h in range(DN_H):
                        mm = pe.matmul(quad(5)[0:w, h, 0:w], dn["xi"][0:w, h, 0:w], dn["yy"][0:w, h, 0:w],
                                       start=True, stop=True)
                    mm.then_inc(S["pe_x"], 1)
                    if l < LEVELS - 1 and not smp:
                        for h in range(DN_H):
                            mm = pe.matmul(quad(4)[0:w, h, 0:w], dn["yy"][0:w, h, 0:w], dn["xi"][0:w, h, 0:w],
                                           start=True, stop=True)
                        mm.then_inc(S["pe_xi"], 1)
                pe.wait_ge(S["kbg_r"], c + 1)
                pe.wait_ge(S["dec_r"], c + 1)
                pe.wait_ge(S["egb_r"], c + 1)
                if not smp:
                    for h in range(DN_H):
                        mm = pe.matmul(quad(0)[:, h, :], dn["kbg"][:, h, :], dn["st"][:, h, :], start=True, stop=True)
                    mm.then_inc(S["pe_ks"], 1)
                else:
                    pe.wait_ge(S["qg_r"], c + 1)
                    pe.wait_ge(S["s0_in"], 16)
                    kq_out = ps[:, 0, 0:DN_H * 2 * SMP].rearrange("p (h a t) -> p h a t", h=DN_H, a=2)
                    for b in range(DEC_BATCH):
                        sl = slice(b * DEC_SEQ, (b + 1) * DEC_SEQ)
                        for h in range(DN_H):
                            mm = pe.matmul(kq_out[:, h, :, sl], s0[:, b, h, :], kq_s[:, h, :, sl], start=True, stop=True)
                    mm.then_inc(S["pe_ks"], 1)
                    pe.wait_ge(S["y_sb"], QB * LEVELS + 2)
                    for h in range(DN_H):
                        mm = pe.transpose(quad(1)[0:w, h, :], ks_s[:, h, 0, :], ident[:, :])
                    mm.then_inc(S["pe_ks"], 1)
                pe.wait_ge(S["rr_r"], c + 1)
                pe.wait_ge(S["x_sb"], c * LEVELS + levels)
                for h in range(DN_H):
                    mm = pe.matmul(quad(1)[0:w, h, :], dn["xti"][0:w, h, 0:w], dn["rr"][0:w, h, :], start=True, stop=True)
                mm.then_inc(S["pe_vn"], 1)
                pe.wait_ge(S["vn_r"], c + 1)
                pe.wait_ge(S["attn_r"], c + 1)
                pe.wait_ge(S["cols_r"], c + 1)
                if not smp:
                    pe.wait_ge(S["qg_r"], c + 1)
                    for h in range(DN_H):
                        pe.matmul(quad(2)[:, h, :], dn["st"][:, h, :], dn["qg"][:, h, :], start=True, stop=False)
                        mm = pe.matmul(quad(2)[:, h, :], dn["vn"][:, h, :], dn["attn"][:, h, :], start=False, stop=True)
                    mm.then_inc(S["pe_o"], 1)
                    pe.wait_ge(S["kd_r"], c + 1)
                    for h in range(DN_H):
                        mm = pe.matmul(quad(6)[:, h, :], dn["kd"][:, h, :], dn["vn"][:, h, :], start=True, stop=True)
                    mm.then_inc(S["pe_ds"], 1)
                else:
                    for h in range(DN_H):
                        mm = pe.matmul(quad(2)[:, h, 0:w], dn["vn"][0:w, h, :], dn["attn"][0:w, h, 0:w],
                                       start=True, stop=True)
                    mm.then_inc(S["pe_o"], 1)
                    pe.wait_ge(S["vb_r"], c + 1)
                    for b in range(DEC_BATCH):
                        pe.wait_ge(S["kdm_r"], b + 1)
                        if b >= 4:
                            pe.wait_ge(S["s0_out"], b - 3)
                        for h in range(DN_H):
                            mm = pe.matmul(quad(4 + b % 4)[:, h, :], kdm[0:w, b, h, :], dn["vn"][0:w, h, :],
                                           start=True, stop=True)
                        mm.then_inc(S["pe_ds"], 1)

            with pe.Fori(0, QB) as c:
                pe_chunk(c, c * P, P, LEVELS, False)
            pe_chunk(QB, SEQ, SMP, 1, True)
            head_norms(1, 8, (0, 1, 2, 3))
            end_phase(pe, "pe")
            pe.wait_ge(S["mix_h"], KT)
            pe.wait_ge(S["mix_l"], KT)
            units(pe, FIRST["rec_out"], U_REC_OUT, 2, unit(KT, xh, xl, CUTS352))

            def mlp(l):
                first = FIRST[f"mlp{l}"]

                def chunk(c, first_q):
                    for q in range(first_q, FT):
                        unit(KT, xh, xl, CUTS352)(first + q, c * 12)

                    def hidden(k):
                        pe.wait_ge(S["hh_r"], c * FT + (l * FF_CHUNKS * FT + k + 1))
                        pe.wait_ge(S["hl_r"], c * FT + (l * FF_CHUNKS * FT + k + 1))

                    for q in range(KT):
                        unit(FT, hh, hl, CUTS352, None if q else hidden)(first + FT + q, c * 12)

                first_unit(SHARED_N[("mlp", l)], first)
                chunk(0, 1)
                with pe.Fori(1, FF_CHUNKS) as c:
                    chunk(c, 0)

            mlp(0)
            rest_of_pe(pe, unit, first_unit, norm_sum, mlp)

        @block.scalar
        def _(act):
            own = Chain(act, act_chain)
            act.dma_start(xtok[:, 0:4, :], A["x_prompt"][0, 0:512].rearrange("(t p) d -> p t d", p=P)).then_inc(S["tok_in"], 16)
            act.dma_start(xtok[:, 4:8, :], A["x_prompt"][0, 512:1024].rearrange("(t p) d -> p t d", p=P)).then_inc(S["tok_in"], 16)
            act.dma_start(xtok[0:SMP, QB, :], A["x_sample"].rearrange("b t d -> (b t) d")).then_inc(S["tok_in"], 16)
            for k in range(0, 2 * (QB + 1), 2):
                t = k // 2
                w = P if t < QB else SMP
                act.wait_ge(S["xt_mm"], k + 1)
                act.activation(x[:, 0:4, t * P:t * P + w], quad(2 + k % 6)[:, :, 0:w], ACT.Copy).then_inc(S["xt_act"], 1)
            end_phase(act, "act")

            def split_hi(n, gain):
                for k in range(KT):
                    act.activation(xh[:, k, :], x[:, k, :], ACT.Copy, scale=prm[:, gain + k:gain + k + 1])\
                        .then_inc(S["xh_ready"], 1)

            def square(n, k, par, xk):
                if n:
                    act.wait_ge(S["sq_added"], k + (8 * n - 1))
                elif k >= 2:
                    act.wait_ge(S["sq_added"], k - 1)
                act.activation(sq[:, par, :], xk, ACT.Square).then_inc(S["sq_ready"], 1)

            def square_unit(n, first):
                def body(j, off):
                    act.wait_ge(set_free, j + off + 3)
                    square(n, j + off - first, (j - first) % 2, x[:, ds(j + off - first, 1), :].rearrange("p a t -> p (a t)"))
                return body

            def norm_root(n):
                act.wait_ge(S["ms_ready"], n + 1)
                act.activation(rstd[:, :], rstd[:, :], ACT.Sqrt).then_inc(S["rt_ready"], 1)

            act.dma_start(x_spill, x[:, :, :]).then_inc(S["x_spilled"], 16)
            split_hi(0, R_MIX0)
            for k in range(KT):
                square(0, k, k % 2, x[:, k, :])
            norm_root(0)
            act.wait_ge(S["x_spilled"], 16)

            def conv_unit(j, off):
                u = j + off
                act.wait_ge(set_free, u + 3)
                act.wait_ge(S["conv_done"], u + 1)
                heads = ub[:, 3 + SEQ:UB].rearrange("p (b t) -> p b t", b=DEC_BATCH)
                own.then(act.activation(heads[:, :, 0:3],
                                        hist[:, ds(u, 1), :].rearrange("p a (b t) -> p (a b) t", b=DEC_BATCH), ACT.Copy))
                own.did(act.activation(ctail[:, ds(u, 1), 0:3].rearrange("p a t -> p (a t)"), ub[:, SEQ:SEQ + 3], ACT.Copy))
                own.did(act.activation(ctail[:, ds(u, 1), 3:].rearrange("p a (b t) -> p (a b) t", b=DEC_BATCH),
                                       heads[:, :, DEC_SEQ:], ACT.Copy))
                act.activation(uc[:, 0:UB - 3], ub[:, 0:UB - 3], ACT.Copy, scale=prm[:, ds(R_CONV + u, 1)])\
                    .then_inc(S["uc0"], 1)
                act.wait_ge(S["conv_done"], u + 2)

            ucs = uc[:, 3 + SEQ:UB].rearrange("p (b t) -> p b t", b=DEC_BATCH)[:, :, 0:DEC_SEQ]

            def rg_unit(j, off):
                u = j + off
                conv_unit(j, off)
                bias = prm[:, ds(R_BCONV + u, 1)]
                own.did(act.activation(xr[:, ds(u, 1), 0:SEQ].rearrange("p a t -> p (a t)"), uc[:, 0:SEQ], ACT.Identity, bias=bias))
                own.did(act.activation(xr[:, ds(u, 1), SEQ:].rearrange("p a (b t) -> p (a b) t", b=DEC_BATCH), ucs,
                                       ACT.Identity, bias=bias))

            def qkv_unit(j, off):
                u = j + off
                conv_unit(j, off)
                own.did(act.activation(qkvz[:, ds(u - RT, 1), 0:SEQ].rearrange("p a t -> p (a t)"), uc[:, 0:SEQ], ACT.Silu))
                own.did(act.activation(qkvz[:, ds(u - RT, 1), SEQ:].rearrange("p a (b t) -> p (a b) t", b=DEC_BATCH), ucs,
                                       ACT.Silu))

            with own.loop(2, 10) as i:
                for j in range(2):
                    rg_unit(j, i * 2)
            with own.loop(6, 10) as i:
                for j in range(2):
                    qkv_unit(RT + j, i * 2)
            end_phase(act, "act")

            for k in range(4):
                act.wait_ge(S["tail_mm"], k + 1)
                act.activation(tail_rows[:, k * 512:(k + 1) * 512], ps[0:3 + DEC_BATCH * 3, 6 + k % 2, :], ACT.Copy)\
                    .then_inc(S["tail_sb"], 1)
            act.wait_ge(S["tail_sb"], 4)
            act.dma_start(O["conv_p"][0, 0], tail_rows[0:3, :]).then_inc(S["state_out"], 16)
            act.dma_start(O["conv_s"][0].rearrange("b i c -> (b i) c"), tail_rows[3:, :]).then_inc(S["state_out"], 16)

            for m in range(RT):
                for g, (dst, bias) in enumerate(((r_t, R_BA), (i_t, R_BX))):
                    act.wait_ge(S["ri_mm"], 2 * m + g + 1)
                    b = prm[:, bias + m:bias + m + 1]
                    own.did(act.activation(dst[:, m, 0:SEQ].rearrange("p (a t) -> p a t", a=2), ps[:, 3 * g:3 * g + 2, :],
                                           ACT.Sigmoid, bias=b))
                    act.activation(dst[:, m, SEQ:], ps[:, 3 * g + 2, 0:SMP], ACT.Sigmoid, bias=b).then_inc(S["ri_read"], 1)
            e, w, lw = tmp4[0], tmp4[1], tmp4[2]
            own.then(act.activation(e, prm[:, R_LAM:R_LAM + RT], ACT.Abs))
            own.then(act.activation(e, e, ACT.Exp, scale=-1.0))
            act.activation(w, e, ACT.Identity, bias=one_col).then_inc(S["rows_a"], 1)
            act.wait_ge(S["rows_a"], 1)
            act.activation(lw, w, ACT.Ln).then_inc(S["rows_a"], 1)
            own.then(act.activation(nea[32:32 + DN_H, :], nea[32:32 + DN_H, :], ACT.Exp))
            act.wait_ge(S["ri_read"], 2 * RT)
            act.wait_ge(S["rows_a"], 3)
            for m in range(RT):
                act.activation(a_t[:, m, :], r_t[:, m, :], ACT.Exp, scale=spl[:, m:m + 1]).then_inc(S["rg_exp"], 1)
                act.activation(r_t[:, m, :], r_t[:, m, :], ACT.Tanh, scale=spn[:, m:m + 1]).then_inc(S["rg_exp"], 1)
            hr = slice(32, 32 + DN_H)
            own.then(act.activation(rows_raw[hr, :], rows_b[hr, :], ACT.Abs))
            own.then(act.activation(rows_raw[hr, :], rows_raw[hr, :], ACT.Exp, scale=-1.0))
            act.activation(rows_raw[hr, :], rows_raw[hr, :], ACT.Ln, bias=one_col[hr, :]).then_inc(S["rows_exp"], 1)
            for m in range(RT):
                act.wait_ge(S["rg_m2"], m + 1)
                act.activation(r_t[:, m, :], r_t[:, m, :], ACT.Sqrt).then_inc(S["rg_sqrt"], 1)
            for m in range(RT):
                act.activation(gate[:, m, :], gate[:, m, :], ACT.Gelu_apprx_tanh).then_inc(S["rg_gelu"], 1)
            act.wait_ge(S["ht_mm"], 1)
            act.activation(hT_rows[:, :], ps[0:DEC_BATCH + 1, 6, :], ACT.Copy).then_inc(S["ht_sb"], 1)
            act.wait_ge(S["ht_sb"], 1)
            act.dma_start(O["h_p"][0], hT_rows[0:1, :]).then_inc(S["state_out"], 16)
            act.dma_start(O["h_s"][0], hT_rows[1:, :]).then_inc(S["state_out"], 16)
            end_phase(act, "act")
            act.dma_start(cst[:, :, :], A["dn_cst"]).then_inc(S["gate_w"], 16)
            end_phase(act, "act")

            def head_norms(batch, tiles, mean):
                for n, tile in enumerate(tiles):
                    act.activation(sq8[:, n, :], tile, ACT.Square).then_inc(S["cn_sq"], 1)
                act.wait_ge(S["cn_mm"], batch + 1)
                act.activation(norm_rows[:, :].rearrange("p (a t) -> p a t", a=3), ps[0:NR, 0:3, 0:352], ACT.Sqrt,
                               bias=eps_col[0:NR, :], scale=mean).then_inc(S["cn_sqrt"], 1)

            own.did(act.activation(rows[0:DN_H, :], rows_raw[0:DN_H, :], ACT.Sigmoid))
            head_norms(0, [qkvz[:, n, :] for n in range(8)], 1.0)
            act.wait_ge(S["rows_b"], 1)
            own.did(act.activation(rows[64:64 + DN_H, :], rows[64:64 + DN_H, :], ACT.Exp))
            act.wait_ge(S["gate_w"], 96)
            end_phase(act, "act")

            def act_chunk(c, t0, w, levels, smp):
                act.wait_ge(S["st_r"], c + 1)
                act.wait_ge(S["pe_bc"], c + 1)
                act.activation(dn["egb"][:, :, 0:w], quad(0)[:, :, 0:w], ACT.Exp).then_inc(S["egb_r"], 1)
                act.wait_ge(S["pe_col"], c + 1)
                act.activation(cols[0:w, :], ps[0:w, 2, 0:P], ACT.Copy).then_inc(S["cols_r"], 1)
                act.wait_ge(S["cols_r"], c + 1)
                act.wait_ge(S["pe_kt"], c + 1)
                for h in range(DN_H):
                    last = act.activation(dn["kd"][0:w, h, :], quad(6)[0:w, h, :], ACT.Copy, scale=cols[0:w, 64 + h:65 + h])
                last.then_inc(S["kd_r"], 1)
                act.wait_ge(S["dec_r"], c + 1)
                act.activation(dn["dec"][0:w, :, 0:w], dn["dec"][0:w, :, 0:w], ACT.Exp).then_inc(S["dec_e"], 1)
                act.wait_ge(S["pe_vt"], c + 1)
                for h in range(DN_H):
                    last = act.activation(dn["vb"][0:w, h, :], quad(7)[0:w, h, :], ACT.Copy, scale=cols[0:w, h:h + 1])
                last.then_inc(S["vb_r"], 1)
                act.wait_ge(S["pe_l"], c + 1)
                act.activation(dn["lm"][0:w, :, 0:w], quad(5)[0:w, :, 0:w], ACT.Copy).then_inc(S["lm_r"], 1)
                for l in range(levels):
                    act.wait_ge(S["pe_y"], c * LEVELS + l + 1)
                    act.activation(dn["yy"][0:w, :, 0:w], quad(3)[0:w, :, 0:w], ACT.Copy).then_inc(S["y_sb"], 1)
                if smp:
                    act.wait_ge(S["pe_ks"], QB + 1)
                    act.activation(ks_s[:, :, :, :].rearrange("p h a t -> p (h a t)"), ps[:, 0, 0:DN_H * 2 * SMP], ACT.Copy)\
                        .then_inc(S["y_sb"], 1)
                act.wait_ge(S["pe_vn"], c + 1)
                act.activation(dn["vn"][0:w, :, :], quad(1)[0:w, :, :], ACT.Copy).then_inc(S["vn_r"], 1)
                if not smp:
                    act.wait_ge(S["pe_o"], c + 1)
                    act.activation(qkvz[:, 0:4, ds(t0, w)], quad(2)[:, :, 0:w], ACT.Copy).then_inc(S["o_st"], 1)

            with act.Fori(0, QB) as c:
                act_chunk(c, c * P, P, LEVELS, False)
            act.wait_ge(S["st_r"], QB + 1)
            act.dma_start(O["S_p"][0, 0].rearrange("h k v -> k h v"), dn["st"][:, :, :]).then_inc(S["state_out"], 16)
            act.wait_ge(S["kc_cp"], QB + 1)
            act.dma_start(s0[:, :, :, :], A["state_S"][0].rearrange("b h k v -> k b h v")).then_inc(S["s0_in"], 16)
            act_chunk(QB, SEQ, SMP, 1, True)
            act.wait_ge(S["s0_out"], DEC_BATCH)
            act.dma_start(O["S_s"][0].rearrange("b h k v -> k b h v"), s0[:, :, :, :]).then_inc(S["state_out"], 16)
            for m in range(DN_H):
                act.activation(qkvz[:, 12 + m, :], qkvz[:, 12 + m, :], ACT.Silu).then_inc(S["silu_z"], 1)
            act.wait_ge(S["o_st"], QB + 2)
            head_norms(1, [qkvz[:, n, :] for n in range(DN_H)], 1.0 / DK)
            act.wait_ge(S["cn_bc"], 12)
            act.dma_start(x[:, 0:4, :], x_spill[:, 0:4, :]).then_inc(S["x_back0"], 16)
            act.wait_ge(S["state_out"], 16 * 6)
            end_phase(act, "act")
            for m in range(RT):
                act.activation(xh[:, m, :], gate[:, m, :], ACT.Copy).then_inc(S["mix_h"], 1)
            for m in range(DN_H):
                act.activation(xh[:, RT + m, :], qkvz[:, 12 + m, :], ACT.Copy).then_inc(S["mix_h"], 1)
            act.wait_ge(S["mix_h"], KT)
            act.wait_ge(S["mix_l"], KT)
            act.dma_start(x[:, 4:8, :], x_spill[:, 4:8, :]).then_inc(S["x_back1"], 16)
            units(act, FIRST["rec_out"], U_REC_OUT, 2, square_unit(1, FIRST["rec_out"]))

            def mlp(l, next_gain):
                n_mlp = SHARED_N[("mlp", l)]
                first = FIRST[f"mlp{l}"]
                act.wait_ge(mm_out, first + 2)
                split_hi(n_mlp, R_MLP0 + 8 * l)
                norm_root(n_mlp)
                base_h = l * FF_CHUNKS * FT

                def chunk(c):
                    for q in range(FT):
                        n = c * FT + (base_h + q)
                        act.wait_ge(S["hu_r"], n + 1)
                        act.activation(hs[:, q % 2, :], hu[:, q % 2, :], ACT.Square).then_inc(S["hsq_r"], 1)
                        act.wait_ge(S["hsq_r"], n + 1)
                        act.activation(hh[:, q, :], hs[:, q % 2, :], ACT.Copy).then_inc(S["hh_r"], 1)

                with act.Fori(0, FF_CHUNKS) as c:
                    chunk(c)
                for m in range(KT):
                    act.wait_ge(set_free, first + U_MLP - KT + m + 3)
                    if next_gain is not None:
                        act.activation(xh[:, m, :], x[:, m, :], ACT.Copy, scale=prm[:, next_gain + m:next_gain + m + 1])\
                            .then_inc(S["xh_ready"], 1)
                    square(n_mlp + 1, m, m % 2, x[:, m, :])

            mlp(0, R_MIX1)
            rest_of_act(act, own, norm_root, square_unit, mlp)

        @block.vector
        def _(dve):
            own = Chain(dve, dve_chain)
            for name in ("uc0", "conv_done", "o_st", "st_r"):
                dve.sem_inc(S[name], 1)
            dve.wait_ge(mm_out, 1)
            dve.tensor_copy(prm[:, 0:R_ALL], ps[:, 0, 0:R_ALL]).then_inc(set_free, 1)
            dve.wait_ge(mm_out, 2)
            nh = CT * DEC_BATCH * 3
            own.did(dve.tensor_copy(flat(hist[:, :, :]), ps[:, 1, 0:nh]))
            dve.tensor_copy(flat(h0T), ps[:, 1, nh:nh + RT * DEC_BATCH]).then_inc(set_free, 1)
            for k in range(1, 2 * (QB + 1), 2):
                t = k // 2
                w = P if t < QB else SMP
                dve.wait_ge(S["xt_mm"], k + 1)
                dve.tensor_copy(x[:, 4:8, t * P:t * P + w], quad(2 + k % 6)[:, :, 0:w]).then_inc(S["xt_dve"], 1)
            end_phase(dve, "dve")

            def add_square(n, k, par):
                dve.wait_ge(S["sq_ready"], k + (8 * n + 1))
                if n:
                    dve.wait_ge(S["sq_added"], k + 8 * n)
                elif k:
                    dve.wait_ge(S["sq_added"], k)
                dve.tensor_tensor(sumsq[:, :], sumsq[:, :], sq[:, par, :], ALU.add).then_inc(S["sq_added"], 1)

            def norm_mean(n, bank):
                dve.wait_ge(S["ss_mm"], n + 1)
                dve.tensor_scalar(rstd[:, :].rearrange("p (a t) -> p a t", a=3), ps[:, bank:bank + 3, 0:352], 1.0 / D_MODEL, EPS,
                                  ALU.mult, ALU.add).then_inc(S["ms_ready"], 1)
                dve.wait_ge(S["rt_ready"], n + 1)
                dve.reciprocal(rstd[:, :], rstd[:, :]).then_inc(S["rstd_ready"], 1)
                dve.wait_ge(S["rstd_ready"], n + 1)

            def low_part(n, k, gain):
                dve.wait_ge(S["xh_ready"], 8 * n + k + 1)
                dve.scalar_tensor_tensor(xl[:, k, :], x[:, k, :], prm[:, gain + k:gain + k + 1],
                                         xh[:, k, :].bitcast(F32), ALU.mult, ALU.subtract).then_inc(S["xl_ready"], 1)

            own.did(dve.memset(ub[:, 0:3], 0.0))
            own.then(dve.memset(sumsq[:, :], 0.0))
            for k in range(KT):
                low_part(0, k, R_MIX0)
            for k in range(KT):
                add_square(0, k, k % 2)
            norm_mean(0, 3 - 3 * (FIRST["rec_in"] % 2))
            dve.wait_ge(S["x_spilled"], 16)
            r3 = rstd[:, :].rearrange("p (a t) -> p a t", a=3)
            rs_s = rstd[:, SEQ:].rearrange("p (b t) -> p b t", b=DEC_BATCH)

            def conv_unit(j, off):
                u = j + off
                dve.wait_ge(mm_out, u + 3)
                dve.wait_ge(S["uc0"], u + 1)
                dve.wait_ge(S["conv_done"], u + 1)
                own.did(dve.tensor_tensor(ub[:, 3:3 + 704].rearrange("p (a t) -> p a t", a=2), set_view(j, 0, 2)[:, :, 0:352],
                                          r3[:, 0:2, :], ALU.mult))
                own.did(dve.tensor_tensor(ub[:, 3 + 704:3 + SEQ], ps[:, 3 * (j % 2) + 2, 0:SEQ - 704], rstd[:, 704:SEQ], ALU.mult))
                heads = ub[:, 3 + SEQ:UB].rearrange("p (b t) -> p b t", b=DEC_BATCH)
                dve.tensor_tensor(heads[:, :, 3:],
                                  ps[:, 3 * (j % 2) + 2, SEQ - 704:352].rearrange("p (b t) -> p b t", b=DEC_BATCH),
                                  rs_s, ALU.mult).then_inc(set_free, 1)
                dve.wait_ge(S["uc0"], u + 2)
                for i in range(1, CONV_W):
                    ins = dve.scalar_tensor_tensor(uc[:, 0:UB - 3], ub[:, i:i + UB - 3], prm[:, ds(R_CONV + i * CT + u, 1)],
                                                   uc[:, 0:UB - 3], ALU.mult, ALU.add)
                    if i < CONV_W - 1:
                        own.then(ins)
                    else:
                        ins.then_inc(S["conv_done"], 1)

            with own.loop(8, 8) as i:
                for j in range(2):
                    conv_unit(j, i * 2)

            def plain_unit(dst, first):
                def body(j, off):
                    u = j + off
                    dve.wait_ge(mm_out, u + 3)
                    dve.tensor_tensor(dst[:, ds(u - first, 1), :].rearrange("p o (a t) -> p (o a) t", a=3),
                                      set_view(j, 0, 3)[:, :, 0:352], r3, ALU.mult).then_inc(set_free, 1)
                return body

            units(dve, 16, 4, 2, plain_unit(gate, 16))
            units(dve, 20, 4, 2, plain_unit(qkvz, 8))
            j = 24
            dve.wait_ge(mm_out, j + 3)
            dve.tensor_tensor(rows_raw[:, :].rearrange("p (a t) -> p a t", a=3), set_view(j, 0, 3)[0:64, :, 0:352],
                              r3[0:64], ALU.mult).then_inc(set_free, 1)
            dve.wait_ge(set_free, 2 + U_REC_IN)
            hr = slice(32, 32 + DN_H)
            own.did(dve.tensor_scalar(rows_b[hr, :], rows_raw[hr, :], dtb[hr, :], None, ALU.add))
            end_phase(dve, "dve")

            lam = prm[:, R_LAM:R_LAM + RT]
            e, w, lw, d, z, o = tmp4
            dve.wait_ge(S["rows_a"], 2)
            own.then(dve.tensor_scalar(d, w, -1.0, 0.0, ALU.add, ALU.add))
            own.then(dve.tensor_scalar(z, d, 0.0, None, ALU.is_equal))
            own.then(dve.tensor_tensor(d, d, z, ALU.add))
            own.then(dve.reciprocal(d, d))
            own.then(dve.tensor_tensor(lw, lw, e, ALU.mult))
            own.then(dve.tensor_tensor(lw, lw, d, ALU.mult))
            own.then(dve.tensor_tensor(z, z, e, ALU.mult))
            own.then(dve.tensor_tensor(lw, lw, z, ALU.add))
            own.then(dve.tensor_scalar(o, lam, -1.0, 0.0, ALU.mult, ALU.max))
            own.then(dve.tensor_tensor(lw, lw, o, ALU.add))
            own.then(dve.tensor_scalar(spl, lw, -RG_C, None, ALU.mult))
            dve.tensor_scalar(spn, lw, RG_C, None, ALU.mult).then_inc(S["rows_a"], 1)

            for m in range(RT):
                dve.wait_ge(S["ri_read"], 2 * RT)
                own.then(dve.tensor_tensor(i_t[:, m, :], xr[:, m, :], i_t[:, m, :], ALU.mult))
                dve.wait_ge(S["rg_exp"], 2 * m + 2)
                own.then(dve.tensor_tensor(xr[:, m, :], a_t[:, m, :], a_t[:, m, :], ALU.mult))
                own.then(dve.scalar_tensor_tensor(r_t[:, m, :], xr[:, m, :], 1.0, r_t[:, m, :], ALU.add, ALU.mult))
                own.then(dve.tensor_scalar(r_t[:, m, :], r_t[:, m, :], 0.0, None, ALU.max))
                dve.memset(r_t[:, m, 0:1], 1.0).then_inc(S["rg_m2"], 1)
            first = slice(SEQ, TOK, DEC_SEQ)
            last_t = slice(SEQ + DEC_SEQ - 1, TOK, DEC_SEQ)
            for m in range(RT):
                dve.wait_ge(S["rg_sqrt"], m + 1)
                own.then(dve.tensor_tensor(i_t[:, m, :], i_t[:, m, :], r_t[:, m, :], ALU.mult))
                own.then(dve.tensor_tensor(h0T[:, m, :], a_t[:, m, first], h0T[:, m, :], ALU.mult))
                own.then(dve.tensor_tensor(i_t[:, m, first], i_t[:, m, first], h0T[:, m, :], ALU.add))
                own.then(dve.memset(a_t[:, m, first], 0.0))
                own.then(dve.tensor_tensor_scan(xr[:, m, :], a_t[:, m, :], i_t[:, m, :], 0.0, ALU.mult, ALU.add))
                own.did(dve.tensor_copy(hT[:, m, 0:1], xr[:, m, SEQ - 1:SEQ]))
                dve.tensor_copy(hT[:, m, 1:], xr[:, m, last_t]).then_inc(S["rg_done"], 1)
                dve.wait_ge(S["rg_gelu"], m + 1)
                own.did(dve.tensor_tensor(gate[:, m, :], xr[:, m, :], gate[:, m, :], ALU.mult))
            dve.wait_ge(S["rows_exp"], 1)
            own.then(dve.scalar_tensor_tensor(rows_b[hr, :], rows_b[hr, :], 0.0, rows_raw[hr, :], ALU.max, ALU.add))
            own.then(dve.tensor_scalar(rows_b[hr, :], rows_b[hr, :], nea[hr, :], -1.0, ALU.mult, ALU.mult))
            end_phase(dve, "dve")
            end_phase(dve, "dve")
            own.then(dve.tensor_tensor_scan(rows[hr, :], reset[hr, :], rows_b[hr, :], 0.0, ALU.mult, ALU.add))
            ks = slice(64, 64 + DN_H)
            for lo, n, q in ((0, QB, P), (SEQ, DEC_BATCH, DEC_SEQ)):
                g = rows[hr, lo:lo + n * q].rearrange("p (c t) -> p c t", t=q)
                e2 = rows[ks, lo:lo + n * q].rearrange("p (c t) -> p c t", t=q)
                ins = dve.tensor_tensor(e2, g[:, :, q - 1:q].to_broadcast([DN_H, n, q]), g, ALU.subtract)
                if lo == 0:
                    own.did(ins)
                else:
                    ins.then_inc(S["rows_b"], 1)

            def invert_norms(batch):
                dve.wait_ge(S["cn_sqrt"], batch + 1)
                dve.reciprocal(norm_rows[:, :], norm_rows[:, :]).then_inc(S["cn_rec"], 1)

            def head_scale(n, par, dst, factor):
                dve.wait_ge(S["cn_bc"], n + 1)
                dst = dst.rearrange("p (a t) -> p a t", a=3)
                dve.scalar_tensor_tensor(dst, dst, factor, ps[:, 3 * par:3 * par + 3, 0:352], ALU.mult, ALU.mult)\
                    .then_inc(S["cn_out"], 1)

            invert_norms(0)
            for n in range(8):
                head_scale(n, n % 2, qkvz[:, n, :], DK ** -0.5 if n < 4 else 1.0)
            end_phase(dve, "dve")

            def mask(k, w):
                return cst[0:w, k:k + 1, 0:w].to_broadcast([w, DN_H, w])

            def dve_chunk(c, t0, w, levels, smp):
                dve.wait_ge(S["pe_bc"], c + 1)
                dve.wait_ge(S["cols_r"], c + 1)
                for h in range(DN_H):
                    last = dve.tensor_scalar(dn["dec"][0:w, h, 0:w], quad(0)[0:w, h, 0:w], cols[0:w, 32 + h:33 + h], 0.0,
                                             ALU.subtract, ALU.min)
                last.then_inc(S["dec_r"], 1)
                dve.wait_ge(S["kc_cp"], c + 1)
                kbg = kq_s[:, :, 0, :] if smp else dn["kbg"][:, :, :]
                qg = kq_s[:, :, 1, :] if smp else dn["qg"][:, :, :]
                own.then(dve.tensor_tensor(kbg, dn["kc"][:, :, 0:w], quad(1)[:, :, 0:w], ALU.mult))
                dve.wait_ge(S["egb_r"], c + 1)
                dve.tensor_tensor(kbg, kbg, dn["egb"][:, :, 0:w], ALU.mult).then_inc(S["kbg_r"], 1)
                dve.tensor_tensor(qg, qkvz[:, 0:4, ds(t0, w)], dn["egb"][:, :, 0:w], ALU.mult).then_inc(S["qg_r"], 1)
                dve.wait_ge(S["dec_e"], c + 1)
                dec, decb = dn["dec"][0:w, :, 0:w], dn["decb"][0:w, :, 0:w]
                own.then(dve.tensor_tensor(dec, dec, mask(C_UPPER_S if smp else C_UPPER, w), ALU.mult))
                own.then(dve.tensor_tensor(decb, dec, quad(1)[0:w, :, 0:w], ALU.mult))
                own.then(dve.tensor_tensor(decb, decb, mask(C_STRICT_S if smp else C_STRICT, w), ALU.mult))
                dve.wait_ge(S["pe_kk"], c + 1)
                dve.tensor_tensor(dn["lt"][0:w, :, 0:w], quad(3)[0:w, :, 0:w], decb, ALU.mult).then_inc(S["lt_r"], 1)
                dve.tensor_tensor(dn["attn"][0:w, :, 0:w], quad(4)[0:w, :, 0:w], dec, ALU.mult).then_inc(S["attn_r"], 1)
                dve.wait_ge(S["lt_r"], c + 1)
                xi, xti = dn["xi"][0:w, :, 0:w], dn["xti"][0:w, :, 0:w]
                own.then(dve.tensor_tensor(xti, dn["lt"][0:w, :, 0:w], mask(C_NEG1T, w), ALU.mult))
                own.then(dve.tensor_tensor(xti, xti, mask(C_IDENT, w), ALU.add))
                dve.wait_ge(S["lm_r"], c + 1)
                own.then(dve.tensor_tensor(xi, dn["lm"][0:w, :, 0:w], mask(C_NEG1, w), ALU.mult))
                dve.tensor_tensor(xi, xi, mask(C_IDENT, w), ALU.add).then_inc(S["x0_r"], 1)
                dve.wait_ge(S["x0_r"], c + 1)
                for l in range(levels):
                    dve.wait_ge(S["pe_x"], c * LEVELS + l + 1)
                    dve.tensor_tensor(xti, xti, quad(5)[0:w, :, 0:w], ALU.subtract).then_inc(S["x_sb"], 1)
                    if l < LEVELS - 1 and not smp:
                        dve.wait_ge(S["pe_xi"], c * (LEVELS - 1) + l + 1)
                        dve.tensor_tensor(xi, xi, quad(4)[0:w, :, 0:w], ALU.subtract).then_inc(S["xi_sb"], 1)
                        dve.wait_ge(S["xi_sb"], c * (LEVELS - 1) + l + 1)
                    dve.wait_ge(S["x_sb"], c * LEVELS + l + 1)
                dve.wait_ge(S["vb_r"], c + 1)
                if not smp:
                    dve.wait_ge(S["pe_ks"], c + 1)
                    dve.tensor_tensor(dn["rr"][:, :, :], dn["vb"][:, :, :], quad(0), ALU.subtract).then_inc(S["rr_r"], 1)
                    dve.wait_ge(S["pe_ds"], c + 1)
                    for h in range(DN_H):
                        last = dve.scalar_tensor_tensor(dn["st"][:, h, :], dn["st"][:, h, :], dn["egb"][:, h, w - 1:w],
                                                        quad(6)[:, h, :], ALU.mult, ALU.add)
                    last.then_inc(S["st_r"], 1)
                else:
                    dve.wait_ge(S["pe_ks"], c + 2)
                    dve.tensor_tensor(dn["rr"][0:w, :, :], dn["vb"][0:w, :, :], quad(1)[0:w], ALU.subtract)\
                        .then_inc(S["rr_r"], 1)
                    dve.wait_ge(S["kd_r"], c + 1)
                    dve.wait_ge(S["vc_cp"], c + 1)
                    for b in range(DEC_BATCH):
                        dve.tensor_scalar(kdm[0:w, b, :, :], dn["kd"][0:w, :, :], cst[0:w, C_COLS, b:b + 1], None, ALU.mult)\
                            .then_inc(S["kdm_r"], 1)
                    dve.wait_ge(S["pe_o"], c + 1)
                    dve.tensor_tensor(qkvz[:, 0:4, SEQ:TOK], quad(2)[:, :, 0:w], ks_s[:, :, 1, :], ALU.add)\
                        .then_inc(S["o_st"], 1)
                    for b in range(DEC_BATCH):
                        dve.wait_ge(S["pe_ds"], c + b + 1)
                        t = b * DEC_SEQ + DEC_SEQ - 1
                        for h in range(DN_H):
                            last = dve.scalar_tensor_tensor(s0[:, b, h, :], s0[:, b, h, :], dn["egb"][:, h, t:t + 1],
                                                            quad(4 + b % 4)[:, h, :], ALU.mult, ALU.add)
                        last.then_inc(S["s0_out"], 1)

            with own.loop(QB, 7) as c:
                dve_chunk(c, c * P, P, LEVELS, False)
            dve_chunk(QB, SEQ, SMP, 1, True)
            invert_norms(1)
            for n in range(8, 12):
                dve.wait_ge(S["silu_z"], n - 7)
                head_scale(n, n % 2, qkvz[:, n - 8, :], prm[:, R_DN:R_DN + 1])
                dve.wait_ge(S["cn_out"], n + 1)
                own.did(dve.tensor_tensor(qkvz[:, n + 4, :], qkvz[:, n - 8, :], qkvz[:, n + 4, :], ALU.mult))
            end_phase(dve, "dve")
            for m in range(KT):
                src = gate[:, m, :] if m < RT else qkvz[:, 8 + m, :]
                dve.wait_ge(S["mix_h"], m + 1)
                dve.tensor_tensor(xl[:, m, :], src, xh[:, m, :].bitcast(F32), ALU.subtract).then_inc(S["mix_l"], 1)

            def add_unit(first, n):
                def body(j, off):
                    dve.wait_ge(mm_out, j + off + 3)
                    xm = x[:, ds(j + off - first, 1), :].rearrange("p o (a t) -> p (o a) t", a=3)
                    dve.tensor_tensor(xm, xm, set_view(j, 0, 3)[:, :, 0:352], ALU.add).then_inc(set_free, 1)
                    add_square(n, j + off - first, (j - first) % 2)
                return body

            def output_units(first, n, backs):
                dve.wait_ge(S["mix_l"], KT * (backs // 16))
                own.then(dve.memset(sumsq[:, :], 0.0))
                dve.wait_ge(S["x_back0"], backs)
                for j in range(4):
                    add_unit(first, n)(first + j, 0)
                dve.wait_ge(S["x_back1"], backs)
                for j in range(4, 8):
                    add_unit(first, n)(first + j, 0)

            output_units(FIRST["rec_out"], 1, 16)

            def mlp(l, next_gain):
                n_mlp = SHARED_N[("mlp", l)]
                first = FIRST[f"mlp{l}"]
                for k in range(KT):
                    low_part(n_mlp, k, R_MLP0 + 8 * l)
                norm_mean(n_mlp, 3 - 3 * (first % 2))
                own.then(dve.memset(sumsq[:, :], 0.0))
                base_h = l * FF_CHUNKS * FT

                def chunk(c, last):
                    for q in range(FT + 1):
                        if q < FT:
                            n = c * FT + (base_h + q)
                            dve.wait_ge(mm_out, c * 12 + (first + q + 3))
                            if q >= 2:
                                dve.wait_ge(S["hsq_r"], n - 1)
                            dve.scalar_tensor_tensor(hu[:, q % 2, :].rearrange("p (a t) -> p a t", a=3),
                                                     set_view(first + q, 0, 3)[:, :, 0:352], 0.0, r3, ALU.max, ALU.mult)\
                                .then_inc(S["hu_r"], 1)
                            dve.wait_ge(S["hu_r"], n + 1)
                            dve.sem_inc(set_free, 1)
                        if q:
                            n = c * FT + (base_h + q - 1)
                            dve.wait_ge(S["hh_r"], n + 1)
                            dve.tensor_tensor(hl[:, q - 1, :], hs[:, (q - 1) % 2, :], hh[:, q - 1, :].bitcast(F32), ALU.subtract)\
                                .then_inc(S["hl_r"], 1)
                    for q in range(KT):
                        add_unit_at(first + FT + q, c * 12, q)
                        if last:
                            if next_gain is not None:
                                low_part(n_mlp + 1, q, next_gain)
                            add_square(n_mlp + 1, q, q % 2)

                with dve.Fori(0, FF_CHUNKS - 1) as c:
                    chunk(c, False)
                chunk(FF_CHUNKS - 1, True)

            def add_unit_at(j, off, m):
                dve.wait_ge(mm_out, off + (j + 3))
                xm = x[:, m, :].rearrange("p (a t) -> p a t", a=3)
                dve.tensor_tensor(xm, xm, set_view(j, 0, 3)[:, :, 0:352], ALU.add).then_inc(set_free, 1)

            mlp(0, R_MIX1)
            rest_of_dve(dve, own, norm_mean, output_units, mlp)


_OUTS = [("y_prompt", (1, 1024, 1024)), ("y_sample", (8, 4, 1024)), ("conv_p", (1, 1, 3, 2048)), ("h_p", (1, 1, 512)),
         ("S_p", (1, 1, 4, 128, 128)), ("k_p", (1, 1, 1024, 2, 128)), ("v_p", (1, 1, 1024, 2, 128)),
         ("kidx_p", (1, 1, 1024, 64)), ("conv_s", (1, 8, 3, 2048)), ("h_s", (1, 8, 512)), ("S_s", (1, 8, 4, 128, 128)),
         ("k_s", (1, 8, 4, 2, 128)), ("v_s", (1, 8, 4, 2, 128)), ("kidx_s", (1, 8, 4, 64))]


def kernel(**inputs):
    import concourse.bacc as _bacc
    from concourse.bass_utils import run_bass_kernel_spmd as _run

    nc = _bacc.Bacc("TRN2", target_bir_lowering=False, num_devices=1)
    arrays = {name: np.ascontiguousarray(a) for name, a in inputs.items()}
    arrays["dn_cst"] = dn_constants()
    arrays["row_reset"] = row_reset()
    arrays["att_cst"] = att_constants()
    arrays["att_bits"] = att_bits()
    A, O = {}, {}
    for name, a in arrays.items():
        A[name] = nc.dram_tensor("in_" + name, a.shape, mybir.dt.from_np(a.dtype), kind="ExternalInput").ap()
    for name, shape in _OUTS:
        O[name] = nc.dram_tensor("out_" + name, shape, F32, kind="ExternalOutput").ap()
    build(nc, A, O)
    r = _run(nc, [{"in_" + name: a for name, a in arrays.items()}], core_ids=[0])
    return tuple(r.results[0]["out_" + name] for name, _ in _OUTS)
```
